# Optimizing a Trainium2 kernel written in Bass

```python
import jax, jax.numpy as jnp
from jax import lax
import numpy as np

D_MODEL = 1024
BATCH = 1
SEQ = 512
DEPTH = 2

N_MIXERS = 2
N_POOL_LAYERS = (DEPTH + 1) // 2
N_MLA_LAYERS = DEPTH // 2

POOL_WINDOWS = (2, 4, 8, 16)
N_POOL_GROUPS = len(POOL_WINDOWS)
POOL_GROUP = D_MODEL // N_POOL_GROUPS

N_HEADS = D_MODEL // 128
QK_NOPE_DIM = 128
QK_ROPE_DIM = 64
V_HEAD_DIM = 128
Q_LORA_RANK = 3 * D_MODEL // 8
KV_LORA_RANK = D_MODEL // 8
QK_HEAD_DIM = QK_NOPE_DIM + QK_ROPE_DIM
ROPE_THETA = 10000.0
Q_BLOCK = 128

D_FF = ((8 * D_MODEL // 3 + 255) // 256) * 256

RMS_EPS = 1e-6


def rms_norm(x, g):
    xf = x.astype(jnp.float32)
    y = xf * lax.rsqrt(jnp.mean(xf * xf, axis=-1, keepdims=True) + RMS_EPS)
    return (y * g.astype(jnp.float32)).astype(x.dtype)

def pool_mixer(h, w, scale):
    B, S, D = h.shape
    hf = h.astype(jnp.float32).reshape(B, S, N_POOL_GROUPS, POOL_GROUP)
    cs = jnp.cumsum(hf, axis=1)
    n_avail = jnp.arange(1, S + 1, dtype=jnp.float32)
    outs = []
    for g, win in enumerate(POOL_WINDOWS):
        c = cs[:, :, g]
        lag = jnp.pad(c[:, :-win], ((0, 0), (win, 0), (0, 0)))
        mean = (c - lag) / jnp.minimum(n_avail, float(win))[:, None]
        outs.append(mean - hf[:, :, g])
    p = jnp.stack(outs, axis=2).astype(h.dtype)
    y = jnp.einsum('bsgc,gcd->bsgd', p, w).reshape(B, S, D)
    return y * scale

def rope_tables(positions):
    inv = 1.0 / (ROPE_THETA ** (jnp.arange(0, QK_ROPE_DIM, 2, dtype=jnp.float32) / QK_ROPE_DIM))
    ang = positions.astype(jnp.float32)[..., None] * inv
    return jnp.cos(ang), jnp.sin(ang)

def apply_rope(x, cos, sin):
    xf = x.astype(jnp.float32)
    half = QK_ROPE_DIM // 2
    x1, x2 = xf[..., :half], xf[..., half:]
    return jnp.concatenate([x1 * cos - x2 * sin, x2 * cos + x1 * sin], axis=-1).astype(x.dtype)

def causal_attention(q, k, v):
    B, S, H, Dq = q.shape
    nb = S // Q_BLOCK
    qb = q.reshape(B, nb, Q_BLOCK, H, Dq).transpose(1, 0, 2, 3, 4)
    key_pos = jnp.arange(S)
    sm_scale = Dq ** -0.5

    def one_block(args):
        blk, qi = args
        s = jnp.einsum('bqhd,bkhd->bhqk', qi, k).astype(jnp.float32) * sm_scale
        q_pos = blk * Q_BLOCK + jnp.arange(Q_BLOCK)
        mask = key_pos[None, :] <= q_pos[:, None]
        s = jnp.where(mask, s, -jnp.inf)
        p = jax.nn.softmax(s, axis=-1).astype(v.dtype)
        return jnp.einsum('bhqk,bkhd->bqhd', p, v)

    o = lax.map(one_block, (jnp.arange(nb), qb))
    return o.transpose(1, 0, 2, 3, 4).reshape(B, S, H, v.shape[-1])

def mla(h, cos, sin, w_down, q_norm, w_uq, kv_norm, w_ukv, w_o):
    B, S, _ = h.shape
    d = h @ w_down
    cq = rms_norm(d[..., :Q_LORA_RANK], q_norm)
    ckv = rms_norm(d[..., Q_LORA_RANK:Q_LORA_RANK + KV_LORA_RANK], kv_norm)
    k_rope = apply_rope(d[..., Q_LORA_RANK + KV_LORA_RANK:], cos, sin)
    q = (cq @ w_uq).reshape(B, S, N_HEADS, QK_HEAD_DIM)
    q_rope = apply_rope(q[..., QK_NOPE_DIM:], cos[:, :, None], sin[:, :, None])
    q = jnp.concatenate([q[..., :QK_NOPE_DIM], q_rope], axis=-1)
    kv = (ckv @ w_ukv).reshape(B, S, N_HEADS, QK_NOPE_DIM + V_HEAD_DIM)
    k = jnp.concatenate(
        [kv[..., :QK_NOPE_DIM],
         jnp.broadcast_to(k_rope[:, :, None, :], (B, S, N_HEADS, QK_ROPE_DIM))], axis=-1)
    v = kv[..., QK_NOPE_DIM:]
    o = causal_attention(q, k, v)
    return o.reshape(B, S, N_HEADS * V_HEAD_DIM) @ w_o

def swiglu(h, w_gate, w_up, w_down):
    return (jax.nn.silu(h @ w_gate) * (h @ w_up)) @ w_down

def first_inputs(seed: int = 0) -> dict:
    key = jax.random.key(seed)
    ks = jax.random.split(key, 16)
    f32 = jnp.float32

    def nrm(k, shape, fan_in):
        return jax.random.normal(k, shape, f32) * (fan_in ** -0.5)

    def gain(k, shape):
        return 1.0 + 0.02 * jax.random.normal(k, shape, f32)

    x = jax.random.normal(ks[0], (BATCH, SEQ, D_MODEL), f32)
    positions = jnp.broadcast_to(jnp.arange(SEQ, dtype=jnp.int32)[None, :], (BATCH, SEQ))
    return {
        "x": x,
        "positions": positions,
        "norm_mix": gain(ks[1], (DEPTH, D_MODEL)),
        "norm_ffn": gain(ks[2], (DEPTH, D_MODEL)),
        "norm_final": gain(ks[3], (D_MODEL,)),
        "pool_w": nrm(ks[4], (N_POOL_LAYERS, N_POOL_GROUPS, POOL_GROUP, POOL_GROUP), POOL_GROUP),
        "pool_scale": gain(ks[5], (N_POOL_LAYERS, D_MODEL)),
        "mla_w_down": nrm(ks[6], (N_MLA_LAYERS, D_MODEL, Q_LORA_RANK + KV_LORA_RANK + QK_ROPE_DIM), D_MODEL),
        "mla_q_norm": gain(ks[7], (N_MLA_LAYERS, Q_LORA_RANK)),
        "mla_w_uq": nrm(ks[8], (N_MLA_LAYERS, Q_LORA_RANK, N_HEADS * QK_HEAD_DIM), Q_LORA_RANK),
        "mla_kv_norm": gain(ks[9], (N_MLA_LAYERS, KV_LORA_RANK)),
        "mla_w_ukv": nrm(ks[10], (N_MLA_LAYERS, KV_LORA_RANK, N_HEADS * (QK_NOPE_DIM + V_HEAD_DIM)), KV_LORA_RANK),
        "mla_w_o": nrm(ks[11], (N_MLA_LAYERS, N_HEADS * V_HEAD_DIM, D_MODEL), N_HEADS * V_HEAD_DIM),
        "ffn_w_gate": nrm(ks[12], (DEPTH, D_MODEL, D_FF), D_MODEL),
        "ffn_w_up": nrm(ks[13], (DEPTH, D_MODEL, D_FF), D_MODEL),
        "ffn_w_down": nrm(ks[14], (DEPTH, D_FF, D_MODEL), D_FF),
    }

def first_block(x, positions, norm_mix, norm_ffn, norm_final, pool_w, pool_scale,
              mla_w_down, mla_q_norm, mla_w_uq, mla_kv_norm, mla_w_ukv, mla_w_o,
              ffn_w_gate, ffn_w_up, ffn_w_down):
    cos, sin = rope_tables(positions)
    for i in range(DEPTH):
        h = rms_norm(x, norm_mix[i])
        j = i // N_MIXERS
        if i % N_MIXERS == 0:
            x = x + pool_mixer(h, pool_w[j], pool_scale[j])
        else:
            x = x + mla(h, cos, sin, mla_w_down[j], mla_q_norm[j], mla_w_uq[j],
                        mla_kv_norm[j], mla_w_ukv[j], mla_w_o[j])
        h = rms_norm(x, norm_ffn[i])
        x = x + swiglu(h, ffn_w_gate[i], ffn_w_up[i], ffn_w_down[i])
    return rms_norm(x, norm_final)


DEPTH_2 = 1

PLE_DIM = 256
D_MIX = D_MODEL
HEAD_DIM = 64

CONV_W = D_MIX // 4
CONV_K = 3

NSA_HEADS = 6
NSA_KV_HEADS = 2
NSA_GROUP = NSA_HEADS // NSA_KV_HEADS
NSA_W = NSA_HEADS * HEAD_DIM
NSA_KV_W = NSA_KV_HEADS * HEAD_DIM
CMP_BLOCK = 32
CMP_STRIDE = 16
SLC_BLOCK = 64
SLC_TOPK = 16
WIN = 512
FORCE_SCORE = 1e4

DIL_PAIRS = ((128, 1), (512, 4), (2048, 16))
DIL_HEADS_PER_PAIR = 2
DIL_HEADS = DIL_HEADS_PER_PAIR * len(DIL_PAIRS)
DIL_W = DIL_HEADS * HEAD_DIM
DIL_BLOCK = 128

IN_SIZES = ((CONV_W,) * 4
            + (NSA_W,) + (NSA_KV_W,) * 6
            + (NSA_HEADS * 3, NSA_W)
            + (DIL_W,) * 4)
D_IN = sum(IN_SIZES)


def _rmsnorm(x, g):
    x32 = x.astype(jnp.float32)
    y = x32 * lax.rsqrt(jnp.mean(x32 * x32, axis=-1, keepdims=True) + RMS_EPS)
    return (y * g.astype(jnp.float32)).astype(x.dtype)

def _masked_softmax(s, mask):
    s = jnp.where(mask, s.astype(jnp.float32), -jnp.inf)
    m = jnp.max(s, axis=-1, keepdims=True)
    m = jnp.where(jnp.isfinite(m), m, 0.0)
    e = jnp.where(mask, jnp.exp(s - m), 0.0)
    den = jnp.sum(e, axis=-1, keepdims=True)
    return e / jnp.maximum(den, 1e-30), m, den

def _short_conv(u, w, b):
    y = lax.conv_general_dilated(
        u, w[:, None, :].astype(u.dtype), window_strides=(1,), padding=((CONV_K - 1, 0),),
        dimension_numbers=("NWC", "WIO", "NWC"), feature_group_count=u.shape[-1])
    return y + b.astype(u.dtype)

def _nsa(q, kc_raw, vc_raw, ks_raw, vs_raw, kw_raw, vw_raw, gates, pe, w1, w2):
    B, T, G, R, E = q.shape
    scale = E ** -0.5
    n_cmp = (T - CMP_BLOCK) // CMP_STRIDE + 1
    cmp_start = jnp.arange(n_cmp) * CMP_STRIDE
    cmp_idx = cmp_start[:, None] + jnp.arange(CMP_BLOCK)[None, :]

    def compress(a, pe_, w1_, w2_):
        blk = a[:, cmp_idx] + pe_[None, None, :, None, :].astype(a.dtype)
        flat = jnp.moveaxis(blk, 3, 2).reshape(B, n_cmp, G, CMP_BLOCK * E)
        return jax.nn.silu(flat @ w1_) @ w2_

    k_cmp = compress(kc_raw, pe[0], w1[0], w2[0])
    v_cmp = compress(vc_raw, pe[1], w1[1], w2[1])
    cmp_last = cmp_start + CMP_BLOCK - 1
    n_slc = T // SLC_BLOCK
    slc_start = jnp.arange(n_slc) * SLC_BLOCK
    overlap = ((cmp_start[:, None] < slc_start[None, :] + SLC_BLOCK)
               & (cmp_start[:, None] + CMP_BLOCK > slc_start[None, :])).astype(jnp.float32)
    k_slc = ks_raw.reshape(B, n_slc, SLC_BLOCK, G, E).transpose(0, 3, 1, 2, 4)
    v_slc = vs_raw.reshape(B, n_slc, SLC_BLOCK, G, E).transpose(0, 3, 1, 2, 4)
    top = min(SLC_TOPK, n_slc)
    b_ix = jnp.arange(B)[:, None, None, None]
    g_ix = jnp.arange(G)[None, None, :, None]
    k_win = jnp.pad(kw_raw, ((0, 0), (WIN, 0), (0, 0), (0, 0)))
    v_win = jnp.pad(vw_raw, ((0, 0), (WIN, 0), (0, 0), (0, 0)))

    def block(qi):
        q0 = qi * Q_BLOCK
        t = q0 + jnp.arange(Q_BLOCK)
        qb = lax.dynamic_slice_in_dim(q, q0, Q_BLOCK, axis=1)
        gb = lax.dynamic_slice_in_dim(gates, q0, Q_BLOCK, axis=1)
        s_c = jnp.einsum("bqgrd,bngd->bqgrn", qb, k_cmp) * scale
        m_c = (cmp_last[None, :] <= t[:, None])[None, :, None, None, :]
        p_c, _, _ = _masked_softmax(s_c, m_c)
        o_c = jnp.einsum("bqgrn,bngd->bqgrd", p_c.astype(qb.dtype), v_cmp)
        imp = jnp.einsum("bqgrn,ns->bqgs", p_c, overlap)
        blk = jnp.arange(n_slc)[None, :]
        cur = (t // SLC_BLOCK)[:, None]
        forced = (blk == 0) | (blk == cur) | (blk == cur - 1)
        causal = blk * SLC_BLOCK <= t[:, None]
        imp = jnp.where(forced[None, :, None, :], FORCE_SCORE, imp)
        imp = jnp.where(causal[None, :, None, :], imp, -1.0)
        _, sel = lax.top_k(imp, top)
        k_sel = k_slc[b_ix, g_ix, sel]
        v_sel = v_slc[b_ix, g_ix, sel].reshape(B, Q_BLOCK, G, top * SLC_BLOCK, E)
        pos = sel[..., None] * SLC_BLOCK + jnp.arange(SLC_BLOCK)
        m_s = (pos <= t[None, :, None, None, None]).reshape(B, Q_BLOCK, G, 1, top * SLC_BLOCK)
        s_s = jnp.einsum("bqgrd,bqgkld->bqgrkl", qb, k_sel).reshape(
            B, Q_BLOCK, G, R, top * SLC_BLOCK) * scale
        p_s, _, _ = _masked_softmax(s_s, m_s)
        o_s = jnp.einsum("bqgrk,bqgkd->bqgrd", p_s.astype(qb.dtype), v_sel)
        kw = lax.dynamic_slice_in_dim(k_win, q0, WIN + Q_BLOCK, axis=1)
        vw = lax.dynamic_slice_in_dim(v_win, q0, WIN + Q_BLOCK, axis=1)
        kpos = q0 - WIN + jnp.arange(WIN + Q_BLOCK)
        dist = t[:, None] - kpos[None, :]
        m_w = ((dist >= 0) & (dist < WIN) & (kpos[None, :] >= 0))[None, :, None, None, :]
        s_w = jnp.einsum("bqgrd,bkgd->bqgrk", qb, kw) * scale
        p_w, _, _ = _masked_softmax(s_w, m_w)
        o_w = jnp.einsum("bqgrk,bkgd->bqgrd", p_w.astype(qb.dtype), vw)
        return gb[..., 0:1] * o_c + gb[..., 1:2] * o_s + gb[..., 2:3] * o_w

    out = lax.map(block, jnp.arange(T // Q_BLOCK))
    return jnp.moveaxis(out, 0, 1).reshape(B, T, G * R * E)

def _dilated_group(q, k, v, window, dil):
    B, T, H, E = q.shape
    L = T // dil
    Lp = -(-L // DIL_BLOCK) * DIL_BLOCK
    nb = Lp // DIL_BLOCK
    steps = window // dil

    def sub(a):
        a = a.reshape(B, L, dil, H, E).transpose(0, 2, 3, 1, 4)
        a = jnp.pad(a, ((0, 0), (0, 0), (0, 0), (0, Lp - L), (0, 0)))
        return a.reshape(B, dil, H, nb, DIL_BLOCK, E)

    def with_prev(a):
        prev = jnp.concatenate([jnp.zeros_like(a[:, :, :, :1]), a[:, :, :, :-1]], axis=3)
        return jnp.concatenate([prev, a], axis=4)

    qs = sub(q)
    kc = with_prev(sub(k))
    vc = with_prev(sub(v))
    s = jnp.einsum("bdhnqe,bdhnke->bdhnqk", qs, kc) * (E ** -0.5)
    a_i = jnp.arange(DIL_BLOCK)
    c_i = jnp.arange(2 * DIL_BLOCK)
    dist = a_i[:, None] + DIL_BLOCK - c_i[None, :]
    j = jnp.arange(nb)[:, None, None] * DIL_BLOCK - DIL_BLOCK + c_i[None, None, :]
    mask = (dist[None] >= 0) & (dist[None] <= steps) & (j >= 0)
    p, m, den = _masked_softmax(s, mask)
    o = jnp.einsum("bdhnqk,bdhnke->bdhnqe", p.astype(v.dtype), vc)
    lse = (m + jnp.log(den))[..., 0]
    o = o.reshape(B, dil, H, Lp, E)[:, :, :, :L].transpose(0, 3, 1, 2, 4).reshape(B, T, H, E)
    lse = lse.reshape(B, dil, H, Lp)[:, :, :, :L].transpose(0, 3, 1, 2).reshape(B, T, H)
    return o, lse

def _dilated_mixer(q, k, v):
    B, T, _, E = q.shape
    outs, lses = [], []
    for gi, (window, dil) in enumerate(DIL_PAIRS):
        sl = slice(gi * DIL_HEADS_PER_PAIR, (gi + 1) * DIL_HEADS_PER_PAIR)
        o, lse = _dilated_group(q[:, :, sl], k[:, :, sl], v[:, :, sl], window, dil)
        outs.append(o)
        lses.append(lse)
    alpha = jax.nn.softmax(jnp.stack(lses, axis=0), axis=0)
    y = jnp.concatenate([alpha[gi][..., None].astype(outs[gi].dtype) * outs[gi]
                         for gi in range(len(DIL_PAIRS))], axis=2)
    return y.reshape(B, T, DIL_W)

def second_inputs(seed: int = 0) -> dict:
    key = jax.random.key(seed)
    ks = jax.random.split(key, 13)
    f32 = jnp.float32
    x = jax.random.normal(ks[0], (BATCH, SEQ, D_MODEL), f32)
    p = jax.random.normal(ks[1], (DEPTH_2, BATCH, SEQ, PLE_DIM), f32)
    norm_mix = 1.0 + 0.05 * jax.random.normal(ks[2], (DEPTH_2, D_MODEL), f32)
    w_in = jax.random.normal(ks[3], (DEPTH_2, D_MODEL, D_IN), f32) * D_MODEL ** -0.5
    conv_w = jax.random.normal(ks[4], (DEPTH_2, CONV_K, CONV_W), f32) * CONV_K ** -0.5
    conv_b = 0.02 * jax.random.normal(ks[5], (DEPTH_2, CONV_W), f32)
    cmp_pe = 0.5 * jax.random.normal(ks[6], (DEPTH_2, 2, CMP_BLOCK, HEAD_DIM), f32)
    cmp_w1 = jax.random.normal(ks[7], (DEPTH_2, 2, CMP_BLOCK * HEAD_DIM, HEAD_DIM), f32) * (CMP_BLOCK * HEAD_DIM) ** -0.5
    cmp_w2 = jax.random.normal(ks[8], (DEPTH_2, 2, HEAD_DIM, HEAD_DIM), f32) * HEAD_DIM ** -0.5
    w_out = jax.random.normal(ks[9], (DEPTH_2, D_MIX, D_MODEL), f32) * D_MIX ** -0.5
    w_ple_gate = jax.random.normal(ks[10], (DEPTH_2, D_MODEL, D_MODEL), f32) * D_MODEL ** -0.5
    w_ple_proj = jax.random.normal(ks[11], (DEPTH_2, PLE_DIM, D_MODEL), f32) * PLE_DIM ** -0.5
    norm_final = 1.0 + 0.05 * jax.random.normal(ks[12], (D_MODEL,), f32)
    return {"x": x, "p": p, "norm_mix": norm_mix, "w_in": w_in, "conv_w": conv_w,
            "conv_b": conv_b, "cmp_pe": cmp_pe, "cmp_w1": cmp_w1, "cmp_w2": cmp_w2,
            "w_out": w_out, "w_ple_gate": w_ple_gate, "w_ple_proj": w_ple_proj,
            "norm_final": norm_final}

def second_block(x, p, norm_mix, w_in, conv_w, conv_b, cmp_pe, cmp_w1, cmp_w2,
              w_out, w_ple_gate, w_ple_proj, norm_final):
    B, T, _ = x.shape
    E = HEAD_DIM
    split_points = np.cumsum(IN_SIZES)[:-1].tolist()
    h = x
    for i in range(DEPTH_2):
        xn = _rmsnorm(h, norm_mix[i])
        u = xn @ w_in[i]
        (a_b, a_c, a_h, a_z,
         n_q, n_kc, n_vc, n_ks, n_vs, n_kw, n_vw, n_g, n_z,
         d_q, d_k, d_v, d_z) = jnp.split(u, split_points, axis=-1)
        y_a = a_b * _short_conv(a_c * a_h, conv_w[i], conv_b[i]) * jax.nn.silu(a_z)
        kv = lambda a: a.reshape(B, T, NSA_KV_HEADS, E)
        gates = jax.nn.sigmoid(n_g.astype(jnp.float32)).astype(u.dtype).reshape(
            B, T, NSA_KV_HEADS, NSA_GROUP, 3)
        y_b = _nsa(n_q.reshape(B, T, NSA_KV_HEADS, NSA_GROUP, E), kv(n_kc), kv(n_vc),
                   kv(n_ks), kv(n_vs), kv(n_kw), kv(n_vw), gates,
                   cmp_pe[i], cmp_w1[i], cmp_w2[i]) * jax.nn.silu(n_z)
        hd = lambda a: a.reshape(B, T, DIL_HEADS, E)
        y_c = _dilated_mixer(hd(d_q), hd(d_k), hd(d_v)) * jax.nn.silu(d_z)
        h = h + jnp.concatenate([y_a, y_b, y_c], axis=-1) @ w_out[i]
        gate = jax.nn.sigmoid((h @ w_ple_gate[i]).astype(jnp.float32)).astype(h.dtype)
        h = h + gate * (p[i] @ w_ple_proj[i])
    return _rmsnorm(h, norm_final)


def setup_inputs(seed=0):
    out = dict(first_inputs(seed))
    for name, value in second_inputs(seed + 1).items():
        if name != "x":
            out[name + "_2"] = value
    return out


def reference(
    x, positions, norm_mix, norm_ffn, norm_final, pool_w, pool_scale, mla_w_down, mla_q_norm,
    mla_w_uq, mla_kv_norm, mla_w_ukv, mla_w_o, ffn_w_gate, ffn_w_up, ffn_w_down, p_2,
    norm_mix_2, w_in_2, conv_w_2, conv_b_2, cmp_pe_2, cmp_w1_2, cmp_w2_2, w_out_2, w_ple_gate_2,
    w_ple_proj_2, norm_final_2,
):
    x = first_block(
        x, positions, norm_mix, norm_ffn, norm_final, pool_w, pool_scale, mla_w_down,
        mla_q_norm, mla_w_uq, mla_kv_norm, mla_w_ukv, mla_w_o, ffn_w_gate, ffn_w_up, ffn_w_down,
    )
    return second_block(
        x, p_2, norm_mix_2, w_in_2, conv_w_2, conv_b_2, cmp_pe_2, cmp_w1_2, cmp_w2_2, w_out_2,
        w_ple_gate_2, w_ple_proj_2, norm_final_2,
    )


_drawn_inputs = setup_inputs


def setup_inputs(seed=0):
    import zlib

    import numpy as np

    out = dict(_drawn_inputs(seed))
    spreads = {}
    factors = {'norm_mix': 3.482,
     'norm_ffn': 3.234,
     'norm_final': 8.878,
     'pool_scale': 3.473,
     'mla_q_norm': 8.0,
     'mla_kv_norm': 8.0,
     'conv_b_2': 78.855,
     'norm_mix_2': 5.715,
     'cmp_pe_2': 25.025,
     'p_2': 8.0,
     'cmp_w1_2': 3.026,
     'w_ple_gate_2': 8.0,
     'w_ple_proj_2': 8.0}
    for name, (base, spread) in spreads.items():
        noise = np.random.default_rng([zlib.crc32(name.encode()), seed]).standard_normal(out[name].shape)
        drawn = base * np.exp(spread * noise) if base else spread * noise
        out[name] = __import__('jax').numpy.asarray(drawn.astype(out[name].dtype))
    for name, factor in factors.items():
        out[name] = (out[name] * factor).astype(out[name].dtype)
    return out
```

```python
from contextlib import ExitStack

import concourse.bass as bass
from concourse import mybir

F32 = mybir.dt.float32
F32R = mybir.dt.float32r
I32 = mybir.dt.int32
ALU = mybir.AluOpType
ACT = mybir.ActivationFunctionType
AX = mybir.AxisListType

P = 128
T = 512
NB = T // P
D = 1024
KD = D // P
FF = 2816
KF = FF // P
EPS = 1e-6
WINDOWS = (2, 4, 8, 16)
BAND = P + 16
QL, KVL, ROPE = 384, 128, 64
HEADS = 8
NEG = -1e30
U_COLS = 2048
DOWN_SPLIT = ((0, 6), (6, 6), (12, 5), (17, 5))

ROWS = {}
for _name, _n in (("norm_mix", 16), ("norm_ffn", 16), ("norm_final", 8), ("pool_scale", 8), ("norm_mix_2", 8),
                  ("norm_final_2", 8), ("mla_q_norm", 3), ("mla_kv_norm", 1), ("conv_w_2", 6), ("conv_b_2", 2)):
    ROWS[_name] = (sum(n for _, n in ROWS.values()), _n)
NROWS = sum(n for _, n in ROWS.values())


def weight_units():
    first, n = {}, 0
    for name, count in (("pool", 1), ("gateup0", 22), ("down0", 16), ("mla_down", 3), ("heads", 4), ("mla_o", 4),
                        ("gateup1", 22), ("down1", 16), ("w_in", 17), ("compress", 1), ("w_out", 4), ("ple_proj", 1), ("ple_gate", 4)):
        first[name] = n
        n += count
    return first, n


FIRST, UNITS = weight_units()


MARKS = {
    "scalar_mark": ("tok_root", "mix_root", "ffn0_root", "ckv_hi", "kr_hi", "attn_root", "ffn1_root", "inner_root",
                    "gates_ready", "cmp_exp", "fin_root"),
    "tensor_mark": ("vec_turned", "mix_stat", "ffn0_stat", "attn_stat", "ffn1_stat", "inner_stat", "g_turned", "pe_turned",
                    "c_scored", "fin_stat"),
    "vector_mark": ("angle_ready", "cols_ready", "gain2_ready", "tok_rstd", "rope_ready", "sum_clear", "mix_rstd",
                    "ffn0_rstd", "cq_clear", "rq_ready", "rkv_ready", "ckv_ready", "ckv_lo", "kr_ready", "kr_lo",
                    "attn_clear", "attn_rstd", "ffn1_rstd", "inner_ready", "dmask_ready", "kcv_padded", "gates_kept",
                    "pe_kept", "cmp_shifted", "cmp_probs", "fin_clear", "fin_rstd"),
}


def program(nc, a, out):
    ctx = ExitStack()
    with ctx:
        def sb(name, shape, dt=F32, stack=ctx):
            return stack.enter_context(nc.sbuf_tensor(name, shape, dt))

        sems = {}

        def sem(name):
            if name not in sems:
                sems[name] = ctx.enter_context(nc.semaphore(name))
            return sems[name]

        given = {engine: 0 for engine in MARKS}

        def at(name):
            engine = next(e for e, names in MARKS.items() if name in names)
            return sem(engine), MARKS[engine].index(name) + 1

        def mark(name):
            engine = next(e for e, names in MARKS.items() if name in names)
            assert MARKS[engine][given[engine]] == name
            given[engine] += 1
            return sem(engine), 1

        xT = sb("xT", [P, KD, T])
        xg_hi = sb("xg_hi", [P, KD, T], F32R)
        xg_lo = sb("xg_lo", [P, KD, T], F32R)
        w_raw = sb("w_raw", [P, 2, U_COLS])
        w_hi = sb("w_hi", [P, 2, U_COLS], F32R)
        w_lo = sb("w_lo", [P, 2, U_COLS], F32R)
        ident = sb("ident", [P, P])
        ones = sb("ones", [P, P])
        cols = sb("cols", [P, NROWS])
        eps_col = sb("eps_col", [P, 4])
        rstd = sb("rstd", [P, T])
        root = sb("root", [P, T])
        squares = sb("squares", [P, 2, T])
        sq_sum = sb("sq_sum", [P, T])
        sq_sum2 = sb("sq_sum2", [P, T])
        ident_r = sb("ident_r", [P, P], F32R)
        causal = sb("causal", [P, P], F32R)
        neg_max = sb("neg_max", [P, 8])
        row_sum = sb("row_sum", [P, 8])
        row_inv = sb("row_inv", [P, 8])
        rope_col = sb("rope_col", [P, 2])
        gain2 = sb("gain2", [P, KD])
        bank = [ctx.enter_context(nc.psum_tensor(f"bank{i}", [P, T], F32)) for i in range(8)]

        def gain(name, m):
            c = ROWS[name][0] + m
            return cols[:, c:c + 1] if isinstance(c, int) else cols[:, bass.ds(c, 1)]

        rope_mem = ExitStack()
        cos_t = sb("cos_t", [P, T], stack=rope_mem)
        sin_t = sb("sin_t", [P, T], stack=rope_mem)
        pool_mem = ExitStack()
        x_tok = sb("x_tok", [P, NB, D], stack=pool_mem)
        h_tok = sb("h_tok", [P, NB, D], stack=pool_mem)
        pooled_hi = sb("pooled_hi", [P, KD, T], F32R, pool_mem)
        pooled_lo = sb("pooled_lo", [P, KD, T], F32R, pool_mem)
        band = sb("band", [P, len(WINDOWS), 2, BAND], stack=pool_mem)
        tok_stat = sb("tok_stat", [P, 3, NB], stack=pool_mem)
        vec_rows = sb("vec_rows", [P, P], stack=pool_mem)
        pos_i = sb("pos_i", [P, T], I32, pool_mem)
        angle = sb("angle", [P, 3, T], stack=pool_mem)
        masks0 = sb("masks0", [P, P], stack=pool_mem)
        pool_mem.close()

        ffn_mem = ExitStack()
        act_hi = sb("act_hi", [P, KF, T], F32R, ffn_mem)
        act_lo = sb("act_lo", [P, KF, T], F32R, ffn_mem)
        ffn_mem.close()
        gate_z, up_z, gate_s = squares[:, 1, :], squares[:, 0, :], root[:, :]

        mla_mem = ExitStack()
        o_hi = sb("o_hi", [P, HEADS, T], F32R, mla_mem)
        o_lo = sb("o_lo", [P, HEADS, T], F32R, mla_mem)
        pt_hi = sb("pt_hi", [P, 2, NB, T], F32R, mla_mem)
        pt_lo = sb("pt_lo", [P, 2, NB, T], F32R, mla_mem)
        probs = sb("probs", [P, 4, T], stack=mla_mem)
        cq_hi = sb("cq_hi", [P, 3, T], F32R, mla_mem)
        cq_lo = sb("cq_lo", [P, 3, T], F32R, mla_mem)
        ckv_hi = sb("ckv_hi", [P, T], F32R, mla_mem)
        ckv_lo = sb("ckv_lo", [P, T], F32R, mla_mem)
        cos_s = sb("cos_s", [P, T], stack=mla_mem)
        sin_s = sb("sin_s", [P, T], stack=mla_mem)
        mla_mem.close()
        rope_mem.close()

        mix_mem = ExitStack()
        ptc_hi = sb("ptc_hi", [32, T], F32R, mix_mem)
        ptc_lo = sb("ptc_lo", [32, T], F32R, mix_mem)
        q_st = sb("q_st", [P, 6, T], F32R, mix_mem)
        k_st = sb("k_st", [P, 4, 2, T], F32R, mix_mem)
        v_st = sb("v_st", [P, 3, 2, NB, P], F32R, mix_mem)
        br = sb("br", [P, 8, T], stack=mix_mem)
        du = sb("du", [P, 9, T], stack=mix_mem)
        pm = sb("pm", [P, 4, T], stack=mix_mem)
        dmask = sb("dmask", [P, 5, P], F32R, mix_mem)
        cmask = sb("cmask", [P, NB, 32], stack=mix_mem)
        cvalid = sb("cvalid", [P, NB], stack=mix_mem)
        gates = sb("gates", [P, NB, 32], stack=mix_mem)
        kc_st = sb("kc_st", [P, 2, 2, 32], F32R, mix_mem)
        vc_st = sb("vc_st", [32, 2, P], F32R, mix_mem)
        cst = sb("cst", [P, 4, 24], stack=mix_mem)
        pe_rows = sb("pe_rows", [32, 2, P], stack=mix_mem)
        pe_cols = sb("pe_cols", [P, 2, 32], stack=mix_mem)
        w2_t = sb("w2_t", [64, 2, 2, 64], stack=mix_mem)
        h1 = sb("h1", [64, 2, 64], stack=mix_mem)
        mix_mem.close()
        kcv = pm[:, 0:3, :].rearrange("p a t -> p (a t)")[:, 0:2 * 528].rearrange("p (a t) -> p a t", a=2)
        cpe = squares[:, :, :].rearrange("p a t -> p (a t)").rearrange("p (l g n) -> p l g n", l=16, g=2)
        p_cmp = squares[:, :, :].rearrange("p a t -> p (a t)")[:, 0:768]
        pt2_hi, pt2_lo = (x[:, :, :].rearrange("p (b j) t -> p b j t", b=2) for x in (xg_hi, xg_lo))

        tail_mem = ExitStack()
        xs_hi = sb("xs_hi", [P, KD, T], F32R, tail_mem)
        xs_lo = sb("xs_lo", [P, KD, T], F32R, tail_mem)
        p_tok = sb("p_tok", [P, NB, 256], stack=tail_mem)
        p_hi = sb("p_hi", [P, 2, T], F32R, tail_mem)
        p_lo = sb("p_lo", [P, 2, T], F32R, tail_mem)
        emb = sb("emb", [P, KD, T], stack=tail_mem)
        out_tok = sb("out_tok", [P, 4, T], stack=tail_mem)
        fin = sb("fin", [P, 3, 2 * NB], stack=tail_mem)
        tail_mem.close()
        down_q = probs
        QN, KN, VV, QR, KR = 0, 2, 4, 6, 7

        raw_sem = [sem("weights_loaded0"), sem("weights_loaded1")]
        hi_sem, lo_sem = sem("weights_hi"), sem("weights_lo")
        unit_src = {}

        def raw(n):
            return w_raw[:, n % 2, :]

        def tiles256(ap, k):
            return ap[:, 0:k * 256].rearrange("p (k c) -> p k c", k=k)

        unit_src[0] = [(tiles256(raw(0), 8), a["pool_w"].rearrange("l g (k p) d -> p (l g k) d", p=P))]
        wd = a["mla_w_down"][0].rearrange("(k p) n -> p k n", p=P)
        n = FIRST["mla_down"]
        for j in range(2):
            unit_src[n + j] = [(tiles256(raw(n + j), 8), wd[:, :, j * 256:(j + 1) * 256])]
        r0 = QL + KVL
        unit_src[n + 2] = [(tiles256(raw(n + 2), 8)[:, :, c:c + w], wd[:, :, s0:s0 + w]) for c, w, s0 in
                           ((0, 64, r0), (64, 64, r0), (128, 32, r0 + 32), (160, 32, r0), (192, 32, r0 + 32), (224, 32, r0))]
        wq = a["mla_w_uq"][0].rearrange("(k p) n -> p k n", p=P)
        for pr in range(HEADS // 2):
            n = FIRST["heads"] + pr
            t16 = raw(n).rearrange("p (t c) -> p t c", c=P)
            q0, q1 = 2 * pr * 192, (2 * pr + 1) * 192
            unit_src[n] = [(t16[:, 0:3, :], wq[:, :, q0:q0 + P]), (t16[:, 3:6, :], wq[:, :, q1:q1 + P])]
            for e, q in ((0, q0 + P), (64, q1 + P)):
                unit_src[n] += [(t16[:, 6:9, e:e + 64], wq[:, :, q:q + 64]),
                                (t16[:, 9:12, e:e + 32], wq[:, :, q + 32:q + 64]), (t16[:, 9:12, e + 32:e + 64], wq[:, :, q:q + 32])]
            unit_src[n] += [(raw(n)[:, 12 * P:16 * P], a["mla_w_ukv"][0][:, pr * 512:(pr + 1) * 512])]

        def square_units(stage, w):
            wv = w.rearrange("(k p) n -> p k n", p=P)
            for j in range(4):
                n = FIRST[stage] + j
                unit_src[n] = [(tiles256(raw(n), 8), wv[:, :, j * 256:(j + 1) * 256])]

        square_units("mla_o", a["mla_w_o"][0])
        wi = a["w_in_2"][0].rearrange("(k p) n -> p k n", p=P)
        for j in range(17):
            n = FIRST["w_in"] + j
            c0, w = (256 * j, 256) if j < 9 else (2194 + 256 * (j - 9), 256 if j < 16 else 128)
            unit_src[n] = [(tiles256(raw(n), 8)[:, :, 0:w], wi[:, :, c0:c0 + w])]
        n = FIRST["compress"]
        unit_src[n] = [(raw(n)[:, 1024 * j:1024 * (j + 1)].rearrange("p (l c) -> p l c", c=64), a["cmp_w1_2"][0, j].rearrange("(l p) c -> p l c", p=P))
                       for j in range(2)]
        square_units("w_out", a["w_out_2"][0])
        square_units("ple_gate", a["w_ple_gate_2"][0])
        n = FIRST["ple_proj"]
        unit_src[n] = [(raw(n).rearrange("p (k c) -> p k c", k=2), a["w_ple_proj_2"][0].rearrange("(k p) n -> p k n", p=P))]
        loads = [len(unit_src.get(n, [0])) for n in range(UNITS)]

        def loaded(n):
            return 16 * sum(loads[m] for m in range(n % 2, n + 1, 2))

        used = {}

        def hi_tiles(n, k, c=None):
            return tiles256(w_hi[:, n % 2, :], k), tiles256(w_lo[:, n % 2, :], k)

        block = ctx.enter_context(nc.Block())
        used[0] = (sem("mixed_done"), 8)
        for l in range(2):
            for i in range(11):
                used[FIRST[f"gateup{l}"] + 2 * i] = (sem(f"gateup{l}_done"), 4 * i + 2)
                used[FIRST[f"gateup{l}"] + 2 * i + 1] = (sem(f"gateup{l}_done"), 4 * i + 4)
            for d in range(16):
                used[FIRST[f"down{l}"] + d] = (sem(f"down{l}_done"), 2 * d + 2)
        for j in range(3):
            used[FIRST["mla_down"] + j] = (sem("mla_down_done"), 2 * j + 2)
        for pr in range(4):
            used[FIRST["heads"] + pr] = (sem("proj_done"), 8 * pr + 8)
            used[FIRST["mla_o"] + pr] = (sem("mla_o_done"), 2 * pr + 2)
            used[FIRST["w_out"] + pr] = (sem("w_out_done"), 2 * pr + 2)
            used[FIRST["ple_gate"] + pr] = (sem("ple_gate_done"), 2 * pr + 2)
        used[FIRST["ple_proj"]] = (sem("ple_proj_done"), KD)
        used[FIRST["compress"]] = (sem("cmp_hidden"), 2)
        for j in range(17):
            used[FIRST["w_in"] + j] = (sem("u_done"), min(2 * j + 2, 33))

        PROJ = ("qn0", "kn0", "v0", "u", "us", "qn1", "kn1", "v1")

        def after_step(h, ii):
            g, odd = divmod(h + 1, 2)
            if g >= HEADS // 2:
                return ()
            if odd:
                return ((g, ("qn1", "kn1", "v1")[ii]),) if ii < 3 else ()
            return ((g, ("qn0", "kn0", "v0")[ii]),) if ii < 3 else ((g, "u"), (g, "us"))

        ffn_from = ("mix", "attn")
        ffn_to = ("ffn0", "ffn1")
        
        def ffn_gain(l, k):
            if l == 1:
                return gain2[:, bass.ds(k, 1)]
            return cols[:, bass.ds(k + (ROWS["norm_mix"][0] + KD), 1)]

        def inner_gain(k):
            return cols[:, bass.ds(k + ROWS["norm_final"][0], 1)]


        KINDS = (["ab"] * 2 + ["ac"] * 2 + ["ah"] * 2 + ["az"] * 2 + ["nq"] * 3 + ["kc", "vc", "ks", "vs", "kw", "vw", "gate"]
                 + ["z"] * 3 + ["dq"] * 3 + ["dk"] * 3 + ["dv"] * 3 + ["z"] * 3)
        NT = len(KINDS)
        SCRATCHED = [t for t in range(NT) if KINDS[t] in ("nq", "ks", "vs", "kw", "vw", "gate")]
        VTILES = [t for t in range(NT) if KINDS[t] in ("vs", "vw")]

        def u_dst(t):
            kind = KINDS[t]
            if t < 8:
                return br[:, t, :]
            if kind in ("kc", "vc"):
                return kcv[:, int(kind == "vc"), 0:T]
            if kind == "z":
                return br[:, t - 18 if t < 21 else 3 + t - 30, :]
            if kind[0] == "d":
                return du[:, t - 21, :]
            return squares[:, SCRATCHED.index(t) % 2, :]

        NSTEP = [(h, b, i) for h in range(6) for b in range(2) for i in (3, 2, 1, 0)]
        DSTEP = [(j, i) for j in range(2) for i in (3, 2, 1, 0)]

        def d_keys(g, i):
            return list(range(max(i - 1, 0), i + 1)) if g == 0 else list(range(i + 1))

        def d_turned(g, kb, i):
            if g:
                return (slice(None), g - 1, kb, slice(i * P, (i + 1) * P))
            return (slice(None), kb // 2, 2 + kb % 2, slice((i - kb) * P, (i - kb + 1) * P))

        @block.sync
        def _(sp):
            def load(n):
                if n >= 2:
                    sp.wait_ge(lo_sem, n - 1)
                for dst, src in unit_src[n]:
                    sp.dma_start(dst, src).then_inc(raw_sem[n % 2], 16)

            sp.dma_start(x_tok[:, 0:2, :], a["x"][0].rearrange("(i p) f -> p i f", p=P)[:, 0:2]).then_inc(sem("x_loaded0"), 16)
            sp.dma_start(x_tok[:, 2:4, :], a["x"][0].rearrange("(i p) f -> p i f", p=P)[:, 2:4]).then_inc(sem("x_loaded1"), 16)
            sp.dma_start(ident[:, :], a["c_ident"]).then_inc(sem("ident_loaded"), 16)
            for name, (r, n) in ROWS.items():
                v = a[name]
                flat = v if len(v.shape) == 1 else v.rearrange("a b -> (a b)") if len(v.shape) == 2 else v.rearrange("a b c -> (a b c)")
                sp.dma_start(vec_rows[r:r + n, :], flat.rearrange("(r p) -> r p", p=P)).then_inc(sem("vectors_loaded"), 16)
            sp.dma_start(band[:, :, :, :], a["c_band"]).then_inc(sem("band_loaded"), 16)
            sp.dma_start(pos_i[:, :], a["positions"][0:1, :].to_broadcast([P, T])).then_inc(sem("pos_loaded"), 16)
            sp.dma_start(rope_col[:, :], a["c_rope"]).then_inc(sem("pos_loaded"), 16)
            sp.dma_start(masks0[:, :], a["c_masks"][:, 0, :]).then_inc(sem("mask_loaded"), 16)
            load(0)
            for l in range(2):
                if l == 1:
                    for n in range(FIRST["mla_down"], FIRST["gateup1"]):
                        load(n)
                up, gate, down = (a[f"ffn_w_{x}"][l] for x in ("up", "gate", "down"))
                gv, uv = (w.rearrange("(k p) n -> p k n", p=P) for w in (gate, up))
                dv = down.rearrange("(k p) n -> p k n", p=P)
                n0 = FIRST[f"gateup{l}"]
                with sp.Fori(0, 11) as i:
                    for j, src in enumerate((gv, uv)):
                        n = n0 + j
                        sp.wait_ge(lo_sem, i * 2 + (n - 1))
                        sp.dma_start(tiles256(raw(n), 8), src[:, :, bass.ds(i * 256, 256)]).then_inc(raw_sem[n % 2], 16)
                n0 = FIRST[f"down{l}"]
                with sp.Fori(0, 4) as q:
                    for j, (k0, nk) in enumerate(DOWN_SPLIT):
                        n = n0 + j
                        sp.wait_ge(lo_sem, q * 4 + (n - 1))
                        sp.dma_start(tiles256(raw(n), nk), dv[:, k0:k0 + nk, bass.ds(q * 256, 256)]).then_inc(raw_sem[n % 2], 16)

            n_mix, n_out = FIRST["w_in"], FIRST["w_out"]
            for n in range(n_mix, n_mix + 2):
                load(n)
            sp.wait_ge(sem("down1_done"), 32)
            for src, dst in ((a["c_masks"][:, 1:6, :], du[:, 0:2, :].rearrange("p a t -> p (a t)")[:, 0:5 * P].rearrange("p (m c) -> p m c", c=P)),
                             (a["c_cmask"], cmask[:, :, :]), (a["c_cvalid"], cvalid[:, :]),
                             (a["cmp_pe_2"][0].rearrange("j l e -> l j e"), pe_rows[:, :, 0:64]),
                             (a["cmp_pe_2"][0].rearrange("j l e -> l j e"), pe_rows[:, :, 64:128]),
                             (a["cmp_w2_2"][0].rearrange("j a e -> a j e"), w2_t[:, :, 0, :]),
                             (a["cmp_w2_2"][0].rearrange("j a e -> a j e"), w2_t[:, :, 1, :])):
                sp.dma_start(dst, src).then_inc(sem("mix_loaded"), 16)
            for n in range(n_mix + 2, n_out + 1):
                load(n)
            sp.wait_ge(sem("cmp_hidden"), 2)
            load(n_out + 1)
            sp.wait_ge(sem("d_out"), 6)
            sp.dma_start(p_tok[:, :, :], a["p_2"][0, 0].rearrange("(i p) f -> p i f", p=P)).then_inc(sem("p_loaded"), 16)
            for n in range(n_out + 2, UNITS):
                load(n)
            ov = out[0].rearrange("(i p) f -> p i f", p=P)
            for o in range(2 * NB):
                i, half = divmod(o, 2)
                sp.wait_ge(sem("out_ready"), o + 1)
                sp.dma_start(ov[:, i, half * T:(half + 1) * T], out_tok[:, o % 4, :]).then_inc(sem(f"out_stored{o % 4}"), 16)
            for o in range(4):
                sp.wait_ge(sem(f"out_stored{o}"), 32)

        @block.gpsimd
        def _(pool):
            pool.memset(ones[:, :], 1.0).then_inc(sem("ones_set"), 1)
            pool.memset(eps_col[:, 0:1], EPS).then_inc(sem("eps_set"), 1)
            pool.memset(eps_col[:, 1:2], EPS * (128 + ROPE)).then_inc(sem("eps_set"), 1)

        @block.scalar
        def _(act):
            def split_hi(n, waits=()):
                act.wait_ge(raw_sem[n % 2], loaded(n))
                if n >= 2:
                    act.wait_ge(*used[n - 2])
                act.activation(w_hi[:, n % 2, :], raw(n), ACT.Copy).then_inc(hi_sem, 1)

            def chain(tag, k, m, gcol, extra=None):
                act.wait_ge(sem(f"{tag}_dve"), k * 3 + 1)
                act.activation(xg_hi[:, m, :], xT[:, m, :], ACT.Copy, scale=gcol).then_inc(sem(f"{tag}_act"), 1)
                act.activation(squares[:, k % 2 if isinstance(k, int) else 0, :], xT[:, m, :], ACT.Square).then_inc(sem(f"{tag}_act"), 1)

            act.preload_act_table(ACT.Sqrt)
            for i in range(NB):
                act.wait_ge(sem(f"x_loaded{i // 2}"), 16)
                act.activation(h_tok[:, i, :], x_tok[:, i, :], ACT.Square, accum_out=tok_stat[:, 0, i:i + 1]).then_inc(sem("tok_squares"), 1)
            act.wait_ge(sem("eps_set"), 2)
            act.wait_ge(sem("tok_squares"), NB)
            act.activation(tok_stat[:, 1, :], tok_stat[:, 0, :], ACT.Sqrt, scale=1.0 / D, bias=eps_col[:, 0:1]).then_inc(*mark("tok_root"))
            act.preload_act_table(ACT.Sin)
            act.wait_ge(*at("angle_ready"))
            act.activation(sin_t[:, :], angle[:, 0, :], ACT.Sin).then_inc(sem("sin_done"), 1)
            act.activation(cos_t[:, :], angle[:, 1, :], ACT.Sin).then_inc(sem("sin_done"), 1)
            act.preload_act_table(ACT.Sqrt)
            split_hi(0)
            act.wait_ge(*at("cols_ready"))
            for c in range(KD):
                act.wait_ge(sem("pooled_done"), c + 1)
                act.activation(pooled_hi[:, c, :], bank[4 + c % 2][:, :], ACT.Copy, scale=gain("norm_mix", c)).then_inc(sem("pooled_hi"), 1)
            split_hi(1)
            for m in range(KD):
                chain("mix", m, m, gain("norm_ffn", m))

            def ffn(l):
                tag, to = ffn_from[l], ffn_to[l]
                n0, d0 = FIRST[f"gateup{l}"], FIRST[f"down{l}"]
                gu, gd, ga = sem(f"gateup{l}_done"), sem(f"gated{l}_dve"), sem(f"gated{l}_act")
                act.wait_ge(*at(f"{tag}_stat"))
                act.activation(root[:, :], bank[7][:, :], ACT.Sqrt, scale=1.0 / D, bias=eps_col[:, 0:1]).then_inc(*mark(f"{tag}_root"))
                act.preload_act_table(ACT.Silu)
                act.wait_ge(*used[n0 - 1])

                def gateup_turn(i, first):
                    for j in (1, 2):
                        n = n0 + j
                        act.wait_ge(raw_sem[n % 2], i * 16 + loaded(n))
                        if not (first and j == 1):
                            act.wait_ge(gu, i * 4 + 2 * (j - 1))
                        act.activation(w_hi[:, n % 2, :], raw(n), ACT.Copy).then_inc(hi_sem, 1)
                    for c in range(2):
                        act.wait_ge(gd, i * 8 + 4 * c + 1)
                        act.activation(gate_s, gate_z, ACT.Silu).then_inc(ga, 1)
                        act.wait_ge(gd, i * 8 + 4 * c + 3)
                        act.activation(act_hi[:, bass.ds(i * 2 + c, 1), :].rearrange("p a t -> p (a t)"), gate_z, ACT.Copy).then_inc(ga, 1)
                gateup_turn(0, True)
                with act.Fori(1, 11) as i:
                    gateup_turn(i, False)
                dn = sem(f"down{l}_done")

                def down_turn(q, first):
                    for j in range(4):
                        n = d0 + j + 1
                        act.wait_ge(raw_sem[n % 2], q * 32 + loaded(n))
                        if first and j == 0:
                            act.wait_ge(gu, 44)
                        else:
                            act.wait_ge(dn, q * 8 + 2 * j)
                        act.activation(w_hi[:, n % 2, :], raw(n), ACT.Copy).then_inc(hi_sem, 1)
                    for c in range(2):
                        k = q * 2 + c
                        act.wait_ge(sem(f"{to}_dve"), q * (6 + 2 * l) + (3 + l) * c + 1)
                        xt = xT[:, bass.ds(k, 1), :].rearrange("p a t -> p (a t)")
                        act.activation(xg_hi[:, bass.ds(k, 1), :].rearrange("p a t -> p (a t)"), xt, ACT.Copy,
                                       scale=ffn_gain(l, k)).then_inc(sem(f"{to}_act"), 1)
                        act.activation(squares[:, c, :], xt, ACT.Square).then_inc(sem(f"{to}_act"), 1)
                        if l == 1:
                            act.activation(root[:, :], xt, ACT.Square, scale=inner_gain(k)).then_inc(sem(f"{to}_act"), 1)

                down_turn(0, True)
                with act.Fori(1, 4) as q:
                    down_turn(q, False)

            def mla():
                n0 = FIRST["mla_down"]
                s2 = 1.0 / (128 + ROPE)
                act.wait_ge(*at("ffn0_stat"))
                act.activation(root[:, :], bank[7][:, :], ACT.Sqrt, scale=1.0 / D, bias=eps_col[:, 0:1]).then_inc(*mark("ffn0_root"))
                split_hi(n0 + 1)
                for t in range(4):
                    act.wait_ge(sem("down_q_ready"), t + 1)
                    if t < 3:
                        act.activation(cq_hi[:, t, :], down_q[:, t, :], ACT.Copy, scale=gain("mla_q_norm", t)).then_inc(sem("cq_act"), 1)
                    if t >= 2:
                        act.wait_ge(sem("cq_sum"), t - 1)
                    act.activation(squares[:, t % 2, :], down_q[:, t, :], ACT.Square).then_inc(sem("cq_act"), 1)
                    if t == 1:
                        split_hi(n0 + 2)
                split_hi(n0 + 3)
                act.wait_ge(sem("cq_stat"), 1)
                act.activation(root[:, :], bank[6][:, :], ACT.Sqrt, scale=1.0 / (QL * s2), bias=eps_col[:, 1:2]).then_inc(sem("cq_root"), 1)
                act.wait_ge(sem("cq_stat"), 2)
                act.activation(squares[:, 0, :], bank[7][:, :], ACT.Sqrt, scale=1.0 / KVL, bias=eps_col[:, 0:1]).then_inc(sem("cq_root"), 1)
                act.preload_act_table(ACT.Exp)
                act.wait_ge(*at("ckv_ready"))
                act.activation(ckv_hi[:, :], down_q[:, 3, :], ACT.Copy).then_inc(*mark("ckv_hi"))
                act.wait_ge(*at("kr_ready"))
                act.activation(xg_hi[:, KR, :], down_q[:, 0, :], ACT.Copy).then_inc(*mark("kr_hi"))

                def proj(pr, what):
                    idx = 8 * pr + PROJ.index(what)
                    h = 2 * pr + int(what[-1] == "1")
                    if what == "u":
                        return
                    if what in ("us", "qn0", "qn1"):
                        act.wait_ge(sem("proj_tmp"), 3 * pr + ("qn0", "us", "qn1").index(what) + 1)
                        src = root[:, :] if what != "us" else squares[:, 0, :]
                    else:
                        act.wait_ge(sem("proj_done"), idx + 1)
                        src = bank[idx % 2][:, :]
                    slot = QR if what == "us" else {"q": QN, "k": KN, "v": VV}[what[0]] + h % 2
                    if what == "us" and pr >= 1:
                        act.wait_ge(sem("att_scored"), 8 * pr)
                    elif what[0] in "qk" and h >= 2:
                        act.wait_ge(sem("att_scored"), 4 * (h - 1))
                    elif what[0] == "v" and h >= 2:
                        act.wait_ge(sem("att_out_done"), h - 1)
                    act.activation(xg_hi[:, slot, :], src, ACT.Copy).then_inc(sem("proj_hi"), 1)

                for what in PROJ[:5]:
                    proj(0, what)

                def softmax_exp(s):
                    act.wait_ge(sem("att_max"), s + 1)
                    if s >= 4:
                        act.wait_ge(sem("att_turned"), s - 3)
                    w = (NB - s % NB) * P
                    act.activation(probs[:, s % 4, 0:w], bank[2 + s % 3][:, 0:w], ACT.Exp, bias=neg_max[:, s % 8:s % 8 + 1],
                                   accum_out=row_sum[:, s % 8:s % 8 + 1]).then_inc(sem("att_exp"), 1)

                def turned_hi(s):
                    h, ii = divmod(s, NB)
                    i = NB - 1 - ii
                    act.wait_ge(sem("att_turned"), s + 1)
                    if h >= 2:
                        act.wait_ge(sem("att_out_done"), h - 1)
                    act.activation(pt_hi[:, h % 2, 0:i + 1, i * P:(i + 1) * P], bank[5 + s % 2][:, 0:(i + 1) * P].rearrange("p (j q) -> p j q", q=P),
                                   ACT.Copy).then_inc(sem("att_hi"), 1)

                def head_out(h):
                    act.wait_ge(sem("att_out_done"), h + 1)
                    act.activation(o_hi[:, h, :], bank[7][:, :], ACT.Copy).then_inc(sem("att_out_hi"), 1)

                for s in range(NB * HEADS + 5):
                    h, ii = divmod(s, NB)
                    if s < NB * HEADS:
                        softmax_exp(s)
                    if 0 <= s - 2 < NB * HEADS:
                        turned_hi(s - 2)
                    if s < NB * HEADS:
                        for t in after_step(h, ii):
                            proj(*t)
                        if h % 2 == 0 and ii == 3:
                            split_hi(FIRST["heads"] + 1 + h // 2)
                    if s >= 7 and (s - 4) % NB == NB - 1:
                        head_out((s - 4) // NB)
                act.preload_act_table(ACT.Sqrt)
                for u in range(1, 5):
                    split_hi(FIRST["mla_o"] + u)
                    for m in (2 * u - 2, 2 * u - 1):
                        chain("attn", m, m, gain("norm_ffn", 8 + m))

            def w_in():
                n0 = FIRST["w_in"]
                act.wait_ge(*at("ffn1_stat"))
                act.activation(root[:, :], bank[7][:, :], ACT.Sqrt, scale=1.0 / D, bias=eps_col[:, 0:1]).then_inc(*mark("ffn1_root"))
                split_hi(n0 + 1)
                act.wait_ge(*at("inner_ready"))
                act.activation(root[:, :], sq_sum[:, :], ACT.Sqrt, scale=1.0 / D, bias=eps_col[:, 0:1]).then_inc(*mark("inner_root"))
                act.preload_act_table(ACT.Silu)
                for t in range(NT):
                    kind = KINDS[t]
                    ready = (sem("u_free"), t + 1)
                    if kind == "az":
                        act.wait_ge(*ready)
                        act.activation(br[:, t, :], br[:, t, :], ACT.Silu).then_inc(sem("conv_gate"), 1)
                    elif kind == "z":
                        act.wait_ge(*ready)
                        act.activation(u_dst(t), u_dst(t), ACT.Silu).then_inc(sem("z_gate"), 1)
                    elif kind == "nq":
                        act.wait_ge(*ready)
                        for e in range(2):
                            r = slice(64 * e, 64 * e + 64)
                            act.activation(q_st[r, 2 * (t - 8) + e, :], u_dst(t)[r, :], ACT.Copy, scale=0.125).then_inc(sem("nq_hi"), 1)
                    elif kind in ("ks", "kw"):
                        act.wait_ge(*ready)
                        for g in range(2):
                            for e in range(2):
                                act.activation(k_st[64 * e:64 * e + 64, 2 * int(kind == "kw") + g, 0, :], u_dst(t)[64 * g:64 * g + 64, :], ACT.Copy)\
                                   .then_inc(sem("nk_hi"), 1)
                    elif kind == "gate":
                        act.preload_act_table(ACT.Sigmoid)
                        act.wait_ge(*ready)
                        act.activation(u_dst(t)[0:32, :], u_dst(t)[0:32, :], ACT.Sigmoid).then_inc(*mark("gates_ready"))
                        act.preload_act_table(ACT.Silu)
                    if t - 2 in VTILES:
                        v = VTILES.index(t - 2)
                        act.wait_ge(sem("nv_turned"), v + 1)
                        act.activation(v_st[:, v, :, :, 0:64], bank[5 + v][:, :].rearrange("p (j h d) -> p h j d", h=2, d=64), ACT.Copy)\
                           .then_inc(sem("nv_hi"), 1)
                    if t % 2 == 0 and t // 2 + 2 <= 18:
                        split_hi(n0 + t // 2 + 2)

            def compress():
                for kv in range(2):
                    act.wait_ge(sem("cmp_hidden"), kv + 1)
                    act.activation(h1[:, kv, :], bank[kv][0:64, 0:64], ACT.Silu).then_inc(sem("cmp_act"), 1)
                act.preload_act_table(ACT.Exp)
                act.wait_ge(sem("cmp_done"), 1)
                act.activation(kc_st[:, 0, :, :].rearrange("p g n -> p (g n)"), bank[2][:, 0:64], ACT.Copy).then_inc(sem("cmp_kv_hi"), 1)
                act.wait_ge(sem("cmp_done"), 2)
                act.activation(vc_st[:, :, 0:64], bank[3][0:32, 0:P].rearrange("n (g e) -> n g e", g=2), ACT.Copy).then_inc(sem("cmp_kv_hi"), 1)
                act.wait_ge(*at("cmp_shifted"))
                act.activation(p_cmp, p_cmp, ACT.Exp).then_inc(*mark("cmp_exp"))

            def nsa():
                def softmax_exp(s):
                    h, b, i = NSTEP[s]
                    act.wait_ge(sem("n_max"), s + 1)
                    if s >= 4:
                        act.wait_ge(sem("n_turned"), s - 3)
                    w = (i + 1) * P
                    act.activation(pm[:, s % 4, 0:w], bank[s % 4][:, 0:w], ACT.Exp, bias=neg_max[:, s % 8:s % 8 + 1],
                                   accum_out=row_sum[:, s % 8:s % 8 + 1]).then_inc(sem("n_exp"), 1)

                def turned_hi(s):
                    i, u = NSTEP[s][2], s // NB
                    act.wait_ge(sem("n_turned"), s + 1)
                    if u >= 2:
                        act.wait_ge(sem("n_pv"), u - 1)
                    act.activation(pt2_hi[:, u % 2, 0:i + 1, i * P:(i + 1) * P], bank[5 + s % 2][:, 0:(i + 1) * P].rearrange("p (j q) -> p j q", q=P),
                                   ACT.Copy).then_inc(sem("n_hi"), 1)

                for s in range(len(NSTEP) + 5):
                    if s < len(NSTEP):
                        softmax_exp(s)
                        if s % 8 == 0:
                            h = s // 8
                            act.wait_ge(sem("c_turned"), h + 1)
                            if h:
                                act.wait_ge(sem("n_pv"), 2 * h - 1)
                            act.activation(ptc_hi[:, :], bank[4][0:32, :], ACT.Copy).then_inc(sem("c_hi"), 1)
                    if 0 <= s - 2 < len(NSTEP):
                        turned_hi(s - 2)
                    if s >= 11 and (s - 4) % 8 == 7:
                        h = (s - 4) // 8
                        act.wait_ge(sem("n_pv"), 2 * h + 2)
                        if h:
                            act.wait_ge(sem("n_sum"), h)
                        act.activation(root[0:64, :], bank[7][64:128, :], ACT.Copy).then_inc(sem("n_out_act"), 1)

            def dilated():
                act.wait_ge(sem("n_scored"), len(NSTEP))
                for g in range(3):
                    for e in range(2):
                        r = slice(64 * e, 64 * e + 64)
                        act.activation(q_st[r, 2 * g + e, :], du[r, g, :], ACT.Copy, scale=0.125).then_inc(sem("dq_hi"), 1)
                kd = k_st[:, :, :, :].rearrange("p a b t -> p (a b) t")

                def keys(j):
                    if j:
                        act.wait_ge(sem("d_scored"), 12)
                    for g in range(3):
                        for e in range(2):
                            act.activation(kd[64 * e:64 * e + 64, 2 * g, :], du[64 * j:64 * j + 64, 3 + g, :], ACT.Copy).then_inc(sem("dk_hi"), 1)

                keys(0)
                for g in range(3):
                    act.wait_ge(sem("dv_turned"), g + 1)
                    act.activation(v_st[:, g, :, :, 0:64], bank[5 + g % 2][:, :].rearrange("p (j h d) -> p h j d", h=2, d=64), ACT.Copy)\
                       .then_inc(sem("dv_hi"), 1)

                def softmax_exp(s):
                    j, i = DSTEP[s]
                    act.wait_ge(sem("d_max"), s + 1)
                    for g in range(3):
                        x = 3 * s + g
                        if x >= 4:
                            act.wait_ge(sem("d_turned"), x - 3)
                        w = len(d_keys(g, i)) * P
                        act.activation(pm[:, x % 4, 0:w], bank[x % 5][:, 0:w], ACT.Exp, bias=neg_max[:, 4 + s % 2:5 + s % 2],
                                       accum_out=row_sum[:, 4 * (s % 2) + g:4 * (s % 2) + g + 1]).then_inc(sem("d_exp"), 1)

                def turned_hi(s):
                    j, i = DSTEP[s]
                    for g in range(3):
                        x = 3 * s + g
                        act.wait_ge(sem("d_turned"), x + 1)
                        if j:
                            act.wait_ge(sem("d_pv"), 3)
                        for n, kb in enumerate(d_keys(g, i)) if g == 0 else ((0, slice(0, i + 1)),):
                            src = bank[5 + x % 2][:, n * P:(n + 1) * P] if g == 0 else \
                                bank[5 + x % 2][:, 0:(i + 1) * P].rearrange("p (j q) -> p j q", q=P)
                            act.activation(pt2_hi[d_turned(g, kb, i)], src, ACT.Copy).then_inc(sem("d_hi"), 1)

                def out(j):
                    for g in range(3):
                        act.wait_ge(sem("d_pv"), 3 * j + g + 1)
                        act.wait_ge(sem("n_sum"), 6)
                        if 3 * j + g:
                            act.wait_ge(sem("d_out"), 3 * j + g)
                        act.activation(root[0:64, :], bank[7][64:128, :], ACT.Copy).then_inc(sem("d_out_act"), 1)

                for s in range(len(DSTEP) + 1):
                    if s == 4:
                        keys(1)
                    if s < len(DSTEP):
                        softmax_exp(s)
                    if s:
                        turned_hi(s - 1)
                    if s == 4:
                        out(0)
                out(1)

            def tail():
                n_out, n_pp, n_pg = FIRST["w_out"], FIRST["ple_proj"], FIRST["ple_gate"]
                act.preload_act_table(ACT.Sigmoid)
                for f in range(KD):
                    if f == 0:
                        act.wait_ge(sem("conv_step"), 14)
                        act.wait_ge(sem("d_pv"), 6)
                    elif f == 2:
                        act.wait_ge(sem("n_sum"), 6)
                    elif f >= 5:
                        act.wait_ge(sem("d_out"), f - 1)
                    act.activation(xg_hi[:, f, :], br[:, (f + 6) % 8, :], ACT.Copy).then_inc(sem("y_hi"), 1)
                for j in range(2):
                    act.wait_ge(sem("p_turned"), j + 1)
                    act.activation(p_hi[:, j, :], bank[5 + j][:, :], ACT.Copy).then_inc(sem("p_hi_ready"), 1)
                for m in range(KD):
                    if m % 2 == 0:
                        split_hi(n_out + m // 2 + 1)
                    act.wait_ge(sem("w_out_added"), m + 1)
                    act.activation(xs_hi[:, m, :], xT[:, m, :], ACT.Copy).then_inc(sem("xs_hi_ready"), 1)
                split_hi(n_pg)
                for m in range(KD):
                    if m % 2 == 0 and m < 6:
                        split_hi(n_pg + m // 2 + 1)
                    act.wait_ge(sem("ple_gate_done"), m + 1)
                    if m >= 2:
                        act.wait_ge(sem("ple_dve"), 3 * (m - 2) + 1)
                    act.activation((root, rstd)[m % 2][:, :], bank[m % 4][:, :], ACT.Sigmoid).then_inc(sem("ple_act"), 1)
                    act.wait_ge(sem("ple_dve"), 3 * m + 2)
                    act.activation(squares[:, m % 2, :], xT[:, m, :], ACT.Square).then_inc(sem("ple_act"), 1)
                    act.activation(emb[:, m, :], xT[:, m, :], ACT.Copy, scale=gain("norm_final_2", m)).then_inc(sem("fin_gained"), 1)
                act.preload_act_table(ACT.Sqrt)
                act.wait_ge(*at("fin_stat"))
                act.activation(fin[:, 0, :], bank[4][:, 0:2 * NB], ACT.Sqrt, scale=1.0 / D, bias=eps_col[:, 0:1]).then_inc(*mark("fin_root"))
                act.wait_ge(*at("fin_rstd"))
                for o in range(1, 2 * NB, 2):
                    i = o // 2
                    act.wait_ge(sem("fin_turned"), o + 1)
                    if o >= 4:
                        act.wait_ge(sem(f"out_stored{o % 4}"), 16)
                    act.wait_ge(sem("out_ready"), o)
                    act.activation(out_tok[:, o % 4, :], bank[o % 4][:, :], ACT.Copy, scale=fin[:, 1, 2 * i:2 * i + 1]).then_inc(sem("out_ready"), 1)

            ffn(0)
            mla()
            ffn(1)
            w_in()
            compress()
            nsa()
            dilated()
            tail()

        @block.vector
        def _(dve):
            def split_lo(n):
                dve.wait_ge(hi_sem, n + 1)
                dve.tensor_tensor(w_lo[:, n % 2, :], raw(n), w_hi[:, n % 2, :].bitcast(F32), ALU.subtract).then_inc(lo_sem, 1)

            def chain(tag, k, m, gcol, c=None):
                dv, ac = sem(f"{tag}_dve"), sem(f"{tag}_act")
                dve.wait_ge(ac, k * 2 + 1)
                dve.scalar_tensor_tensor(xg_lo[:, m, :], xT[:, m, :], gcol, xg_hi[:, m, :].bitcast(F32), ALU.mult, ALU.subtract).then_inc(dv, 1)
                dve.wait_ge(ac, k * 2 + 2)
                dve.wait_ge(dv, k * 3)
                dve.tensor_tensor(sq_sum[:, :], sq_sum[:, :], squares[:, c if c is not None else k % 2, :], ALU.add).then_inc(dv, 1)

            MAGIC, TWO_PI = 1.5 * 2.0 ** 23, 6.283185307179586
            parts = (6.28125, 0.001934051513671875, 1.2556659146019695e-06)
            ang = sem("angle_step")
            dve.wait_ge(sem("pos_loaded"), 32)
            dve.tensor_copy(angle[:, 0, :], pos_i[:, :]).then_inc(ang, 1)
            dve.wait_ge(ang, 1)
            dve.tensor_scalar(angle[:, 0, :], angle[:, 0, :], rope_col[:, 0:1], None, ALU.mult).then_inc(ang, 1)
            dve.wait_ge(ang, 2)
            dve.tensor_scalar(angle[:, 1, :], angle[:, 0, :], 1.0 / TWO_PI, MAGIC, ALU.mult, ALU.add).then_inc(ang, 1)
            dve.wait_ge(ang, 3)
            dve.tensor_scalar(angle[:, 1, :], angle[:, 1, :], MAGIC, None, ALU.subtract).then_inc(ang, 1)
            for n, c in enumerate(parts):
                dve.wait_ge(ang, 4 + n)
                dve.scalar_tensor_tensor(angle[:, 0, :], angle[:, 1, :], -c, angle[:, 0, :], ALU.mult, ALU.add).then_inc(ang, 1)
            dve.wait_ge(ang, 7)
            dve.tensor_scalar(angle[:, 0, :], angle[:, 0, :], 3.1415925, -3.1415925, ALU.min, ALU.max).then_inc(ang, 1)
            dve.wait_ge(ang, 8)
            dve.tensor_scalar(angle[:, 1, :], angle[:, 0, :], TWO_PI / 4, None, ALU.is_gt).then_inc(ang, 1)
            dve.tensor_scalar(angle[:, 2, :], angle[:, 0, :], TWO_PI / 4, None, ALU.add).then_inc(ang, 1)
            dve.wait_ge(ang, 10)
            dve.scalar_tensor_tensor(angle[:, 1, :], angle[:, 1, :], -TWO_PI, angle[:, 2, :], ALU.mult, ALU.add).then_inc(ang, 1)
            dve.wait_ge(ang, 11)
            dve.tensor_scalar(angle[:, 1, :], angle[:, 1, :], 3.1415925, -3.1415925, ALU.min, ALU.max).then_inc(*mark("angle_ready"))
            dve.wait_ge(sem("ident_loaded"), 16)
            dve.tensor_copy(ident_r[:, :], ident[:, :]).then_inc(sem("masks_ready"), 1)
            dve.wait_ge(sem("mask_loaded"), 16)
            dve.tensor_copy(causal[:, :], masks0[:, :]).then_inc(sem("masks_ready"), 1)
            dve.wait_ge(*at("vec_turned"))
            dve.tensor_copy(cols[:, :], bank[7][:, 0:NROWS]).then_inc(*mark("cols_ready"))
            dve.wait_ge(*at("cols_ready"))
            f0, m0 = ROWS["norm_final"][0], ROWS["norm_mix_2"][0]
            dve.tensor_tensor(gain2[:, :], cols[:, f0:f0 + KD], cols[:, m0:m0 + KD], ALU.mult).then_inc(*mark("gain2_ready"))
            dve.wait_ge(*at("tok_root"))
            dve.reciprocal(tok_stat[:, 2, :], tok_stat[:, 1, :]).then_inc(*mark("tok_rstd"))
            dve.wait_ge(*at("tok_rstd"))
            for i in range(NB):
                dve.tensor_scalar(h_tok[:, i, :], x_tok[:, i, :], tok_stat[:, 2, i:i + 1], None, ALU.mult).then_inc(sem("h_tok_ready"), 1)
            dve.wait_ge(sem("sin_done"), 2)
            dve.tensor_scalar(sin_t[:, :], sin_t[:, :], rope_col[:, 1:2], None, ALU.mult).then_inc(*mark("rope_ready"))
            split_lo(0)
            for m in range(KD):
                dve.wait_ge(sem("x_turned"), m + 1)
                dve.tensor_copy(xT[:, m, :], bank[m % 4][:, :]).then_inc(sem("xT_ready"), 1)
            dve.memset(sq_sum[:, :], 0.0).then_inc(*mark("sum_clear"))
            dve.wait_ge(*at("cols_ready"))
            for c in range(KD):
                dve.wait_ge(sem("pooled_hi"), c + 1)
                dve.scalar_tensor_tensor(pooled_lo[:, c, :], bank[4 + c % 2][:, :], gain("norm_mix", c), pooled_hi[:, c, :].bitcast(F32),
                                         ALU.mult, ALU.subtract).then_inc(sem("pooled_lo"), 1)
            split_lo(1)
            dve.wait_ge(sem("xT_ready"), KD)
            dve.wait_ge(*at("sum_clear"))
            for m in range(KD):
                dve.wait_ge(sem("mixed_done"), m + 1)
                dve.scalar_tensor_tensor(xT[:, m, :], bank[m % 4][:, :], gain("pool_scale", m), xT[:, m, :], ALU.mult, ALU.add).then_inc(sem("mix_dve"), 1)
                chain("mix", m, m, gain("norm_ffn", m))

            def ffn(l):
                tag, to = ffn_from[l], ffn_to[l]
                n0, d0 = FIRST[f"gateup{l}"], FIRST[f"down{l}"]
                gu, gd, ga, dn = sem(f"gateup{l}_done"), sem(f"gated{l}_dve"), sem(f"gated{l}_act"), sem(f"down{l}_done")
                dve.wait_ge(*at(f"{tag}_root"))
                dve.reciprocal(rstd[:, :], root[:, :]).then_inc(*mark(f"{tag}_rstd"))
                dve.memset(sq_sum[:, :], 0.0).then_inc(sem(f"{to}_clear"), 1)
                dve.memset(sq_sum2[:, :], 0.0).then_inc(sem(f"{to}_clear"), 1)
                dve.wait_ge(*at(f"{tag}_rstd"))
                dve.wait_ge(sem(f"{to}_clear"), 2)

                def gateup_turn(i, first):
                    for j in (1, 2):
                        n = n0 + j
                        dve.wait_ge(hi_sem, i * 2 + (n + 1))
                        dve.tensor_tensor(w_lo[:, n % 2, :], raw(n), w_hi[:, n % 2, :].bitcast(F32), ALU.subtract).then_inc(lo_sem, 1)
                    for c in range(2):
                        dve.wait_ge(gu, i * 4 + c + 1)
                        if not (first and c == 0):
                            dve.wait_ge(gd, i * 8 + 4 * c)
                        dve.tensor_tensor(gate_z, bank[c][:, :], rstd[:, :], ALU.mult).then_inc(gd, 1)
                        dve.wait_ge(gu, i * 4 + c + 3)
                        dve.tensor_tensor(up_z, bank[2 + c][:, :], rstd[:, :], ALU.mult).then_inc(gd, 1)
                        dve.wait_ge(gd, i * 8 + 4 * c + 2)
                        dve.wait_ge(ga, i * 4 + 2 * c + 1)
                        dve.tensor_tensor(gate_z, gate_s, up_z, ALU.mult).then_inc(gd, 1)
                        dve.wait_ge(ga, i * 4 + 2 * c + 2)
                        f = bass.ds(i * 2 + c, 1)
                        dve.tensor_tensor(act_lo[:, f, :].rearrange("p a t -> p (a t)"), gate_z,
                                          act_hi[:, f, :].bitcast(F32).rearrange("p a t -> p (a t)"), ALU.subtract).then_inc(gd, 1)
                gateup_turn(0, True)
                with dve.Fori(1, 11) as i:
                    gateup_turn(i, False)
                dv, ac = sem(f"{to}_dve"), sem(f"{to}_act")

                def down_turn(q, first):
                    for j in range(4):
                        n = d0 + j + 1
                        dve.wait_ge(hi_sem, q * 4 + (n + 1))
                        dve.tensor_tensor(w_lo[:, n % 2, :], raw(n), w_hi[:, n % 2, :].bitcast(F32), ALU.subtract).then_inc(lo_sem, 1)
                    for c in range(2):
                        k = q * 2 + c
                        xt = xT[:, bass.ds(k, 1), :].rearrange("p a t -> p (a t)")
                        xh = xg_hi[:, bass.ds(k, 1), :].bitcast(F32).rearrange("p a t -> p (a t)")
                        xl = xg_lo[:, bass.ds(k, 1), :].rearrange("p a t -> p (a t)")
                        dve.wait_ge(dn, q * 8 + 7 + c)
                        dve.tensor_tensor(xt, bank[c][:, :], xt, ALU.add).then_inc(dv, 1)
                        dve.wait_ge(ac, q * (4 + 2 * l) + (2 + l) * c + 1)
                        dve.scalar_tensor_tensor(xl, xt, ffn_gain(l, k), xh, ALU.mult, ALU.subtract).then_inc(dv, 1)
                        dve.wait_ge(ac, q * (4 + 2 * l) + (2 + l) * c + 2)
                        if not (first and c == 0):
                            dve.wait_ge(dv, q * (6 + 2 * l) + (3 + l) * c)
                        dve.tensor_tensor(sq_sum[:, :], sq_sum[:, :], squares[:, c, :], ALU.add).then_inc(dv, 1)
                        if l == 1:
                            dve.wait_ge(ac, q * 6 + 3 * c + 3)
                            dve.tensor_tensor(sq_sum2[:, :], sq_sum2[:, :], root[:, :], ALU.add).then_inc(dv, 1)

                down_turn(0, True)
                with dve.Fori(1, 4) as q:
                    down_turn(q, False)

            def mla():
                n0 = FIRST["mla_down"]
                dve.wait_ge(*at("ffn0_root"))
                dve.reciprocal(rstd[:, :], root[:, :]).then_inc(*mark("ffn0_rstd"))
                dve.memset(sq_sum[:, :], 0.0).then_inc(*mark("cq_clear"))
                split_lo(n0 + 1)
                dve.wait_ge(*at("ffn0_rstd"))
                dve.wait_ge(*at("rope_ready"))
                dve.tensor_tensor(cos_s[:, :], cos_t[:, :], rstd[:, :], ALU.mult).then_inc(sem("rope_scaled"), 1)
                dve.tensor_tensor(sin_s[:, :], sin_t[:, :], rstd[:, :], ALU.mult).then_inc(sem("rope_scaled"), 1)
                dve.wait_ge(*at("cq_clear"))
                for t in range(4):
                    dve.wait_ge(sem("mla_down_done"), t + 1)
                    dve.tensor_tensor(down_q[:, t, :], bank[t][:, :], rstd[:, :], ALU.mult).then_inc(sem("down_q_ready"), 1)
                    if t < 3:
                        dve.wait_ge(sem("cq_act"), 2 * t + 1)
                        dve.scalar_tensor_tensor(cq_lo[:, t, :], down_q[:, t, :], gain("mla_q_norm", t), cq_hi[:, t, :].bitcast(F32),
                                                 ALU.mult, ALU.subtract).then_inc(sem("cq_lo"), 1)
                        dve.wait_ge(sem("cq_act"), 2 * t + 2)
                        if t:
                            dve.wait_ge(sem("cq_sum"), t)
                        dve.tensor_tensor(sq_sum[:, :], sq_sum[:, :], squares[:, t % 2, :], ALU.add).then_inc(sem("cq_sum"), 1)
                    if t == 1:
                        split_lo(n0 + 2)
                split_lo(n0 + 3)
                dve.wait_ge(sem("cq_root"), 1)
                dve.wait_ge(sem("down_q_ready"), 4)
                dve.reciprocal(rstd[:, :], root[:, :]).then_inc(*mark("rq_ready"))
                dve.wait_ge(sem("cq_root"), 2)
                dve.reciprocal(sq_sum2[:, :], squares[:, 0, :]).then_inc(*mark("rkv_ready"))
                dve.wait_ge(*at("rkv_ready"))
                dve.scalar_tensor_tensor(down_q[:, 3, :], down_q[:, 3, :], gain("mla_kv_norm", 0), sq_sum2[:, :], ALU.mult, ALU.mult)\
                   .then_inc(*mark("ckv_ready"))
                dve.wait_ge(*at("ckv_hi"))
                dve.tensor_tensor(ckv_lo[:, :], down_q[:, 3, :], ckv_hi[:, :].bitcast(F32), ALU.subtract).then_inc(*mark("ckv_lo"))
                dve.wait_ge(sem("mla_down_done"), 5)
                dve.wait_ge(sem("rope_scaled"), 2)
                dve.wait_ge(sem("cq_lo"), 3)
                dve.tensor_tensor(down_q[:, 0, :], bank[4][:, :], cos_s[:, :], ALU.mult).then_inc(sem("kr_step"), 1)
                dve.wait_ge(sem("mla_down_done"), 6)
                dve.tensor_tensor(down_q[:, 1, :], bank[5][:, :], sin_s[:, :], ALU.mult).then_inc(sem("kr_step"), 1)
                dve.wait_ge(sem("kr_step"), 2)
                dve.tensor_tensor(down_q[:, 0, :], down_q[:, 0, :], down_q[:, 1, :], ALU.add).then_inc(*mark("kr_ready"))
                dve.wait_ge(*at("rq_ready"))
                dve.tensor_tensor(cos_s[:, :], cos_t[:, :], rstd[:, :], ALU.mult).then_inc(sem("rope_scaled"), 1)
                dve.tensor_tensor(sin_s[:, :], sin_t[:, :], rstd[:, :], ALU.mult).then_inc(sem("rope_scaled"), 1)
                dve.wait_ge(*at("kr_hi"))
                dve.tensor_tensor(xg_lo[:, KR, :], down_q[:, 0, :], xg_hi[:, KR, :].bitcast(F32), ALU.subtract).then_inc(*mark("kr_lo"))
                dve.wait_ge(sem("rope_scaled"), 4)

                def proj(pr, what):
                    idx = 8 * pr + PROJ.index(what)
                    h = 2 * pr + int(what[-1] == "1")
                    ps = bank[idx % 2][:, :]
                    dve.wait_ge(sem("proj_done"), idx + 1)
                    done = sem("proj_ready")
                    if idx:
                        dve.wait_ge(done, idx)
                    if what == "u":
                        dve.tensor_tensor(squares[:, 0, :], ps, cos_s[:, :], ALU.mult).then_inc(done, 1)
                        return
                    hi = 7 * pr + [x for x in PROJ if x != "u"].index(what) + 1
                    if what == "us":
                        dve.tensor_tensor(squares[:, 1, :], ps, sin_s[:, :], ALU.mult).then_inc(sem("rope_step"), 1)
                        dve.wait_ge(sem("rope_step"), pr + 1)
                        dve.tensor_tensor(squares[:, 0, :], squares[:, 0, :], squares[:, 1, :], ALU.add).then_inc(sem("proj_tmp"), 1)
                        src, slot = squares[:, 0, :], QR
                    elif what[0] == "q":
                        dve.tensor_tensor(root[:, :], ps, rstd[:, :], ALU.mult).then_inc(sem("proj_tmp"), 1)
                        src, slot = root[:, :], QN + h % 2
                    else:
                        src, slot = ps, {"k": KN, "v": VV}[what[0]] + h % 2
                    dve.wait_ge(sem("proj_hi"), hi)
                    dve.tensor_tensor(xg_lo[:, slot, :], src, xg_hi[:, slot, :].bitcast(F32), ALU.subtract).then_inc(done, 1)

                for what in PROJ[:5]:
                    proj(0, what)

                def row_max(s):
                    w = (NB - s % NB) * P
                    dve.wait_ge(sem("att_scored"), s + 1)
                    dve.tensor_reduce(neg_max[:, s % 8:s % 8 + 1], bank[2 + s % 3][:, 0:w], AX.X, ALU.max, negate=True).then_inc(sem("att_max"), 1)

                def normalise(s):
                    w = (NB - s % NB) * P
                    dve.wait_ge(sem("att_exp"), s + 1)
                    dve.reciprocal(row_inv[:, s % 8:s % 8 + 1], row_sum[:, s % 8:s % 8 + 1]).then_inc(sem("att_inv"), 1)
                    dve.wait_ge(sem("att_inv"), s + 1)
                    dve.tensor_scalar(probs[:, s % 4, 0:w], probs[:, s % 4, 0:w], row_inv[:, s % 8:s % 8 + 1], None, ALU.mult)\
                       .then_inc(sem("att_probs"), 1)

                def turned_lo(s):
                    h, ii = divmod(s, NB)
                    i = NB - 1 - ii
                    dve.wait_ge(sem("att_hi"), s + 1)
                    at = (slice(None), h % 2, slice(0, i + 1), slice(i * P, (i + 1) * P))
                    dve.tensor_tensor(pt_lo[at], bank[5 + s % 2][:, 0:(i + 1) * P].rearrange("p (j q) -> p j q", q=P),
                                      pt_hi[at].bitcast(F32), ALU.subtract).then_inc(sem("att_lo"), 1)

                def head_out(h):
                    dve.wait_ge(sem("att_out_hi"), h + 1)
                    dve.tensor_tensor(o_lo[:, h, :], bank[7][:, :], o_hi[:, h, :].bitcast(F32), ALU.subtract).then_inc(sem("att_out"), 1)

                for s in range(NB * HEADS + 5):
                    h, ii = divmod(s, NB)
                    if s < NB * HEADS:
                        row_max(s)
                    if 0 <= s - 1 < NB * HEADS:
                        normalise(s - 1)
                    if 0 <= s - 2 < NB * HEADS:
                        turned_lo(s - 2)
                    if s < NB * HEADS:
                        for t in after_step(h, ii):
                            proj(*t)
                        if h % 2 == 0 and ii == 3:
                            split_lo(FIRST["heads"] + 1 + h // 2)
                    if s >= 7 and (s - 4) % NB == NB - 1:
                        head_out((s - 4) // NB)
                dve.memset(sq_sum[:, :], 0.0).then_inc(*mark("attn_clear"))
                dve.wait_ge(*at("attn_clear"))
                for u in range(1, 5):
                    split_lo(FIRST["mla_o"] + u)
                    for m in (2 * u - 2, 2 * u - 1):
                        dve.wait_ge(sem("mla_o_done"), m + 1)
                        dve.tensor_tensor(xT[:, m, :], bank[m % 4][:, :], xT[:, m, :], ALU.add).then_inc(sem("attn_dve"), 1)
                        chain("attn", m, m, gain("norm_ffn", 8 + m))

            def w_in():
                n0 = FIRST["w_in"]
                dve.wait_ge(*at("ffn1_root"))
                dve.reciprocal(rstd[:, :], root[:, :]).then_inc(*mark("ffn1_rstd"))
                dve.wait_ge(*at("ffn1_rstd"))
                dve.wait_ge(*at("inner_stat"))
                dve.tensor_tensor(sq_sum[:, :], bank[6][:, :], rstd[:, :], ALU.mult).then_inc(sem("inner_step"), 1)
                dve.wait_ge(sem("inner_step"), 1)
                dve.tensor_tensor(sq_sum[:, :], sq_sum[:, :], rstd[:, :], ALU.mult).then_inc(*mark("inner_ready"))
                split_lo(n0 + 1)
                dve.wait_ge(*at("inner_root"))
                dve.reciprocal(sq_sum2[:, :], root[:, :]).then_inc(sem("inner_step"), 1)
                dve.wait_ge(sem("inner_step"), 2)
                dve.tensor_tensor(sq_sum2[:, :], sq_sum2[:, :], rstd[:, :], ALU.mult).then_inc(sem("inner_step"), 1)
                dve.wait_ge(sem("mix_loaded"), 7 * 16)
                dve.tensor_copy(dmask[:, :, :].rearrange("p m c -> p (m c)"), du[:, 0:2, :].rearrange("p a t -> p (a t)")[:, 0:5 * P]).then_inc(*mark("dmask_ready"))
                dve.memset(kcv[:, :, T:528], 0.0).then_inc(*mark("kcv_padded"))
                dve.wait_ge(sem("inner_step"), 3)

                cv = sem("conv_step")

                def conv(n):
                    c0 = 7 * n
                    tap = lambda k: gain("conv_w_2", 2 * k + n)
                    v, c, b, z = br[:, 2 + n, :], br[:, 4 + n, :], br[:, n, :], br[:, 6 + n, :]
                    dve.wait_ge(sem("u_free"), 8)
                    dve.tensor_tensor(v, v, c, ALU.mult).then_inc(cv, 1)
                    dve.wait_ge(cv, c0 + 1)
                    dve.tensor_scalar(c, v, tap(2), gain("conv_b_2", n), ALU.mult, ALU.add).then_inc(cv, 1)
                    for k in (1, 2):
                        dve.wait_ge(cv, c0 + 1 + k)
                        dve.scalar_tensor_tensor(c[:, k:T], v[:, 0:T - k], tap(2 - k), c[:, k:T], ALU.mult, ALU.add).then_inc(cv, 1)
                    dve.wait_ge(cv, c0 + 4)
                    dve.tensor_tensor(b, b, c, ALU.mult).then_inc(cv, 1)
                    dve.wait_ge(cv, c0 + 5)
                    dve.wait_ge(sem("conv_gate"), n + 1)
                    dve.tensor_tensor(z, z, b, ALU.mult).then_inc(cv, 2)

                for t in range(NT):
                    kind, dst = KINDS[t], u_dst(t)
                    dve.wait_ge(sem("u_done"), t + 1)
                    if t in SCRATCHED and SCRATCHED.index(t) >= 2:
                        last = SCRATCHED[SCRATCHED.index(t) - 2]
                        if KINDS[last] == "nq":
                            dve.wait_ge(sem("nq_lo"), 2 * (last - 8) + 2)
                        elif KINDS[last][0] == "k":
                            dve.wait_ge(sem("nk_lo"), 4 + 4 * int(KINDS[last] == "kw"))
                        elif KINDS[last][0] == "v":
                            dve.wait_ge(sem("nv_turned"), VTILES.index(last) + 1)
                    if kind == "z":
                        dve.wait_ge(cv, 14)
                    dve.tensor_tensor(dst, bank[t % 4][:, :], sq_sum2[:, :], ALU.mult).then_inc(sem("u_free"), 1)
                    if kind == "nq":
                        for e in range(2):
                            r, other = slice(64 * e, 64 * e + 64), slice(64 - 64 * e, 128 - 64 * e)
                            h = 2 * (t - 8) + e
                            dve.wait_ge(sem("nq_hi"), h + 1)
                            dve.scalar_tensor_tensor(q_st[other, h, :], dst[r, :], 0.125, q_st[r, h, :].bitcast(F32), ALU.mult, ALU.subtract)\
                               .then_inc(sem("nq_lo"), 1)
                    elif kind in ("ks", "kw"):
                        b = int(kind == "kw")
                        for g in range(2):
                            r = slice(64 * g, 64 * g + 64)
                            dve.wait_ge(sem("nk_hi"), 4 * b + 2 * g + 2)
                            for e in range(2):
                                dve.tensor_tensor(k_st[64 * e:64 * e + 64, 2 * b + g, 1, :], dst[r, :], k_st[r, 2 * b + g, 0, :].bitcast(F32),
                                                  ALU.subtract).then_inc(sem("nk_lo"), 1)
                    if t - 2 in VTILES:
                        v = VTILES.index(t - 2)
                        dve.wait_ge(sem("nv_hi"), v + 1)
                        dve.tensor_tensor(v_st[:, v, :, :, 64:128], bank[5 + v][:, :].rearrange("p (j h d) -> p h j d", h=2, d=64),
                                          v_st[:, v, :, :, 0:64].bitcast(F32), ALU.subtract).then_inc(sem("nv_lo"), 1)
                    if t == 19:
                        dve.wait_ge(*at("g_turned"))
                        dve.tensor_copy(gates[:, :, :].rearrange("p i c -> p (i c)"), bank[5][:, 0:P]).then_inc(*mark("gates_kept"))
                    if t == 8:
                        conv(0)
                    if t == 10:
                        conv(1)
                    if t >= 24 and t < 32:
                        m = t - 24
                        dve.wait_ge(sem("ffn1_act"), 24)
                        dve.scalar_tensor_tensor(xT[:, m, :], xT[:, m, :], gain("norm_final", m), rstd[:, :], ALU.mult, ALU.mult)\
                           .then_inc(sem("x_normed"), 1)
                    if t % 2 == 0 and t // 2 + 2 <= 18:
                        split_lo(n0 + t // 2 + 2)

            def compress():
                dve.wait_ge(*at("pe_turned"))
                dve.tensor_copy(pe_cols[:, :, :].rearrange("p j l -> p (j l)"), bank[6][:, 0:64]).then_inc(*mark("pe_kept"))
                dve.wait_ge(*at("pe_kept"))
                dve.wait_ge(*at("kcv_padded"))
                dve.wait_ge(sem("u_free"), NT)
                for kv in range(2):
                    if kv:
                        dve.wait_ge(sem("cmp_hidden"), 1)
                    for g in range(2):
                        for par in range(2):
                            r = slice(64 * g, 64 * g + 64)
                            win = bass.AP(kcv.tensor, kcv[r, kv, par:par + 1].offset,
                                                                                       [list(kcv[r, kv, 0:1].ap[0]), [2, 16], [16, 32]])
                            off = pe_cols[r, kv, par:32:2].rearrange("p (l o) -> p l o", o=1).to_broadcast([64, 16, 32])
                            dve.tensor_tensor(cpe[64 * par:64 * par + 64, :, g, :], win, off, ALU.add).then_inc(sem("cmp_windows"), 1)
                dve.wait_ge(sem("cmp_kv_hi"), 1)
                dve.tensor_tensor(kc_st[:, 1, :, :].rearrange("p g n -> p (g n)"), bank[2][:, 0:64],
                                  kc_st[:, 0, :, :].bitcast(F32).rearrange("p g n -> p (g n)"), ALU.subtract).then_inc(sem("cmp_kv_lo"), 1)
                dve.wait_ge(sem("cmp_kv_hi"), 2)
                dve.tensor_tensor(vc_st[:, :, 64:128], bank[3][0:32, 0:P].rearrange("n (g e) -> n g e", g=2),
                                  vc_st[:, :, 0:64].bitcast(F32), ALU.subtract).then_inc(sem("cmp_kv_lo"), 1)
                st = sem("cmp_step")
                dve.wait_ge(*at("c_scored"))
                dve.wait_ge(sem("cmp_hidden"), 2)
                cm = cmask[:, :, :].rearrange("p i n -> p (i n)").rearrange("p (o c) -> p o c", o=1)
                dve.tensor_tensor(p_cmp[:, 0:512].rearrange("p (h c) -> p h c", h=4), bank[0][:, :].rearrange("p (h c) -> p h c", h=4),
                                  cm.to_broadcast([P, 4, P]), ALU.add).then_inc(st, 1)
                dve.tensor_tensor(p_cmp[:, 512:768].rearrange("p (h c) -> p h c", h=2), bank[1][:, 0:256].rearrange("p (h c) -> p h c", h=2),
                                  cm.to_broadcast([P, 2, P]), ALU.add).then_inc(st, 1)
                dve.wait_ge(st, 2)
                pc = p_cmp.rearrange("p (x n) -> p x n", n=32)
                wide = lambda k: cst[:, k, :].rearrange("p (x o) -> p x o", o=1).to_broadcast([P, 24, 32])
                dve.tensor_reduce(cst[:, 0, :], pc, AX.X, ALU.max).then_inc(st, 1)
                dve.wait_ge(st, 3)
                dve.tensor_tensor(pc, pc, wide(0), ALU.subtract).then_inc(*mark("cmp_shifted"))
                dve.wait_ge(*at("cmp_exp"))
                dve.tensor_reduce(cst[:, 1, :], pc, AX.X, ALU.add).then_inc(st, 1)
                dve.wait_ge(st, 4)
                dve.reciprocal(cst[:, 2, :], cst[:, 1, :]).then_inc(st, 1)
                dve.wait_ge(st, 5)
                hi_ = lambda k: cst[:, k, :].rearrange("p (h i) -> p h i", h=6)
                dve.tensor_tensor(hi_(2), hi_(2), cvalid[:, :].rearrange("p (o i) -> p o i", o=1).to_broadcast([P, 6, NB]), ALU.mult).then_inc(st, 1)
                dve.wait_ge(st, 6)
                dve.wait_ge(*at("gates_kept"))
                dve.tensor_tensor(hi_(3), hi_(2), gates[:, :, 0:18:3].rearrange("p i h -> p h i"), ALU.mult).then_inc(st, 1)
                dve.wait_ge(st, 7)
                dve.tensor_tensor(pc, pc, wide(3), ALU.mult).then_inc(*mark("cmp_probs"))

            def add_halves(r, dst, done):
                dve.tensor_tensor(sq_sum[r, :], bank[7][0:64, :], root[0:64, :], ALU.add).then_inc(sem("halves"), 1)
                sums[0] += 1
                dve.wait_ge(sem("halves"), sums[0])
                dve.tensor_tensor(dst, dst, sq_sum[r, :], ALU.mult).then_inc(done, 1)

            sums = [0]

            def nsa():
                dve.wait_ge(sem("z_gate"), 6)

                def row_max(s):
                    i = NSTEP[s][2]
                    dve.wait_ge(sem("n_scored"), s + 1)
                    dve.tensor_reduce(neg_max[:, s % 8:s % 8 + 1], bank[s % 4][:, 0:(i + 1) * P], AX.X, ALU.max, negate=True).then_inc(sem("n_max"), 1)

                def normalise(s):
                    h, b, i = NSTEP[s]
                    w = (i + 1) * P
                    dve.wait_ge(sem("n_exp"), s + 1)
                    dve.reciprocal(row_inv[:, s % 8:s % 8 + 1], row_sum[:, s % 8:s % 8 + 1]).then_inc(sem("n_inv"), 1)
                    dve.wait_ge(sem("n_inv"), s + 1)
                    c = 3 * h + 1 + b
                    dve.tensor_scalar(pm[:, s % 4, 0:w], pm[:, s % 4, 0:w], row_inv[:, s % 8:s % 8 + 1], gates[:, i, c:c + 1], ALU.mult, ALU.mult)\
                       .then_inc(sem("n_probs"), 1)

                def turned_lo(s):
                    i, u = NSTEP[s][2], s // NB
                    dve.wait_ge(sem("n_hi"), s + 1)
                    at = (slice(None), u % 2, slice(0, i + 1), slice(i * P, (i + 1) * P))
                    dve.tensor_tensor(pt2_lo[at], bank[5 + s % 2][:, 0:(i + 1) * P].rearrange("p (j q) -> p j q", q=P),
                                      pt2_hi[at].bitcast(F32), ALU.subtract).then_inc(sem("n_lo"), 1)

                for s in range(len(NSTEP) + 5):
                    if s < len(NSTEP):
                        row_max(s)
                        if s % 8 == 0:
                            dve.wait_ge(sem("c_hi"), s // 8 + 1)
                            dve.tensor_tensor(ptc_lo[:, :], bank[4][0:32, :], ptc_hi[:, :].bitcast(F32), ALU.subtract).then_inc(sem("c_lo"), 1)
                    if 0 <= s - 1 < len(NSTEP):
                        normalise(s - 1)
                    if 0 <= s - 2 < len(NSTEP):
                        turned_lo(s - 2)
                    if s >= 11 and (s - 4) % 8 == 7:
                        h = (s - 4) // 8
                        r = slice(64 * (h % 2), 64 * (h % 2) + 64)
                        dve.wait_ge(sem("n_out_act"), h + 1)
                        add_halves(r, br[r, h // 2, :], sem("n_sum"))

            def dilated():
                for g in range(3):
                    for e in range(2):
                        r, other = slice(64 * e, 64 * e + 64), slice(64 - 64 * e, 128 - 64 * e)
                        dve.wait_ge(sem("dq_hi"), 2 * g + e + 1)
                        dve.scalar_tensor_tensor(q_st[other, 2 * g + e, :], du[r, g, :], 0.125, q_st[r, 2 * g + e, :].bitcast(F32),
                                                 ALU.mult, ALU.subtract).then_inc(sem("dq_lo"), 1)
                kd = k_st[:, :, :, :].rearrange("p a b t -> p (a b) t")

                def keys(j):
                    r = slice(64 * j, 64 * j + 64)
                    for g in range(3):
                        dve.wait_ge(sem("dk_hi"), 6 * j + 2 * g + 2)
                        for e in range(2):
                            dve.tensor_tensor(kd[64 * e:64 * e + 64, 2 * g + 1, :], du[r, 3 + g, :], kd[r, 2 * g, :].bitcast(F32), ALU.subtract)\
                               .then_inc(sem("dk_lo"), 1)

                keys(0)
                for g in range(3):
                    dve.wait_ge(sem("dv_hi"), g + 1)
                    dve.tensor_tensor(v_st[:, g, :, :, 64:128], bank[5 + g % 2][:, :].rearrange("p (j h d) -> p h j d", h=2, d=64),
                                      v_st[:, g, :, :, 0:64].bitcast(F32), ALU.subtract).then_inc(sem("dv_lo"), 1)

                def row_max(s):
                    j, i = DSTEP[s]
                    if s >= 2:
                        dve.wait_ge(sem("d_exp"), 3 * (s - 1))
                    for g in range(3):
                        x = 3 * s + g
                        dve.wait_ge(sem("d_scored"), x + 1)
                        dve.tensor_reduce(row_inv[:, 4 * (s % 2) + g:4 * (s % 2) + g + 1], bank[x % 5][:, 0:len(d_keys(g, i)) * P], AX.X, ALU.max)\
                           .then_inc(sem("d_max3"), 1)
                    dve.wait_ge(sem("d_max3"), 3 * s + 3)
                    dve.tensor_reduce(neg_max[:, 4 + s % 2:5 + s % 2], row_inv[:, 4 * (s % 2):4 * (s % 2) + 3], AX.X, ALU.max, negate=True)\
                       .then_inc(sem("d_max"), 1)

                def normalise(s):
                    j, i = DSTEP[s]
                    c = 4 * (s % 2)
                    dve.wait_ge(sem("d_exp"), 3 * s + 3)
                    dve.tensor_reduce(neg_max[:, s % 2:s % 2 + 1], row_sum[:, c:c + 3], AX.X, ALU.add).then_inc(sem("d_inv"), 1)
                    dve.wait_ge(sem("d_inv"), 2 * s + 1)
                    dve.reciprocal(neg_max[:, 2 + s % 2:3 + s % 2], neg_max[:, s % 2:s % 2 + 1]).then_inc(sem("d_inv"), 1)
                    dve.wait_ge(sem("d_inv"), 2 * s + 2)
                    for g in range(3):
                        x = 3 * s + g
                        w = len(d_keys(g, i)) * P
                        dve.tensor_scalar(pm[:, x % 4, 0:w], pm[:, x % 4, 0:w], neg_max[:, 2 + s % 2:3 + s % 2], None, ALU.mult).then_inc(sem("d_probs"), 1)

                parts = [0]

                def turned_lo(s):
                    j, i = DSTEP[s]
                    for g in range(3):
                        x = 3 * s + g
                        todo = [(n, kb) for n, kb in enumerate(d_keys(g, i))] if g == 0 else [(0, slice(0, i + 1))]
                        parts[0] += len(todo)
                        dve.wait_ge(sem("d_hi"), parts[0])
                        for m, (n, kb) in enumerate(todo):
                            src = bank[5 + x % 2][:, n * P:(n + 1) * P] if g == 0 else \
                                bank[5 + x % 2][:, 0:(i + 1) * P].rearrange("p (j q) -> p j q", q=P)
                            at = d_turned(g, kb, i)
                            dve.tensor_tensor(pt2_lo[at], src, pt2_hi[at].bitcast(F32), ALU.subtract)\
                               .then_inc(sem("d_lo") if m == len(todo) - 1 else sem("d_lo_part"), 1)

                def out(j):
                    for g in range(3):
                        r = slice(64 * j, 64 * j + 64)
                        dve.wait_ge(sem("d_out_act"), 3 * j + g + 1)
                        add_halves(r, br[r, 3 + g, :], sem("d_out"))

                for s in range(len(DSTEP) + 1):
                    if s == 4:
                        keys(1)
                    if s < len(DSTEP):
                        row_max(s)
                    if s:
                        normalise(s - 1)
                        turned_lo(s - 1)
                    if s == 4:
                        out(0)
                out(1)

            def tail():
                n_out, n_pp, n_pg = FIRST["w_out"], FIRST["ple_proj"], FIRST["ple_gate"]
                for f in range(KD):
                    dve.wait_ge(sem("y_hi"), f + 1)
                    dve.tensor_tensor(xg_lo[:, f, :], br[:, (f + 6) % 8, :], xg_hi[:, f, :].bitcast(F32), ALU.subtract).then_inc(sem("y_lo"), 1)
                for j in range(2):
                    dve.wait_ge(sem("p_hi_ready"), j + 1)
                    dve.tensor_tensor(p_lo[:, j, :], bank[5 + j][:, :], p_hi[:, j, :].bitcast(F32), ALU.subtract).then_inc(sem("p_lo_ready"), 1)
                dve.memset(sq_sum[:, :], 0.0).then_inc(*mark("fin_clear"))
                dve.wait_ge(sem("x_normed"), KD)
                for m in range(KD):
                    if m % 2 == 0:
                        split_lo(n_out + m // 2 + 1)
                    dve.wait_ge(sem("w_out_done"), m + 1)
                    dve.tensor_tensor(xT[:, m, :], bank[m % 4][:, :], xT[:, m, :], ALU.add).then_inc(sem("w_out_added"), 1)
                    dve.wait_ge(sem("xs_hi_ready"), m + 1)
                    dve.tensor_tensor(xs_lo[:, m, :], xT[:, m, :], xs_hi[:, m, :].bitcast(F32), ALU.subtract).then_inc(sem("xs_lo_ready"), 1)
                split_lo(n_pg)
                for m in range(KD):
                    dve.wait_ge(sem("ple_proj_done"), m + 1)
                    dve.tensor_copy(emb[:, m, :], bank[4 + m % 2][:, :]).then_inc(sem("emb_ready"), 1)
                dve.wait_ge(sem("emb_ready"), KD)
                dve.wait_ge(*at("fin_clear"))
                pd = sem("ple_dve")
                for m in range(KD):
                    if m % 2 == 0 and m < 6:
                        split_lo(n_pg + m // 2 + 1)
                    gate = (root, rstd)[m % 2][:, :]
                    dve.wait_ge(sem("ple_act"), 2 * m + 1)
                    dve.tensor_tensor(gate, gate, emb[:, m, :], ALU.mult).then_inc(sem("ple_step"), 1)
                    dve.wait_ge(sem("ple_step"), m + 1)
                    dve.wait_ge(sem("w_out_added"), KD)
                    dve.tensor_tensor(xT[:, m, :], xT[:, m, :], gate, ALU.add).then_inc(pd, 2)
                    dve.wait_ge(sem("ple_act"), 2 * m + 2)
                    dve.wait_ge(pd, 3 * m)
                    dve.tensor_tensor(sq_sum[:, :], sq_sum[:, :], squares[:, m % 2, :], ALU.add).then_inc(pd, 1)
                dve.wait_ge(*at("fin_root"))
                dve.reciprocal(fin[:, 1, :], fin[:, 0, :]).then_inc(*mark("fin_rstd"))
                dve.wait_ge(*at("fin_rstd"))
                for o in range(0, 2 * NB, 2):
                    i = o // 2
                    dve.wait_ge(sem("fin_turned"), o + 1)
                    if o >= 4:
                        dve.wait_ge(sem(f"out_stored{o % 4}"), 16)
                    if o:
                        dve.wait_ge(sem("out_ready"), o)
                    dve.tensor_scalar(out_tok[:, o % 4, :], bank[o % 4][:, :], fin[:, 1, 2 * i:2 * i + 1], None, ALU.mult).then_inc(sem("out_ready"), 1)

            ffn(0)
            mla()
            ffn(1)
            w_in()
            compress()
            nsa()
            dilated()
            tail()

        @block.tensor
        def _(pe):
            def triple(o, wh, wl, xh, xl, start, stop):
                pe.matmul(o, wh, xh, start=start, stop=False, skip_group_check=True)
                pe.matmul(o, wh, xl, start=False, stop=False, skip_group_check=True)
                return pe.matmul(o, wl, xh, start=False, stop=stop, skip_group_check=True)

            def chunk(o, n, nk, c, xh, xl, start=True, stop=True, k0=0, before=None):
                wh, wl = hi_tiles(n, nk)
                for k in range(nk):
                    if before:
                        before(k)
                    mm = triple(o, wh[:, k, c * P:(c + 1) * P], wl[:, k, c * P:(c + 1) * P], xh[:, k0 + k, :], xl[:, k0 + k, :],
                                start and k == 0, stop and k == nk - 1)
                return mm

            pe.wait_ge(sem("ident_loaded"), 16)
            pe.wait_ge(sem("vectors_loaded"), 16 * len(ROWS))
            pe.transpose(bank[7][:, 0:NROWS], vec_rows[0:NROWS, :], ident[0:NROWS, 0:NROWS]).then_inc(*mark("vec_turned"))
            for m in range(KD):
                if m >= 4:
                    pe.wait_ge(sem("xT_ready"), m - 3)
                for i in range(NB):
                    pe.wait_ge(sem(f"x_loaded{i // 2}"), 16)
                    mm = pe.transpose(bank[m % 4][:, i * P:(i + 1) * P], x_tok[:, i, m * P:(m + 1) * P], ident[:, :])
                mm.then_inc(sem("x_turned"), 1)
            pe.wait_ge(sem("band_loaded"), 16)
            for c in range(KD):
                if c >= 2:
                    pe.wait_ge(sem("pooled_lo"), c - 1)
                for i in range(NB):
                    pe.wait_ge(sem("h_tok_ready"), i + 1)
                    n = min(BAND, T - i * P)
                    mm = pe.matmul(bank[4 + c % 2][:, i * P:i * P + n], h_tok[:, i, c * P:(c + 1) * P], band[:, c // 2, int(i == 0), 0:n],
                                   start=i == 0, stop=i == NB - 1, skip_group_check=True)
                mm.then_inc(sem("pooled_done"), 1)
            pe.wait_ge(lo_sem, 1)
            pe.wait_ge(sem("xT_ready"), KD)
            wh, wl = hi_tiles(0, 8)
            for m in range(KD):
                g, c = divmod(m, 2)
                if m >= 4:
                    pe.wait_ge(sem("mix_dve"), 3 * (m - 4) + 1)
                for k in range(2):
                    pe.wait_ge(sem("pooled_lo"), 2 * g + k + 1)
                    mm = triple(bank[m % 4][:, :], wh[:, 2 * g + k, c * P:(c + 1) * P], wl[:, 2 * g + k, c * P:(c + 1) * P],
                                pooled_hi[:, 2 * g + k, :], pooled_lo[:, 2 * g + k, :], k == 0, k == 1)
                mm.then_inc(sem("mixed_done"), 1)

            def stat(tag):
                pe.wait_ge(sem(f"{tag}_dve"), 3 * KD)
                pe.wait_ge(sem("ones_set"), 1)
                pe.matmul(bank[7][:, :], ones[:, :], sq_sum[:, :], start=True, stop=True).then_inc(*mark(f"{tag}_stat"))

            def ffn(l):
                tag, to = ffn_from[l], ffn_to[l]
                n0, d0 = FIRST[f"gateup{l}"], FIRST[f"down{l}"]
                gu, gd, dn = sem(f"gateup{l}_done"), sem(f"gated{l}_dve"), sem(f"down{l}_done")

                def turn(i, first):
                    for j in range(2):
                        n = n0 + j
                        pe.wait_ge(lo_sem, i * 2 + (n + 1))
                        for c in range(2):
                            if not first:
                                pe.wait_ge(gd, i * 8 + (4 * c + j + 1 - 8))
                            before = (lambda k: pe.wait_ge(sem(f"{tag}_dve"), 3 * k + 2)) if first and j == c == 0 else None
                            chunk(bank[2 * j + c][:, :], n, 8, c, xg_hi, xg_lo, before=before).then_inc(gu, 1)
                            if first and j == c == 0:
                                stat(tag)

                pe.wait_ge(sem(f"{tag}_dve"), 3 * 7 + 1)
                turn(0, True)
                with pe.Fori(1, 11) as i:
                    turn(i, False)

                def down_turn(q, first):
                    for j, (k0, nk) in enumerate(DOWN_SPLIT):
                        n = d0 + j
                        pe.wait_ge(lo_sem, q * 4 + (n + 1))
                        for c in range(2):
                            if first and j == c == 0:
                                pe.wait_ge(gd, 88)
                            if not first and j == 0:
                                pe.wait_ge(sem(f"{to}_dve"), q * (6 + 2 * l))
                            chunk(bank[c][:, :], n, nk, c, act_hi, act_lo, j == 0, j == 3, k0).then_inc(dn, 1)

                down_turn(0, True)
                with pe.Fori(1, 4) as q:
                    down_turn(q, False)

            def mla():
                n0 = FIRST["mla_down"]
                for idx in range(6):
                    n, c = n0 + idx // 2, idx % 2
                    pe.wait_ge(lo_sem, n + 1)
                    if idx == 0:
                        pe.wait_ge(sem("ffn0_dve"), 3 * 7 + 1)
                    before = (lambda k: pe.wait_ge(sem("ffn0_dve"), 3 * k + 2)) if idx == 0 else None
                    chunk(bank[idx][:, :], n, 8, c, xg_hi, xg_lo, before=before).then_inc(sem("mla_down_done"), 1)
                    if idx == 0:
                        stat("ffn0")
                    if idx == 4:
                        pe.wait_ge(sem("cq_sum"), 3)
                        pe.matmul(bank[6][:, :], ones[:, :], sq_sum[:, :], start=True, stop=True).then_inc(sem("cq_stat"), 1)
                        pe.wait_ge(sem("cq_act"), 7)
                        pe.wait_ge(*at("ffn0_root"))
                        pe.matmul(bank[7][:, :], ones[:, :], squares[:, 1, :], start=True, stop=True).then_inc(sem("cq_stat"), 1)

                def proj(pr, what):
                    idx = 8 * pr + PROJ.index(what)
                    n = FIRST["heads"] + pr
                    wh, wl = (w[:, n % 2, :].rearrange("p (t c) -> p t c", c=P) for w in (w_hi, w_lo))
                    ps = bank[idx % 2]
                    pe.wait_ge(lo_sem, n + 1)
                    if idx < 2:
                        pe.wait_ge(sem("down_q_ready"), 4)
                    else:
                        pe.wait_ge(sem("proj_ready"), idx - 1)
                    if what in ("qn0", "qn1", "u", "us"):
                        pe.wait_ge(sem("cq_lo"), 3)
                        t0 = {"qn0": 0, "qn1": 3, "u": 6, "us": 9}[what]
                        for k in range(3):
                            mm = triple(ps[:, :], wh[:, t0 + k, :], wl[:, t0 + k, :], cq_hi[:, k, :], cq_lo[:, k, :], k == 0, k == 2)
                    else:
                        pe.wait_ge(*at("ckv_lo"))
                        t0 = 12 + 2 * int(what[-1]) + int(what[0] == "v")
                        if what[0] == "k":
                            mm = triple(ps[:, :], wh[:, t0, :], wl[:, t0, :], ckv_hi[:, :], ckv_lo[:, :], True, True)
                        else:
                            for j in range(NB):
                                tok = slice(j * P, (j + 1) * P)
                                mm = triple(ps[:, tok], ckv_hi[:, tok], ckv_lo[:, tok], wh[:, t0, :], wl[:, t0, :], True, True)
                    mm.then_inc(sem("proj_done"), 1)

                for what in PROJ[:5]:
                    proj(0, what)

                def scores(s):
                    h, ii = divmod(s, NB)
                    i = NB - 1 - ii
                    o = bank[2 + s % 3][:, 0:(i + 1) * P]
                    q, k = slice(i * P, (i + 1) * P), slice(0, (i + 1) * P)
                    if s == 0:
                        pe.wait_ge(*at("kr_lo"))
                        pe.wait_ge(sem("masks_ready"), 2)
                    pe.wait_ge(sem("proj_ready"), 8 * (h // 2) + (8 if h % 2 else 5))
                    if s >= 3:
                        pe.wait_ge(sem("att_exp"), s - 2)
                    hs = h % 2
                    triple(o, xg_hi[:, QN + hs, q], xg_lo[:, QN + hs, q], xg_hi[:, KN + hs, k], xg_lo[:, KN + hs, k], True, False)
                    r = slice(64 * hs, 64 * hs + 64)
                    triple(o, xg_hi[r, QR, q], xg_lo[r, QR, q], xg_hi[r, KR, k], xg_lo[r, KR, k], False, False)
                    pe.matmul(o[:, i * P:(i + 1) * P], ident_r[:, :], causal[:, :], start=False, stop=True, skip_group_check=True)\
                      .then_inc(sem("att_scored"), 1)

                def turn(s):
                    i = NB - 1 - s % NB
                    pe.wait_ge(sem("att_probs"), s + 1)
                    if s >= 2:
                        pe.wait_ge(sem("att_lo"), s - 1)
                    for j in range(i + 1):
                        mm = pe.transpose(bank[5 + s % 2][:, j * P:(j + 1) * P], probs[:, s % 4, j * P:(j + 1) * P], ident[:, :])
                    mm.then_inc(sem("att_turned"), 1)

                def values(h):
                    pe.wait_ge(sem("att_lo"), NB * (h + 1))
                    if h:
                        pe.wait_ge(sem("att_out"), h)
                    vh, vl = (x[:, VV + h % 2, :].rearrange("p (j d) -> p j d", d=P) for x in (xg_hi, xg_lo))
                    for j in range(NB):
                        q = slice(j * P, T)
                        mm = triple(bank[7][:, q], vh[:, j, :], vl[:, j, :], pt_hi[:, h % 2, j, q], pt_lo[:, h % 2, j, q], j == 0, j == NB - 1)
                    mm.then_inc(sem("att_out_done"), 1)

                for s in range(NB * HEADS + 4):
                    h, ii = divmod(s, NB)
                    if s < NB * HEADS:
                        scores(s)
                        for t in after_step(h, ii):
                            proj(*t)
                    if 0 <= s - 2 < NB * HEADS:
                        turn(s - 2)
                    if s >= 6 and (s - 3) % NB == NB - 1:
                        values((s - 3) // NB)
                pe.wait_ge(sem("proj_ready"), 32)
                pe.wait_ge(sem("att_exp"), NB * HEADS)
                pe.wait_ge(sem("att_out"), HEADS)
                for m in range(KD):
                    n = FIRST["mla_o"] + m // 2
                    pe.wait_ge(lo_sem, n + 1)
                    if m >= 4:
                        pe.wait_ge(sem("attn_dve"), 3 * (m - 4) + 1)
                    chunk(bank[m % 4][:, :], n, 8, m % 2, o_hi, o_lo).then_inc(sem("mla_o_done"), 1)

            def w_in():
                n0 = FIRST["w_in"]
                for t in range(NT):
                    n = n0 + t // 2
                    pe.wait_ge(lo_sem, n + 1)
                    if t == 0:
                        pe.wait_ge(sem("ffn1_dve"), 4 * 7 + 1)
                    if t >= 4:
                        pe.wait_ge(sem("u_free"), t - 3)
                    before = (lambda k: pe.wait_ge(sem("ffn1_dve"), 4 * k + 2)) if t == 0 else None
                    chunk(bank[t % 4][:, :], n, 8, t % 2, xg_hi, xg_lo, before=before).then_inc(sem("u_done"), 1)
                    if t == 0:
                        pe.wait_ge(sem("ffn1_dve"), 4 * KD)
                        pe.matmul(bank[7][:, :], ones[:, :], sq_sum[:, :], start=True, stop=True).then_inc(*mark("ffn1_stat"))
                        pe.matmul(bank[6][:, :], ones[:, :], sq_sum2[:, :], start=True, stop=True).then_inc(*mark("inner_stat"))
                    if t - 1 in VTILES:
                        v = VTILES.index(t - 1)
                        pe.wait_ge(sem("u_free"), t)
                        if v == 1:
                            pe.wait_ge(*at("inner_ready"))
                        for j in range(NB):
                            mm = pe.transpose(bank[5 + v][:, j * P:(j + 1) * P], u_dst(t - 1)[:, j * P:(j + 1) * P], ident[:, :])
                        mm.then_inc(sem("nv_turned"), 1)
                    if t == 18:
                        pe.wait_ge(*at("gates_ready"))
                        pe.wait_ge(sem("nv_lo"), 1)
                        for j in range(NB):
                            mm = pe.transpose(bank[5][:, j * 32:(j + 1) * 32], u_dst(17)[0:32, j * P:(j + 1) * P], ident[0:32, 0:32])
                        mm.then_inc(*mark("g_turned"))
                    if t == 19:
                        pe.wait_ge(sem("mix_loaded"), 7 * 16)
                        pe.wait_ge(sem("nv_lo"), 2)
                        for j in range(2):
                            mm = pe.transpose(bank[6][:, j * 32:(j + 1) * 32], pe_rows[:, j, :], ident[0:32, 0:32])
                        mm.then_inc(*mark("pe_turned"))

            def compress():
                n = FIRST["compress"]
                pe.wait_ge(raw_sem[n % 2], loaded(n))
                pe.wait_ge(sem("u_free"), NT)
                w1 = raw(n).rearrange("p (j l c) -> p j l c", j=2, c=64)
                for kv in range(2):
                    pe.wait_ge(sem("cmp_windows"), 4 * kv + 4)
                    for l in range(16):
                        mm = pe.matmul(bank[kv][0:64, 0:64], w1[:, kv, l, :], cpe[:, l, :, :].rearrange("p g n -> p (g n)"), start=l == 0, stop=l == 15)
                    mm.then_inc(sem("cmp_hidden"), 1)
                pe.wait_ge(sem("cmp_act"), 1)
                pe.matmul(bank[2][:, 0:64], w2_t[:, 0, :, :].rearrange("p d e -> p (d e)"), h1[:, 0, :], start=True, stop=True).then_inc(sem("cmp_done"), 1)
                pe.wait_ge(sem("cmp_act"), 2)
                for g in range(2):
                    mm = pe.matmul(bank[3][0:32, g * 64:(g + 1) * 64], h1[:, 1, g * 32:(g + 1) * 32], w2_t[:, 1, 0, :], start=True, stop=True)
                mm.then_inc(sem("cmp_done"), 1)
                pe.wait_ge(sem("cmp_kv_lo"), 2)
                pe.wait_ge(sem("nq_lo"), 6)
                for h in range(6):
                    for i in range(NB):
                        c = ((h % 4) * NB + i) * 32
                        for part in range(2):
                            mm = pe.matmul(bank[h // 4][:, c:c + 32], q_st[:, h, i * P:(i + 1) * P], kc_st[:, part, h // 3, :],
                                           start=part == 0, stop=part == 1, skip_group_check=True)
                mm.then_inc(*mark("c_scored"))

            def nsa():
                def scores(s):
                    h, b, i = NSTEP[s]
                    o = bank[s % 4][:, 0:(i + 1) * P]
                    if s == 0:
                        pe.wait_ge(sem("nk_lo"), 8)
                        pe.wait_ge(*at("cmp_shifted"))
                    if s >= 4:
                        pe.wait_ge(sem("n_exp"), s - 3)
                    for part in range(2):
                        pe.matmul(o, q_st[:, h, i * P:(i + 1) * P], k_st[:, 2 * b + h // 3, part, 0:(i + 1) * P], start=part == 0, stop=False,
                                  skip_group_check=True)
                    pe.matmul(o[:, i * P:(i + 1) * P], ident_r[:, :], causal[:, :], start=False, stop=True, skip_group_check=True)\
                      .then_inc(sem("n_scored"), 1)

                def turn(s):
                    i = NSTEP[s][2]
                    pe.wait_ge(sem("n_probs"), s + 1)
                    if s >= 2:
                        pe.wait_ge(sem("n_lo"), s - 1)
                    for j in range(i + 1):
                        mm = pe.transpose(bank[5 + s % 2][:, j * P:(j + 1) * P], pm[:, s % 4, j * P:(j + 1) * P], ident[:, :])
                    mm.then_inc(sem("n_turned"), 1)

                def values(u):
                    h, b = divmod(u, 2)
                    pe.wait_ge(sem("n_lo"), NB * (u + 1))
                    if b == 0:
                        if h:
                            pe.wait_ge(sem("n_sum"), h)
                        pe.wait_ge(sem("c_lo"), h + 1)
                        for part, pt in enumerate((ptc_hi, ptc_lo)):
                            pe.matmul(bank[7][:, :], vc_st[:, h // 3, :], pt[:, :], start=part == 0, stop=False, skip_group_check=True)
                    for j in range(NB):
                        q = slice(j * P, T)
                        for part, pt in enumerate((pt2_hi, pt2_lo)):
                            mm = pe.matmul(bank[7][:, q], v_st[:, b, h // 3, j, :], pt[:, u % 2, j, q], start=False,
                                           stop=b == 1 and j == NB - 1 and part == 1, skip_group_check=True)
                    mm.then_inc(sem("n_pv"), 1)

                pe.wait_ge(sem("nv_lo"), 2)
                for s in range(len(NSTEP) + 4):
                    if s < len(NSTEP):
                        if s % 8 == 0:
                            h = s // 8
                            pe.wait_ge(*at("cmp_probs"))
                            if h:
                                pe.wait_ge(sem("c_lo"), h)
                            for i in range(NB):
                                c = (h * NB + i) * 32
                                mm = pe.transpose(bank[4][0:32, i * P:(i + 1) * P], p_cmp[:, c:c + 32], ident[:, :])
                            mm.then_inc(sem("c_turned"), 1)
                        scores(s)
                    if 0 <= s - 2 < len(NSTEP):
                        turn(s - 2)
                    if s >= 6 and (s - 3) % NB == NB - 1:
                        values((s - 3) // NB)

            def dilated():
                kd = k_st[:, :, :, :].rearrange("p a b t -> p (a b) t")
                pe.wait_ge(sem("n_lo"), len(NSTEP))
                for g in range(3):
                    if g == 2:
                        pe.wait_ge(sem("dv_lo"), 1)
                    for j in range(NB):
                        mm = pe.transpose(bank[5 + g % 2][:, j * P:(j + 1) * P], du[:, 6 + g, j * P:(j + 1) * P], ident[:, :])
                    mm.then_inc(sem("dv_turned"), 1)
                pe.wait_ge(sem("n_exp"), len(NSTEP))
                pe.wait_ge(sem("c_lo"), 6)
                pe.wait_ge(*at("dmask_ready"))
                pe.wait_ge(sem("dq_lo"), 6)

                def scores(s):
                    j, i = DSTEP[s]
                    pe.wait_ge(sem("dk_lo"), 6 * j + 6)
                    for g in range(3):
                        x = 3 * s + g
                        kbs = d_keys(g, i)
                        o = bank[x % 5][:, 0:len(kbs) * P]
                        if x >= 5:
                            pe.wait_ge(sem("d_exp"), x - 4)
                        k = slice(kbs[0] * P, (i + 1) * P)
                        for part in range(2):
                            pe.matmul(o, q_st[:, 2 * g + j, i * P:(i + 1) * P], kd[:, 2 * g + part, k], start=part == 0, stop=False, skip_group_check=True)
                        n = len(kbs) - 1
                        for b in range(n):
                            pe.matmul(o[:, b * P:(b + 1) * P], ident_r[:, :], dmask[:, (0, 1, 3)[g], :], start=False, stop=False, skip_group_check=True)
                        diag = causal[:, :] if g == 0 else dmask[:, 2 * g, :]
                        pe.matmul(o[:, n * P:(n + 1) * P], ident_r[:, :], diag, start=False, stop=True, skip_group_check=True).then_inc(sem("d_scored"), 1)

                def turn(s):
                    j, i = DSTEP[s]
                    for g in range(3):
                        x = 3 * s + g
                        pe.wait_ge(sem("d_probs"), x + 1)
                        if x >= 2:
                            pe.wait_ge(sem("d_lo"), x - 1)
                        for n in range(len(d_keys(g, i))):
                            mm = pe.transpose(bank[5 + x % 2][:, n * P:(n + 1) * P], pm[:, x % 4, n * P:(n + 1) * P], ident[:, :])
                        mm.then_inc(sem("d_turned"), 1)

                def values(j):
                    pe.wait_ge(sem("d_lo"), 12 * (j + 1))
                    pe.wait_ge(sem("n_sum"), 6)
                    for g in range(3):
                        if 3 * j + g:
                            pe.wait_ge(sem("d_out"), 3 * j + g)
                        for kb in range(NB):
                            last = min(kb + 1, NB - 1) if g == 0 else NB - 1
                            a0, a1 = d_turned(g, kb, kb), d_turned(g, kb, last)
                            at = (a0[0], a0[1], a0[2], slice(a0[3].start, a1[3].stop))
                            for part, pt in enumerate((pt2_hi, pt2_lo)):
                                mm = pe.matmul(bank[7][:, kb * P:(last + 1) * P], v_st[:, g, j, kb, :], pt[at], start=kb == 0 and part == 0,
                                               stop=kb == NB - 1 and part == 1, skip_group_check=True)
                        mm.then_inc(sem("d_pv"), 1)

                pe.wait_ge(sem("dv_lo"), 3)
                for s in range(len(DSTEP) + 1):
                    if s < len(DSTEP):
                        scores(s)
                    if s:
                        turn(s - 1)
                    if s == 4:
                        values(0)
                values(1)

            def tail():
                n_out, n_pp, n_pg = FIRST["w_out"], FIRST["ple_proj"], FIRST["ple_gate"]
                pe.wait_ge(sem("p_loaded"), 16)
                for j in range(2):
                    for i in range(NB):
                        mm = pe.transpose(bank[5 + j][:, i * P:(i + 1) * P], p_tok[:, i, j * P:(j + 1) * P], ident[:, :])
                    mm.then_inc(sem("p_turned"), 1)
                pe.wait_ge(sem("d_exp"), 24)
                for m in range(KD):
                    n = n_out + m // 2
                    pe.wait_ge(lo_sem, n + 1)
                    if m >= 4:
                        pe.wait_ge(sem("w_out_added"), m - 3)
                    before = (lambda k: pe.wait_ge(sem("y_lo"), k + 1)) if m == 0 else None
                    chunk(bank[m % 4][:, :], n, 8, m % 2, xg_hi, xg_lo, before=before).then_inc(sem("w_out_done"), 1)
                pe.wait_ge(lo_sem, n_pp + 1)
                pe.wait_ge(sem("p_lo_ready"), 2)
                wh, wl = (w[:, n_pp % 2, :].rearrange("p (k c) -> p k c", k=2) for w in (w_hi, w_lo))
                for m in range(KD):
                    if m >= 2:
                        pe.wait_ge(sem("emb_ready"), m - 1)
                    for k in range(2):
                        mm = triple(bank[4 + m % 2][:, :], wh[:, k, m * P:(m + 1) * P], wl[:, k, m * P:(m + 1) * P], p_hi[:, k, :], p_lo[:, k, :], k == 0, k == 1)
                    mm.then_inc(sem("ple_proj_done"), 1)
                for m in range(KD):
                    n = n_pg + m // 2
                    pe.wait_ge(lo_sem, n + 1)
                    pe.wait_ge(sem("w_out_added"), KD) if m == 0 else None
                    if m >= 4:
                        pe.wait_ge(sem("ple_act"), 2 * (m - 4) + 1)
                    before = (lambda k: pe.wait_ge(sem("xs_lo_ready"), k + 1)) if m == 0 else None
                    chunk(bank[m % 4][:, :], n, 8, m % 2, xs_hi, xs_lo, before=before).then_inc(sem("ple_gate_done"), 1)
                pe.wait_ge(sem("ple_dve"), 24)
                pe.wait_ge(sem("emb_ready"), KD)
                for i in range(NB):
                    mm = pe.matmul(bank[4][:, 2 * i:2 * i + 2], sq_sum[:, i * P:(i + 1) * P], ones[:, 0:2], start=True, stop=True)
                mm.then_inc(*mark("fin_stat"))
                pe.wait_ge(sem("fin_gained"), KD)
                pe.wait_ge(sem("ple_act"), 16)
                for o in range(2 * NB):
                    i, half = divmod(o, 2)
                    if o >= 4:
                        pe.wait_ge(sem("out_ready"), o - 3)
                    for m in range(4):
                        mm = pe.transpose(bank[o % 4][:, m * P:(m + 1) * P], emb[:, 4 * half + m, i * P:(i + 1) * P], ident[:, :])
                    mm.then_inc(sem("fin_turned"), 1)

            ffn(0)
            mla()
            ffn(1)
            w_in()
            compress()
            nsa()
            dilated()
            tail()


def constants():
    import numpy as np
    c = {"c_ident": np.eye(P, dtype=np.float32)}
    s, t = np.arange(P)[:, None], np.arange(BAND)[None, :]
    band = np.zeros((P, len(WINDOWS), 2, BAND), np.float32)
    for g, w in enumerate(WINDOWS):
        inside = (t >= s) & (t - s < w)
        for first in range(2):
            n = np.minimum(t + 1, w) if first else np.full_like(t, w)
            band[:, g, first] = inside / n.astype(np.float32) - (t == s)
    c["c_band"] = band
    lane = np.arange(P)
    inv = 1.0 / (np.float32(10000.0) ** (np.arange(0, ROPE, 2, dtype=np.float32) / np.float32(ROPE)))
    c["c_rope"] = np.stack([inv[lane % 32], np.where(lane % 64 < 32, -1.0, 1.0)], 1).astype(np.float32)
    q, k = np.arange(P)[:, None], np.arange(P)[None, :]
    ok = [k <= q, k >= q]
    for dil in (4, 16):
        same = (q - k) % dil == 0
        ok += [same, same & (k <= q)]
    n = np.arange(32)[None, None, :]
    tok = P * np.arange(NB)[None, :, None] + np.arange(P)[:, None, None]
    c["c_cmask"] = np.where((16 * n + 31 <= tok) & (n < 31), 0.0, NEG).astype(np.float32)
    c["c_cvalid"] = np.ascontiguousarray((tok[:, :, 0] >= 31).astype(np.float32))
    c["c_masks"] = np.ascontiguousarray(np.stack([np.where(m, 0.0, NEG) for m in ok], 1).astype(np.float32))
    return c


def kernel(**inputs):
    import numpy as np
    import concourse.bacc as bacc
    from concourse.bass_utils import run_bass_kernel_spmd

    nc = bacc.Bacc("TRN2", target_bir_lowering=False, num_devices=1)
    arrays, aps = {}, {}
    for name, v in list(inputs.items()) + list(constants().items()):
        v = np.ascontiguousarray(v)
        arrays[f"in_{name}"] = v
        key = name
        aps[key] = nc.dram_tensor(f"in_{name}", v.shape, mybir.dt.from_np(v.dtype), kind="ExternalInput").ap()
    out = nc.dram_tensor("out_0", (1, T, D), F32, kind="ExternalOutput").ap()
    program(nc, aps, out)
    r = run_bass_kernel_spmd(nc, [arrays], core_ids=[0])
    return r.results[0]["out_0"]
```

```python
from contextlib import ExitStack

import concourse.bass as bass
from concourse import mybir

F32 = mybir.dt.float32
F32R = mybir.dt.float32r
I32 = mybir.dt.int32
ALU = mybir.AluOpType
ACT = mybir.ActivationFunctionType
AX = mybir.AxisListType

P = 128
T = 512
NB = T // P
D = 1024
KD = D // P
FF = 2816
KF = FF // P
EPS = 1e-6
WINDOWS = (2, 4, 8, 16)
BAND = P + 16
QL, KVL, ROPE = 384, 128, 64
HEADS = 8
NEG = -1e30
U_COLS = 2048
DOWN_SPLIT = ((0, 6), (6, 6), (12, 5), (17, 5))

ROWS = {}
for _name, _n in (("norm_mix", 16), ("norm_ffn", 16), ("norm_final", 8), ("pool_scale", 8), ("norm_mix_2", 8),
                  ("norm_final_2", 8), ("mla_q_norm", 3), ("mla_kv_norm", 1), ("conv_w_2", 6), ("conv_b_2", 2)):
    ROWS[_name] = (sum(n for _, n in ROWS.values()), _n)
NROWS = sum(n for _, n in ROWS.values())


def weight_units():
    first, n = {}, 0
    for name, count in (("pool", 1), ("gateup0", 22), ("down0", 16), ("mla_down", 3), ("heads", 4), ("mla_o", 4),
                        ("gateup1", 22), ("down1", 16), ("w_in", 17), ("w_out", 4), ("ple_proj", 1), ("ple_gate", 4)):
        first[name] = n
        n += count
    return first, n


FIRST, UNITS = weight_units()


MARKS = {
    "scalar_mark": ("tok_root", "mix_root", "ffn0_root", "kv_root", "kr_hi", "ckv_hi", "rq_root", "attn_root", "ffn1_root", "inner_root",
                    "gates_ready", "cmp_exp", "fin_root"),
    "tensor_mark": ("vec_turned", "mix_stat", "ffn0_stat", "kv_stat", "rq_stat", "attn_stat", "ffn1_stat", "inner_stat", "g_turned", "pe_turned",
                    "c_scored", "fin_stat"),
    "vector_mark": ("angle_ready", "cols_ready", "gain2_ready", "tok_rstd", "rope_ready", "sum_clear", "mix_rstd",
                    "ffn0_rstd", "kr_ready", "rkv_ready", "ckv_ready", "kr_lo", "ckv_lo", "rq_ready",
                    "attn_clear", "attn_rstd", "ffn1_rstd", "inner_ready", "dmask_ready", "kcv_padded", "gates_kept",
                    "pe_kept", "cmp_shifted", "cmp_probs", "fin_clear", "fin_rstd"),
}


def program(nc, a, out):
    ctx = ExitStack()
    with ctx:
        def sb(name, shape, dt=F32, stack=ctx):
            return stack.enter_context(nc.sbuf_tensor(name, shape, dt))

        sems = {}

        def sem(name):
            if name not in sems:
                sems[name] = ctx.enter_context(nc.semaphore(name))
            return sems[name]

        given = {engine: 0 for engine in MARKS}

        def at(name):
            engine = next(e for e, names in MARKS.items() if name in names)
            return sem(engine), MARKS[engine].index(name) + 1

        def mark(name):
            engine = next(e for e, names in MARKS.items() if name in names)
            assert MARKS[engine][given[engine]] == name
            given[engine] += 1
            return sem(engine), 1

        xT = sb("xT", [P, KD, T])
        xg_hi = sb("xg_hi", [P, KD, T], F32R)
        xg_lo = sb("xg_lo", [P, KD, T], F32R)
        w_raw = sb("w_raw", [P, 2, U_COLS])
        w_hi = sb("w_hi", [P, 2, U_COLS], F32R)
        w_lo = sb("w_lo", [P, 2, U_COLS], F32R)
        ident = sb("ident", [P, P])
        ones = sb("ones", [P, P])
        cols = sb("cols", [P, NROWS])
        eps_col = sb("eps_col", [P, 4])
        rstd = sb("rstd", [P, T])
        root = sb("root", [P, T])
        squares = sb("squares", [P, 2, T])
        sq_sum = sb("sq_sum", [P, T])
        sq_sum2 = sb("sq_sum2", [P, T])
        ident_r = sb("ident_r", [P, P], F32R)
        causal = sb("causal", [P, P], F32R)
        neg_max = sb("neg_max", [P, 8])
        row_top = sb("row_top", [P, 8])
        row_sum = sb("row_sum", [P, 8])
        row_inv = sb("row_inv", [P, 8])
        rope_col = sb("rope_col", [P, 2])
        gain2 = sb("gain2", [P, KD])
        bank = [ctx.enter_context(nc.psum_tensor(f"bank{i}", [P, T], F32)) for i in range(8)]

        def gain(name, m):
            c = ROWS[name][0] + m
            return cols[:, c:c + 1] if isinstance(c, int) else cols[:, bass.ds(c, 1)]

        rope_mem = ExitStack()
        cos_t = sb("cos_t", [P, T], stack=rope_mem)
        sin_t = sb("sin_t", [P, T], stack=rope_mem)
        pool_mem = ExitStack()
        x_tok = sb("x_tok", [P, NB, D], stack=pool_mem)
        h_tok = sb("h_tok", [P, NB, D], stack=pool_mem)
        pooled_hi = sb("pooled_hi", [P, KD, T], F32R, pool_mem)
        pooled_lo = sb("pooled_lo", [P, KD, T], F32R, pool_mem)
        band = sb("band", [P, len(WINDOWS), 2, BAND], stack=pool_mem)
        tok_stat = sb("tok_stat", [P, 3, NB], stack=pool_mem)
        vec_rows = sb("vec_rows", [P, P], stack=pool_mem)
        pos_i = sb("pos_i", [P, T], I32, pool_mem)
        angle = sb("angle", [P, 3, T], stack=pool_mem)
        masks0 = sb("masks0", [P, P], stack=pool_mem)
        pool_mem.close()

        ffn_mem = ExitStack()
        act_hi = sb("act_hi", [P, KF, T], F32R, ffn_mem)
        act_lo = sb("act_lo", [P, KF, T], F32R, ffn_mem)
        ffn_mem.close()
        gate_z, up_z, gate_s = squares[:, 1, :], squares[:, 0, :], root[:, :]

        mla_mem = ExitStack()
        o_hi = sb("o_hi", [P, HEADS, T], F32R, mla_mem)
        o_lo = sb("o_lo", [P, HEADS, T], F32R, mla_mem)
        pt_hi = sb("pt_hi", [P, 2, NB, T], F32R, mla_mem)
        pt_lo = sb("pt_lo", [P, 2, NB, T], F32R, mla_mem)
        probs = sb("probs", [P, 4, T], stack=mla_mem)
        cq_hi = sb("cq_hi", [P, 3, T], F32R, mla_mem)
        kr_hi = sb("kr_hi", [P, T], F32R, mla_mem)
        kr_lo = sb("kr_lo", [P, T], F32R, mla_mem)
        cq_lo = sb("cq_lo", [P, 3, T], F32R, mla_mem)
        ckv_hi = sb("ckv_hi", [P, T], F32R, mla_mem)
        ckv_lo = sb("ckv_lo", [P, T], F32R, mla_mem)
        rq = sb("rq", [P, 2, 2 * NB], stack=mla_mem)
        mla_mem.close()
        rope_mem.close()

        mix_mem = ExitStack()
        ptc_hi = sb("ptc_hi", [32, T], F32R, mix_mem)
        ptc_lo = sb("ptc_lo", [32, T], F32R, mix_mem)
        q_st = sb("q_st", [P, 6, T], F32R, mix_mem)
        k_st = sb("k_st", [P, 4, 2, T], F32R, mix_mem)
        v_st = sb("v_st", [P, 3, 2, NB, P], F32R, mix_mem)
        br = sb("br", [P, 8, T], stack=mix_mem)
        du = sb("du", [P, 9, T], stack=mix_mem)
        pm = sb("pm", [P, 4, T], stack=mix_mem)
        dmask = sb("dmask", [P, 5, P], F32R, mix_mem)
        cmask = sb("cmask", [P, NB, 32], stack=mix_mem)
        cvalid = sb("cvalid", [P, NB], stack=mix_mem)
        gates = sb("gates", [P, NB, 32], stack=mix_mem)
        kc_st = sb("kc_st", [P, 2, 2, 32], F32R, mix_mem)
        vc_st = sb("vc_st", [32, 2, P], F32R, mix_mem)
        cst = sb("cst", [P, 4, 24], stack=mix_mem)
        pe_rows = sb("pe_rows", [32, 2, P], stack=mix_mem)
        pe_cols = sb("pe_cols", [P, 2, 32], stack=mix_mem)
        w2_t = sb("w2_t", [64, 2, 2, 64], stack=mix_mem)
        h1 = sb("h1", [64, 2, 64], stack=mix_mem)
        mix_mem.close()
        kcv = pm[:, 0:3, :].rearrange("p a t -> p (a t)")[:, 0:2 * 528].rearrange("p (a t) -> p a t", a=2)
        w1_t = du[:, 2:6, :].rearrange("p a t -> p (a t)").rearrange("p (j l c) -> p j l c", j=2, c=64)
        cpe = [x.rearrange("p a t -> p (a t)").rearrange("p (l g n) -> p l g n", l=16, g=2) for x in (squares[:, :, :], du[:, 6:8, :])]
        p_cmp = squares[:, :, :].rearrange("p a t -> p (a t)")[:, 0:768]
        pt2_hi, pt2_lo = (x[:, :, :].rearrange("p (b j) t -> p b j t", b=2) for x in (xg_hi, xg_lo))

        tail_mem = ExitStack()
        xs_hi = sb("xs_hi", [P, KD, T], F32R, tail_mem)
        xs_lo = sb("xs_lo", [P, KD, T], F32R, tail_mem)
        p_tok = sb("p_tok", [P, NB, 256], stack=tail_mem)
        p_hi = sb("p_hi", [P, 2, T], F32R, tail_mem)
        p_lo = sb("p_lo", [P, 2, T], F32R, tail_mem)
        emb = sb("emb", [P, KD, T], stack=tail_mem)
        out_tok = sb("out_tok", [P, 4, T], stack=tail_mem)
        fin = sb("fin", [P, 3, 2 * NB], stack=tail_mem)
        tail_mem.close()
        down_q = probs
        cos_s, sin_s = probs[:, 0, :], probs[:, 1, :]
        QN, KN, VV, QR = 0, 2, 4, 6

        raw_sem = [sem("weights_loaded0"), sem("weights_loaded1")]
        hi_sem, lo_sem = sem("weights_hi"), sem("weights_lo")
        unit_src = {}

        def raw(n):
            return w_raw[:, n % 2, :]

        def tiles256(ap, k):
            return ap[:, 0:k * 256].rearrange("p (k c) -> p k c", k=k)

        unit_src[0] = [(tiles256(raw(0), 8), a["pool_w"].rearrange("l g (k p) d -> p (l g k) d", p=P))]
        wd = a["mla_w_down"][0].rearrange("(k p) n -> p k n", p=P)
        n = FIRST["mla_down"]
        r0 = QL + KVL
        pieces = ((0, 2 * P, 2 * P), (256, 64, r0), (320, 64, r0), (384, 32, r0 + 32), (416, 32, r0), (448, 32, r0 + 32), (480, 32, r0),
                  (512, 2 * P, 0))
        for j in range(3):
            unit_src[n + j] = [(tiles256(raw(n + j), 8)[:, :, c % 256:c % 256 + w], wd[:, :, s0:s0 + w]) for c, w, s0 in pieces if c // 256 == j]
        wq = a["mla_w_uq"][0].rearrange("(k p) n -> p k n", p=P)
        for pr in range(HEADS // 2):
            n = FIRST["heads"] + pr
            t16 = raw(n).rearrange("p (t c) -> p t c", c=P)
            q0, q1 = 2 * pr * 192, (2 * pr + 1) * 192
            unit_src[n] = [(t16[:, 0:3, :], wq[:, :, q0:q0 + P]), (t16[:, 3:6, :], wq[:, :, q1:q1 + P])]
            for e, q in ((0, q0 + P), (64, q1 + P)):
                unit_src[n] += [(t16[:, 6:9, e:e + 64], wq[:, :, q:q + 64]),
                                (t16[:, 9:12, e:e + 32], wq[:, :, q + 32:q + 64]), (t16[:, 9:12, e + 32:e + 64], wq[:, :, q:q + 32])]
            unit_src[n] += [(raw(n)[:, 12 * P:16 * P], a["mla_w_ukv"][0][:, pr * 512:(pr + 1) * 512])]

        def square_units(stage, w):
            wv = w.rearrange("(k p) n -> p k n", p=P)
            for j in range(4):
                n = FIRST[stage] + j
                unit_src[n] = [(tiles256(raw(n), 8), wv[:, :, j * 256:(j + 1) * 256])]

        square_units("mla_o", a["mla_w_o"][0])
        wi = a["w_in_2"][0].rearrange("(k p) n -> p k n", p=P)
        for j in range(17):
            n = FIRST["w_in"] + j
            c0, w = (256 * j, 256) if j < 9 else (2194 + 256 * (j - 9), 256 if j < 16 else 128)
            unit_src[n] = [(tiles256(raw(n), 8)[:, :, 0:w], wi[:, :, c0:c0 + w])]
        square_units("w_out", a["w_out_2"][0])
        square_units("ple_gate", a["w_ple_gate_2"][0])
        n = FIRST["ple_proj"]
        unit_src[n] = [(raw(n).rearrange("p (k c) -> p k c", k=2), a["w_ple_proj_2"][0].rearrange("(k p) n -> p k n", p=P))]
        loads = [len(unit_src.get(n, [0])) for n in range(UNITS)]

        def loaded(n):
            return 16 * sum(loads[m] for m in range(n % 2, n + 1, 2))

        used = {}

        def hi_tiles(n, k, c=None):
            return tiles256(w_hi[:, n % 2, :], k), tiles256(w_lo[:, n % 2, :], k)

        block = ctx.enter_context(nc.Block())
        used[0] = (sem("mixed_done"), 8)
        for l in range(2):
            for i in range(11):
                used[FIRST[f"gateup{l}"] + 2 * i] = (sem(f"gateup{l}_done"), 4 * i + 2)
                used[FIRST[f"gateup{l}"] + 2 * i + 1] = (sem(f"gateup{l}_done"), 4 * i + 4)
            for d in range(16):
                used[FIRST[f"down{l}"] + d] = (sem(f"down{l}_done"), 2 * d + 2)
        for j in range(3):
            used[FIRST["mla_down"] + j] = (sem("mla_down_done"), 2 * j + 2)
        for pr in range(4):
            used[FIRST["heads"] + pr] = (sem("proj_done"), 8 * pr + 8)
            used[FIRST["mla_o"] + pr] = (sem("mla_o_done"), 2 * pr + 2)
            used[FIRST["w_out"] + pr] = (sem("w_out_done"), 2 * pr + 2)
            used[FIRST["ple_gate"] + pr] = (sem("ple_gate_done"), 2 * pr + 2)
        used[FIRST["ple_proj"]] = (sem("ple_proj_done"), KD)
        for j in range(17):
            used[FIRST["w_in"] + j] = (sem("u_done"), min(2 * j + 2, 33))

        QUERY_TILES = (2, 0, 1)

        PROJ = ("kn0", "qn0", "u", "us", "v0", "kn1", "qn1", "v1")

        def after_step(h, ii):
            this = (("v0", "v1")[h % 2],) if ii == 0 else ()
            if h % 2 == 0:
                return tuple((h // 2, what) for what in this + ((), ("kn1",), ("qn1",), ())[ii])
            later = (("kn0",), ("qn0",), ("u", "us"), ())[ii] if h + 1 < HEADS else ()
            return tuple((h // 2, what) for what in this) + tuple((h // 2 + 1, what) for what in later)

        def rotary_q(pr):
            return xg_hi[:, QR + pr % 2, :], xg_lo[:, QR + pr % 2, :]

        ffn_from = ("mix", "attn")
        ffn_to = ("ffn0", "ffn1")
        
        def ffn_gain(l, k):
            if l == 1:
                return gain2[:, bass.ds(k, 1)]
            return cols[:, bass.ds(k + (ROWS["norm_mix"][0] + KD), 1)]

        def inner_gain(k):
            return cols[:, bass.ds(k + ROWS["norm_final"][0], 1)]


        KINDS = (["ab"] * 2 + ["ac"] * 2 + ["ah"] * 2 + ["az"] * 2 + ["nq"] * 3 + ["kc", "vc", "ks", "vs", "kw", "vw", "gate"]
                 + ["z"] * 3 + ["dq"] * 3 + ["dk"] * 3 + ["dv"] * 3 + ["z"] * 3)
        NT = len(KINDS)
        SCRATCHED = [t for t in range(NT) if KINDS[t] in ("nq", "ks", "vs", "kw", "vw", "gate")]
        VTILES = [t for t in range(NT) if KINDS[t] in ("vs", "vw")]

        def u_dst(t):
            kind = KINDS[t]
            if t < 8:
                return br[:, t, :]
            if kind in ("kc", "vc"):
                return kcv[:, int(kind == "vc"), 0:T]
            if kind == "z":
                return br[:, t - 18 if t < 21 else 3 + t - 30, :]
            if kind[0] == "d":
                return du[:, t - 21, :]
            return squares[:, SCRATCHED.index(t) % 2, :]

        CMP_BANKS = (bank[7], bank[4], bank[5], bank[6])

        def n_out(h):
            return bank[(3, 7)[h % 2]]

        NSTEP = [(h, b, i) for h in range(6) for b in range(2) for i in (3, 2, 1, 0)]
        DSTEP = [(j, i) for j in range(2) for i in (3, 2, 1, 0)]

        def d_keys(g, i):
            return list(range(max(i - 1, 0), i + 1)) if g == 0 else list(range(i + 1))

        def d_turned(g, kb, i):
            if g:
                return (slice(None), g - 1, kb, slice(i * P, (i + 1) * P))
            return (slice(None), kb // 2, 2 + kb % 2, slice((i - kb) * P, (i - kb + 1) * P))

        @block.sync
        def _(sp):
            def load(n):
                if n >= 2:
                    sp.wait_ge(lo_sem, n - 1)
                for dst, src in unit_src[n]:
                    sp.dma_start(dst, src).then_inc(raw_sem[n % 2], 16)

            sp.dma_start(x_tok[:, 0:2, :], a["x"][0].rearrange("(i p) f -> p i f", p=P)[:, 0:2]).then_inc(sem("x_loaded0"), 16)
            sp.dma_start(x_tok[:, 2:4, :], a["x"][0].rearrange("(i p) f -> p i f", p=P)[:, 2:4]).then_inc(sem("x_loaded1"), 16)
            sp.dma_start(ident[:, :], a["c_ident"]).then_inc(sem("ident_loaded"), 16)
            for name, (r, n) in ROWS.items():
                v = a[name]
                flat = v if len(v.shape) == 1 else v.rearrange("a b -> (a b)") if len(v.shape) == 2 else v.rearrange("a b c -> (a b c)")
                sp.dma_start(vec_rows[r:r + n, :], flat.rearrange("(r p) -> r p", p=P)).then_inc(sem("vectors_loaded"), 16)
            sp.dma_start(band[:, :, :, :], a["c_band"]).then_inc(sem("band_loaded"), 16)
            sp.dma_start(pos_i[:, :], a["positions"][0:1, :].to_broadcast([P, T])).then_inc(sem("pos_loaded"), 16)
            sp.dma_start(rope_col[:, :], a["c_rope"]).then_inc(sem("pos_loaded"), 16)
            sp.dma_start(masks0[:, :], a["c_masks"][:, 0, :]).then_inc(sem("mask_loaded"), 16)
            load(0)
            for l in range(2):
                if l == 1:
                    for n in range(FIRST["mla_down"], FIRST["gateup1"]):
                        load(n)
                up, gate, down = (a[f"ffn_w_{x}"][l] for x in ("up", "gate", "down"))
                gv, uv = (w.rearrange("(k p) n -> p k n", p=P) for w in (gate, up))
                dv = down.rearrange("(k p) n -> p k n", p=P)
                n0 = FIRST[f"gateup{l}"]
                with sp.Fori(0, 11) as i:
                    for j, src in enumerate((gv, uv)):
                        n = n0 + j
                        sp.wait_ge(lo_sem, i * 2 + (n - 1))
                        sp.dma_start(tiles256(raw(n), 8), src[:, :, bass.ds(i * 256, 256)]).then_inc(raw_sem[n % 2], 16)
                n0 = FIRST[f"down{l}"]
                with sp.Fori(0, 4) as q:
                    for j, (k0, nk) in enumerate(DOWN_SPLIT):
                        n = n0 + j
                        sp.wait_ge(lo_sem, q * 4 + (n - 1))
                        sp.dma_start(tiles256(raw(n), nk), dv[:, k0:k0 + nk, bass.ds(q * 256, 256)]).then_inc(raw_sem[n % 2], 16)

            n_mix, n_out = FIRST["w_in"], FIRST["w_out"]
            for n in range(n_mix, n_mix + 2):
                load(n)
            sp.wait_ge(sem("down1_done"), 32)
            for src, dst in ((a["c_masks"][:, 1:6, :], du[:, 0:2, :].rearrange("p a t -> p (a t)")[:, 0:5 * P].rearrange("p (m c) -> p m c", c=P)),
                             (a["c_cmask"], cmask[:, :, :]), (a["c_cvalid"], cvalid[:, :]),
                             (a["cmp_pe_2"][0].rearrange("j l e -> l j e"), pe_rows[:, :, 0:64]),
                             (a["cmp_pe_2"][0].rearrange("j l e -> l j e"), pe_rows[:, :, 64:128]),
                             (a["cmp_w2_2"][0].rearrange("j a e -> a j e"), w2_t[:, :, 0, :]),
                             (a["cmp_w2_2"][0].rearrange("j a e -> a j e"), w2_t[:, :, 1, :]),
                             *((a["cmp_w1_2"][0, j].rearrange("(l p) c -> p l c", p=P), w1_t[:, j, :, :]) for j in range(2))):
                sp.dma_start(dst, src).then_inc(sem("mix_loaded"), 16)
            for n in range(n_mix + 2, n_out + 1):
                load(n)
            load(n_out + 1)
            sp.wait_ge(sem("d_out"), 6)
            sp.dma_start(p_tok[:, :, :], a["p_2"][0, 0].rearrange("(i p) f -> p i f", p=P)).then_inc(sem("p_loaded"), 16)
            for n in range(n_out + 2, UNITS):
                load(n)
            ov = out[0].rearrange("(i p) f -> p i f", p=P)
            for o in range(2 * NB):
                i, half = divmod(o, 2)
                sp.wait_ge(sem("out_ready"), o + 1)
                sp.dma_start(ov[:, i, half * T:(half + 1) * T], out_tok[:, o % 4, :]).then_inc(sem(f"out_stored{o % 4}"), 16)
            for o in range(4):
                sp.wait_ge(sem(f"out_stored{o}"), 32)

        @block.gpsimd
        def _(pool):
            pool.memset(ones[:, :], 1.0).then_inc(sem("ones_set"), 1)
            pool.memset(eps_col[:, 0:1], EPS).then_inc(sem("eps_set"), 1)
            pool.memset(eps_col[:, 1:2], EPS * (128 + ROPE)).then_inc(sem("eps_set"), 1)

        @block.scalar
        def _(act):
            def split_hi(n, waits=()):
                act.wait_ge(raw_sem[n % 2], loaded(n))
                if n >= 2:
                    act.wait_ge(*used[n - 2])
                act.activation(w_hi[:, n % 2, :], raw(n), ACT.Copy).then_inc(hi_sem, 1)

            def chain(tag, k, m, gcol, extra=None):
                act.wait_ge(sem(f"{tag}_dve"), k * 3 + 1)
                act.activation(xg_hi[:, m, :], xT[:, m, :], ACT.Copy, scale=gcol).then_inc(sem(f"{tag}_act"), 1)
                act.activation(squares[:, k % 2 if isinstance(k, int) else 0, :], xT[:, m, :], ACT.Square).then_inc(sem(f"{tag}_act"), 1)

            act.preload_act_table(ACT.Sqrt)
            for i in range(NB):
                act.wait_ge(sem(f"x_loaded{i // 2}"), 16)
                act.activation(h_tok[:, i, :], x_tok[:, i, :], ACT.Square, accum_out=tok_stat[:, 0, i:i + 1]).then_inc(sem("tok_squares"), 1)
            act.wait_ge(sem("eps_set"), 2)
            act.wait_ge(sem("tok_squares"), NB)
            act.activation(tok_stat[:, 1, :], tok_stat[:, 0, :], ACT.Sqrt, scale=1.0 / D, bias=eps_col[:, 0:1]).then_inc(*mark("tok_root"))
            act.preload_act_table(ACT.Sin)
            act.wait_ge(*at("angle_ready"))
            act.activation(sin_t[:, :], angle[:, 0, :], ACT.Sin).then_inc(sem("sin_done"), 1)
            act.activation(cos_t[:, :], angle[:, 1, :], ACT.Sin).then_inc(sem("sin_done"), 1)
            act.preload_act_table(ACT.Sqrt)
            split_hi(0)
            act.wait_ge(*at("cols_ready"))
            for c in range(KD):
                act.wait_ge(sem("pooled_done"), c + 1)
                act.activation(pooled_hi[:, c, :], bank[4 + c % 2][:, :], ACT.Copy, scale=gain("norm_mix", c)).then_inc(sem("pooled_hi"), 1)
            split_hi(1)
            for m in range(KD):
                chain("mix", m, m, gain("norm_ffn", m))

            def ffn(l):
                tag, to = ffn_from[l], ffn_to[l]
                n0, d0 = FIRST[f"gateup{l}"], FIRST[f"down{l}"]
                gu, gd, ga = sem(f"gateup{l}_done"), sem(f"gated{l}_dve"), sem(f"gated{l}_act")
                act.wait_ge(*at(f"{tag}_stat"))
                act.activation(root[:, :], bank[7][:, :], ACT.Sqrt, scale=1.0 / D, bias=eps_col[:, 0:1]).then_inc(*mark(f"{tag}_root"))
                act.preload_act_table(ACT.Silu)
                act.wait_ge(*used[n0 - 1])

                def gateup_turn(i, first):
                    for j in (1, 2):
                        n = n0 + j
                        act.wait_ge(raw_sem[n % 2], i * 16 + loaded(n))
                        if not (first and j == 1):
                            act.wait_ge(gu, i * 4 + 2 * (j - 1))
                        act.activation(w_hi[:, n % 2, :], raw(n), ACT.Copy).then_inc(hi_sem, 1)
                    for c in range(2):
                        act.wait_ge(gd, i * 8 + 4 * c + 1)
                        act.activation(gate_s, gate_z, ACT.Silu).then_inc(ga, 1)
                        act.wait_ge(gd, i * 8 + 4 * c + 3)
                        act.activation(act_hi[:, bass.ds(i * 2 + c, 1), :].rearrange("p a t -> p (a t)"), gate_z, ACT.Copy).then_inc(ga, 1)
                gateup_turn(0, True)
                with act.Fori(1, 11) as i:
                    gateup_turn(i, False)
                dn = sem(f"down{l}_done")

                def down_turn(q, first):
                    for j in range(4):
                        n = d0 + j + 1
                        act.wait_ge(raw_sem[n % 2], q * 32 + loaded(n))
                        if first and j == 0:
                            act.wait_ge(gu, 44)
                        else:
                            act.wait_ge(dn, q * 8 + 2 * j)
                        act.activation(w_hi[:, n % 2, :], raw(n), ACT.Copy).then_inc(hi_sem, 1)
                    for c in range(2):
                        k = q * 2 + c
                        act.wait_ge(sem(f"{to}_dve"), q * (6 + 2 * l) + (3 + l) * c + 1)
                        xt = xT[:, bass.ds(k, 1), :].rearrange("p a t -> p (a t)")
                        act.activation(xg_hi[:, bass.ds(k, 1), :].rearrange("p a t -> p (a t)"), xt, ACT.Copy,
                                       scale=ffn_gain(l, k)).then_inc(sem(f"{to}_act"), 1)
                        act.activation(squares[:, c, :], xt, ACT.Square).then_inc(sem(f"{to}_act"), 1)
                        if l == 1:
                            act.activation(root[:, :], xt, ACT.Square, scale=inner_gain(k)).then_inc(sem(f"{to}_act"), 1)

                down_turn(0, True)
                with act.Fori(1, 4) as q:
                    down_turn(q, False)

            def mla():
                n0 = FIRST["mla_down"]
                s2 = 1.0 / (128 + ROPE)
                split_hi(n0 + 1)
                act.wait_ge(*at("ffn0_stat"))
                act.activation(root[:, :], bank[7][:, :], ACT.Sqrt, scale=1.0 / D, bias=eps_col[:, 0:1]).then_inc(*mark("ffn0_root"))
                def proj(pr, what):
                    idx = 8 * pr + PROJ.index(what)
                    h = 2 * pr + int(what[-1] == "1")
                    if what == "u":
                        return
                    if what == "us":
                        act.wait_ge(sem("proj_tmp"), pr + 1)
                        src = squares[:, 0, :]
                    else:
                        act.wait_ge(sem("proj_done"), idx + 1)
                        src = bank[idx % 2][:, :]
                    dst = rotary_q(pr)[0] if what == "us" else xg_hi[:, {"q": QN, "k": KN, "v": VV}[what[0]] + h % 2, :]
                    if what == "us" and pr >= 2:
                        act.wait_ge(sem("att_scored"), 8 * (pr - 1))
                    elif what[0] in "qk" and h >= 2:
                        act.wait_ge(sem("att_scored"), 4 * (h - 1))
                    elif what[0] == "v" and h >= 2:
                        act.wait_ge(sem("att_out_done"), h - 1)
                    act.activation(dst, src, ACT.Copy).then_inc(sem("proj_hi"), 1)

                act.wait_ge(sem("down_q_ready"), 1)
                act.activation(squares[:, 0, :], down_q[:, 3, :], ACT.Square).then_inc(sem("cq_act"), 1)

                def queries(n):
                    t = QUERY_TILES[n]
                    act.wait_ge(sem("down_q_ready"), n + 2)
                    act.activation(cq_hi[:, t, :], down_q[:, t, :], ACT.Copy, scale=gain("mla_q_norm", t)).then_inc(sem("cq_act"), 1)
                    act.activation(squares[:, n - 1, :] if n else sq_sum[:, :], down_q[:, t, :], ACT.Square).then_inc(sem("cq_act"), 1)

                queries(0)
                split_hi(n0 + 2)
                act.wait_ge(*at("kv_stat"))
                act.activation(squares[:, 1, :], bank[7][:, :], ACT.Sqrt, scale=1.0 / KVL, bias=eps_col[:, 0:1]).then_inc(*mark("kv_root"))
                act.wait_ge(*at("kr_ready"))
                act.activation(kr_hi[:, :], root[:, :], ACT.Copy).then_inc(*mark("kr_hi"))
                act.wait_ge(*at("ckv_ready"))
                act.activation(ckv_hi[:, :], down_q[:, 3, :], ACT.Copy).then_inc(*mark("ckv_hi"))
                split_hi(n0 + 3)
                queries(1)
                queries(2)
                proj(0, "kn0")
                act.wait_ge(*at("rq_stat"))
                act.activation(rq[:, 0, :], bank[6][:, 0:2 * NB], ACT.Sqrt, scale=1.0 / (QL * s2), bias=eps_col[:, 1:2]).then_inc(*mark("rq_root"))
                act.preload_act_table(ACT.Exp)

                for what in PROJ[1:4]:
                    proj(0, what)

                def softmax_exp(s):
                    act.wait_ge(sem("att_max"), s + 1)
                    if s >= 4:
                        act.wait_ge(sem("att_turned"), s - 3)
                    w = (NB - s % NB) * P
                    i = NB - 1 - s % NB
                    act.activation(probs[:, s % 4, 0:w], bank[2 + s % 3][:, 0:w], ACT.Exp, bias=neg_max[:, s % 8:s % 8 + 1],
                                   scale=rq[:, 1, 2 * i:2 * i + 1],
                                   accum_out=row_sum[:, s % 8:s % 8 + 1]).then_inc(sem("att_exp"), 1)

                def turned_hi(s):
                    h, ii = divmod(s, NB)
                    i = NB - 1 - ii
                    act.wait_ge(sem("att_turned"), s + 1)
                    if h >= 2:
                        act.wait_ge(sem("att_out_done"), h - 1)
                    act.activation(pt_hi[:, h % 2, 0:i + 1, i * P:(i + 1) * P], bank[5 + s % 2][:, 0:(i + 1) * P].rearrange("p (j q) -> p j q", q=P),
                                   ACT.Copy).then_inc(sem("att_hi"), 1)

                def head_out(h):
                    act.wait_ge(sem("att_out_done"), h + 1)
                    act.activation(o_hi[:, h, :], bank[7][:, :], ACT.Copy).then_inc(sem("att_out_hi"), 1)

                for s in range(NB * HEADS + 7):
                    h, ii = divmod(s, NB)
                    if s < NB * HEADS:
                        softmax_exp(s)
                    if 0 <= s - 3 < NB * HEADS:
                        turned_hi(s - 3)
                    if s < NB * HEADS:
                        for t in after_step(h, ii):
                            proj(*t)
                        if h % 2 == 0 and ii == 0:
                            split_hi(FIRST["heads"] + 1 + h // 2)
                    if s >= 6 and (s - 6) % NB == NB - 1:
                        head_out((s - 6) // NB)
                act.preload_act_table(ACT.Sqrt)
                for u in range(1, 5):
                    split_hi(FIRST["mla_o"] + u)
                    for m in (2 * u - 2, 2 * u - 1):
                        chain("attn", m, m, gain("norm_ffn", 8 + m))

            def compress(t):
                if t == 22:
                    for kv in range(2):
                        act.wait_ge(sem("cmp_hidden"), kv + 1)
                        act.activation(h1[:, kv, :], CMP_BANKS[kv][0:64, 0:64], ACT.Silu).then_inc(sem("cmp_act"), 1)
                if t == 23:
                    act.wait_ge(sem("cmp_done"), 1)
                    act.activation(kc_st[:, 0, :, :].rearrange("p g n -> p (g n)"), CMP_BANKS[2][:, 0:64], ACT.Copy).then_inc(sem("cmp_kv_hi"), 1)
                    act.wait_ge(sem("cmp_done"), 2)
                    act.activation(vc_st[:, :, 0:64], CMP_BANKS[3][0:32, 0:P].rearrange("n (g e) -> n g e", g=2), ACT.Copy).then_inc(sem("cmp_kv_hi"), 1)
                if t == 26:
                    act.preload_act_table(ACT.Exp)
                    act.wait_ge(*at("cmp_shifted"))
                    act.activation(p_cmp, p_cmp, ACT.Exp).then_inc(*mark("cmp_exp"))
                    act.preload_act_table(ACT.Silu)

            def w_in():
                n0 = FIRST["w_in"]
                act.wait_ge(*at("ffn1_stat"))
                act.activation(root[:, :], bank[7][:, :], ACT.Sqrt, scale=1.0 / D, bias=eps_col[:, 0:1]).then_inc(*mark("ffn1_root"))
                split_hi(n0 + 1)
                act.wait_ge(*at("inner_ready"))
                act.activation(root[:, :], sq_sum[:, :], ACT.Sqrt, scale=1.0 / D, bias=eps_col[:, 0:1]).then_inc(*mark("inner_root"))
                act.preload_act_table(ACT.Silu)
                for t in range(NT):
                    kind = KINDS[t]
                    ready = (sem("u_free"), t + 1)
                    if kind == "az":
                        act.wait_ge(*ready)
                        act.activation(br[:, t, :], br[:, t, :], ACT.Silu).then_inc(sem("conv_gate"), 1)
                    elif kind == "z":
                        act.wait_ge(*ready)
                        act.activation(u_dst(t), u_dst(t), ACT.Silu).then_inc(sem("z_gate"), 1)
                    elif kind == "nq":
                        act.wait_ge(*ready)
                        for e in range(2):
                            r = slice(64 * e, 64 * e + 64)
                            act.activation(q_st[r, 2 * (t - 8) + e, :], u_dst(t)[r, :], ACT.Copy, scale=0.125).then_inc(sem("nq_hi"), 1)
                    elif kind in ("ks", "kw"):
                        act.wait_ge(*ready)
                        for g in range(2):
                            for e in range(2):
                                act.activation(k_st[64 * e:64 * e + 64, 2 * int(kind == "kw") + g, 0, :], u_dst(t)[64 * g:64 * g + 64, :], ACT.Copy)\
                                   .then_inc(sem("nk_hi"), 1)
                    elif kind == "gate":
                        act.preload_act_table(ACT.Sigmoid)
                        act.wait_ge(*ready)
                        act.activation(u_dst(t)[0:32, :], u_dst(t)[0:32, :], ACT.Sigmoid).then_inc(*mark("gates_ready"))
                        act.preload_act_table(ACT.Silu)
                    if t - 2 in VTILES:
                        v = VTILES.index(t - 2)
                        act.wait_ge(sem("nv_turned"), v + 1)
                        act.activation(v_st[:, v, :, :, 0:64], bank[5 + v][:, :].rearrange("p (j h d) -> p h j d", h=2, d=64), ACT.Copy)\
                           .then_inc(sem("nv_hi"), 1)
                    compress(t)
                    if t % 2 == 0 and t // 2 + 2 <= 17:
                        split_hi(n0 + t // 2 + 2)

            def nsa():
                act.preload_act_table(ACT.Exp)

                def softmax_exp(s):
                    h, b, i = NSTEP[s]
                    act.wait_ge(sem("n_max"), s + 1)
                    if s >= 4:
                        act.wait_ge(sem("n_turned"), s - 3)
                    w = (i + 1) * P
                    act.activation(pm[:, s % 4, 0:w], bank[s % 3][:, 0:w], ACT.Exp, bias=neg_max[:, s % 8:s % 8 + 1],
                                   accum_out=row_sum[:, s % 8:s % 8 + 1]).then_inc(sem("n_exp"), 1)

                def turned_hi(s):
                    i, u = NSTEP[s][2], s // NB
                    act.wait_ge(sem("n_turned"), s + 1)
                    if u >= 2:
                        act.wait_ge(sem("n_pv"), NB * (u - 1))
                    act.activation(pt2_hi[:, u % 2, 0:i + 1, i * P:(i + 1) * P], bank[5 + s % 2][:, 0:(i + 1) * P].rearrange("p (j q) -> p j q", q=P),
                                   ACT.Copy).then_inc(sem("n_hi"), 1)

                for s in range(len(NSTEP) + 6):
                    if s < len(NSTEP):
                        softmax_exp(s)
                    if 0 <= s - 3 < len(NSTEP):
                        turned_hi(s - 3)
                    if s < len(NSTEP) and s % 8 == 3:
                        h = s // 8
                        act.wait_ge(sem("c_turned"), h + 1)
                        if h:
                            act.wait_ge(sem("n_pv"), 8 * h - 7)
                        act.activation(ptc_hi[:, :], bank[4][0:32, :], ACT.Copy).then_inc(sem("c_hi"), 1)
                    if s >= 6 and (s - 6) % 8 == 7:
                        h = (s - 6) // 8
                        act.wait_ge(sem("n_pv"), 8 * h + 8)
                        if h:
                            act.wait_ge(sem("n_sum"), h)
                        act.activation(root[0:64, :], n_out(h)[64:128, :], ACT.Copy).then_inc(sem("n_out_act"), 1)

            def dilated():
                act.wait_ge(sem("n_scored"), len(NSTEP))
                for g in range(3):
                    for e in range(2):
                        r = slice(64 * e, 64 * e + 64)
                        act.activation(q_st[r, 2 * g + e, :], du[r, g, :], ACT.Copy, scale=0.125).then_inc(sem("dq_hi"), 1)
                kd = k_st[:, :, :, :].rearrange("p a b t -> p (a b) t")

                def keys(j):
                    if j:
                        act.wait_ge(sem("d_scored"), 12)
                    for g in range(3):
                        for e in range(2):
                            act.activation(kd[64 * e:64 * e + 64, 2 * g, :], du[64 * j:64 * j + 64, 3 + g, :], ACT.Copy).then_inc(sem("dk_hi"), 1)

                keys(0)
                for g in range(3):
                    act.wait_ge(sem("dv_turned"), g + 1)
                    act.activation(v_st[:, g, :, :, 0:64], bank[5 + g % 2][:, :].rearrange("p (j h d) -> p h j d", h=2, d=64), ACT.Copy)\
                       .then_inc(sem("dv_hi"), 1)

                def softmax_exp(s):
                    j, i = DSTEP[s]
                    act.wait_ge(sem("d_max"), s + 1)
                    for g in range(3):
                        x = 3 * s + g
                        if x >= 4:
                            act.wait_ge(sem("d_turned"), x - 3)
                        w = len(d_keys(g, i)) * P
                        act.activation(pm[:, x % 4, 0:w], bank[x % 5][:, 0:w], ACT.Exp, bias=neg_max[:, 4 + s % 2:5 + s % 2],
                                       accum_out=row_sum[:, 4 * (s % 2) + g:4 * (s % 2) + g + 1]).then_inc(sem("d_exp"), 1)

                def turned_hi(s):
                    j, i = DSTEP[s]
                    for g in range(3):
                        x = 3 * s + g
                        act.wait_ge(sem("d_turned"), x + 1)
                        if j:
                            act.wait_ge(sem("d_pv"), 3)
                        for n, kb in enumerate(d_keys(g, i)) if g == 0 else ((0, slice(0, i + 1)),):
                            src = bank[5 + x % 2][:, n * P:(n + 1) * P] if g == 0 else \
                                bank[5 + x % 2][:, 0:(i + 1) * P].rearrange("p (j q) -> p j q", q=P)
                            act.activation(pt2_hi[d_turned(g, kb, i)], src, ACT.Copy).then_inc(sem("d_hi"), 1)

                def out(j):
                    for g in range(3):
                        act.wait_ge(sem("d_pv"), 3 * j + g + 1)
                        act.wait_ge(sem("n_sum"), 6)
                        if 3 * j + g:
                            act.wait_ge(sem("d_out"), 3 * j + g)
                        act.activation(root[0:64, :], bank[7][64:128, :], ACT.Copy).then_inc(sem("d_out_act"), 1)

                for s in range(len(DSTEP) + 1):
                    if s == 4:
                        keys(1)
                    if s < len(DSTEP):
                        softmax_exp(s)
                    if s:
                        turned_hi(s - 1)
                    if s == 4:
                        out(0)
                out(1)

            def tail():
                n_out, n_pp, n_pg = FIRST["w_out"], FIRST["ple_proj"], FIRST["ple_gate"]
                act.preload_act_table(ACT.Sigmoid)
                for f in range(KD):
                    if f == 0:
                        act.wait_ge(sem("conv_step"), 14)
                        act.wait_ge(sem("d_pv"), 6)
                    elif f == 2:
                        act.wait_ge(sem("n_sum"), 6)
                    elif f >= 5:
                        act.wait_ge(sem("d_out"), f - 1)
                    act.activation(xg_hi[:, f, :], br[:, (f + 6) % 8, :], ACT.Copy).then_inc(sem("y_hi"), 1)
                for j in range(2):
                    act.wait_ge(sem("p_turned"), j + 1)
                    act.activation(p_hi[:, j, :], bank[5 + j][:, :], ACT.Copy).then_inc(sem("p_hi_ready"), 1)
                for m in range(KD):
                    if m % 2 == 0:
                        split_hi(n_out + m // 2 + 1)
                    act.wait_ge(sem("w_out_added"), m + 1)
                    act.activation(xs_hi[:, m, :], xT[:, m, :], ACT.Copy).then_inc(sem("xs_hi_ready"), 1)
                split_hi(n_pg)
                for m in range(KD):
                    if m % 2 == 0 and m < 6:
                        split_hi(n_pg + m // 2 + 1)
                    act.wait_ge(sem("ple_gate_done"), m + 1)
                    if m >= 2:
                        act.wait_ge(sem("ple_dve"), 3 * (m - 2) + 1)
                    act.activation((root, rstd)[m % 2][:, :], bank[m % 4][:, :], ACT.Sigmoid).then_inc(sem("ple_act"), 1)
                    act.wait_ge(sem("ple_dve"), 3 * m + 2)
                    act.activation(squares[:, m % 2, :], xT[:, m, :], ACT.Square).then_inc(sem("ple_act"), 1)
                    act.activation(emb[:, m, :], xT[:, m, :], ACT.Copy, scale=gain("norm_final_2", m)).then_inc(sem("fin_gained"), 1)
                act.preload_act_table(ACT.Sqrt)
                act.wait_ge(*at("fin_stat"))
                act.activation(fin[:, 0, :], bank[4][:, 0:2 * NB], ACT.Sqrt, scale=1.0 / D, bias=eps_col[:, 0:1]).then_inc(*mark("fin_root"))
                act.wait_ge(*at("fin_rstd"))
                for o in range(1, 2 * NB, 2):
                    i = o // 2
                    act.wait_ge(sem("fin_turned"), o + 1)
                    if o >= 4:
                        act.wait_ge(sem(f"out_stored{o % 4}"), 16)
                    act.wait_ge(sem("out_ready"), o)
                    act.activation(out_tok[:, o % 4, :], bank[o % 4][:, :], ACT.Copy, scale=fin[:, 1, 2 * i:2 * i + 1]).then_inc(sem("out_ready"), 1)

            ffn(0)
            mla()
            ffn(1)
            w_in()
            nsa()
            dilated()
            tail()

        @block.vector
        def _(dve):
            def split_lo(n, third=None):
                c = slice(0, U_COLS) if third is None else slice((0, 768, 1408)[third], (768, 1408, U_COLS)[third])
                dve.wait_ge(hi_sem, n + 1)
                lo = dve.tensor_tensor(w_lo[:, n % 2, c], raw(n)[:, c], w_hi[:, n % 2, c].bitcast(F32), ALU.subtract)
                if third in (None, 2):
                    lo.then_inc(lo_sem, 1)

            def chain(tag, k, m, gcol, c=None):
                dv, ac = sem(f"{tag}_dve"), sem(f"{tag}_act")
                dve.wait_ge(ac, k * 2 + 1)
                dve.scalar_tensor_tensor(xg_lo[:, m, :], xT[:, m, :], gcol, xg_hi[:, m, :].bitcast(F32), ALU.mult, ALU.subtract).then_inc(dv, 1)
                dve.wait_ge(ac, k * 2 + 2)
                dve.wait_ge(dv, k * 3)
                dve.tensor_tensor(sq_sum[:, :], sq_sum[:, :], squares[:, c if c is not None else k % 2, :], ALU.add).then_inc(dv, 1)

            MAGIC, TWO_PI = 1.5 * 2.0 ** 23, 6.283185307179586
            parts = (6.28125, 0.001934051513671875, 1.2556659146019695e-06)
            ang = sem("angle_step")
            dve.wait_ge(sem("pos_loaded"), 32)
            dve.tensor_copy(angle[:, 0, :], pos_i[:, :]).then_inc(ang, 1)
            dve.wait_ge(ang, 1)
            dve.tensor_scalar(angle[:, 0, :], angle[:, 0, :], rope_col[:, 0:1], None, ALU.mult).then_inc(ang, 1)
            dve.wait_ge(ang, 2)
            dve.tensor_scalar(angle[:, 1, :], angle[:, 0, :], 1.0 / TWO_PI, MAGIC, ALU.mult, ALU.add).then_inc(ang, 1)
            dve.wait_ge(ang, 3)
            dve.tensor_scalar(angle[:, 1, :], angle[:, 1, :], MAGIC, None, ALU.subtract).then_inc(ang, 1)
            for n, c in enumerate(parts):
                dve.wait_ge(ang, 4 + n)
                dve.scalar_tensor_tensor(angle[:, 0, :], angle[:, 1, :], -c, angle[:, 0, :], ALU.mult, ALU.add).then_inc(ang, 1)
            dve.wait_ge(ang, 7)
            dve.tensor_scalar(angle[:, 0, :], angle[:, 0, :], 3.1415925, -3.1415925, ALU.min, ALU.max).then_inc(ang, 1)
            dve.wait_ge(ang, 8)
            dve.tensor_scalar(angle[:, 1, :], angle[:, 0, :], TWO_PI / 4, None, ALU.is_gt).then_inc(ang, 1)
            dve.tensor_scalar(angle[:, 2, :], angle[:, 0, :], TWO_PI / 4, None, ALU.add).then_inc(ang, 1)
            dve.wait_ge(ang, 10)
            dve.scalar_tensor_tensor(angle[:, 1, :], angle[:, 1, :], -TWO_PI, angle[:, 2, :], ALU.mult, ALU.add).then_inc(ang, 1)
            dve.wait_ge(ang, 11)
            dve.tensor_scalar(angle[:, 1, :], angle[:, 1, :], 3.1415925, -3.1415925, ALU.min, ALU.max).then_inc(*mark("angle_ready"))
            dve.wait_ge(sem("ident_loaded"), 16)
            dve.tensor_copy(ident_r[:, :], ident[:, :]).then_inc(sem("masks_ready"), 1)
            dve.wait_ge(sem("mask_loaded"), 16)
            dve.tensor_copy(causal[:, :], masks0[:, :]).then_inc(sem("masks_ready"), 1)
            dve.wait_ge(*at("vec_turned"))
            dve.tensor_copy(cols[:, :], bank[7][:, 0:NROWS]).then_inc(*mark("cols_ready"))
            dve.wait_ge(*at("cols_ready"))
            f0, m0 = ROWS["norm_final"][0], ROWS["norm_mix_2"][0]
            dve.tensor_tensor(gain2[:, :], cols[:, f0:f0 + KD], cols[:, m0:m0 + KD], ALU.mult).then_inc(*mark("gain2_ready"))
            dve.wait_ge(*at("tok_root"))
            dve.reciprocal(tok_stat[:, 2, :], tok_stat[:, 1, :]).then_inc(*mark("tok_rstd"))
            dve.wait_ge(*at("tok_rstd"))
            for i in range(NB):
                dve.tensor_scalar(h_tok[:, i, :], x_tok[:, i, :], tok_stat[:, 2, i:i + 1], None, ALU.mult).then_inc(sem("h_tok_ready"), 1)
            dve.wait_ge(sem("sin_done"), 2)
            dve.tensor_scalar(sin_t[:, :], sin_t[:, :], rope_col[:, 1:2], None, ALU.mult).then_inc(*mark("rope_ready"))
            split_lo(0)
            for m in range(KD):
                dve.wait_ge(sem("x_turned"), m + 1)
                dve.tensor_copy(xT[:, m, :], bank[m % 4][:, :]).then_inc(sem("xT_ready"), 1)
            dve.memset(sq_sum[:, :], 0.0).then_inc(*mark("sum_clear"))
            dve.wait_ge(*at("cols_ready"))
            for c in range(KD):
                dve.wait_ge(sem("pooled_hi"), c + 1)
                dve.scalar_tensor_tensor(pooled_lo[:, c, :], bank[4 + c % 2][:, :], gain("norm_mix", c), pooled_hi[:, c, :].bitcast(F32),
                                         ALU.mult, ALU.subtract).then_inc(sem("pooled_lo"), 1)
            split_lo(1)
            dve.wait_ge(sem("xT_ready"), KD)
            dve.wait_ge(*at("sum_clear"))
            for m in range(KD):
                dve.wait_ge(sem("mixed_done"), m + 1)
                dve.scalar_tensor_tensor(xT[:, m, :], bank[m % 4][:, :], gain("pool_scale", m), xT[:, m, :], ALU.mult, ALU.add).then_inc(sem("mix_dve"), 1)
                chain("mix", m, m, gain("norm_ffn", m))

            def ffn(l):
                tag, to = ffn_from[l], ffn_to[l]
                n0, d0 = FIRST[f"gateup{l}"], FIRST[f"down{l}"]
                gu, gd, ga, dn = sem(f"gateup{l}_done"), sem(f"gated{l}_dve"), sem(f"gated{l}_act"), sem(f"down{l}_done")
                dve.wait_ge(*at(f"{tag}_root"))
                dve.reciprocal(rstd[:, :], root[:, :]).then_inc(*mark(f"{tag}_rstd"))
                dve.memset(sq_sum[:, :], 0.0).then_inc(sem(f"{to}_clear"), 1)
                dve.memset(sq_sum2[:, :], 0.0).then_inc(sem(f"{to}_clear"), 1)
                dve.wait_ge(*at(f"{tag}_rstd"))
                dve.wait_ge(sem(f"{to}_clear"), 2)

                def gateup_turn(i, first):
                    for j in (1, 2):
                        n = n0 + j
                        dve.wait_ge(hi_sem, i * 2 + (n + 1))
                        dve.tensor_tensor(w_lo[:, n % 2, :], raw(n), w_hi[:, n % 2, :].bitcast(F32), ALU.subtract).then_inc(lo_sem, 1)
                    for c in range(2):
                        dve.wait_ge(gu, i * 4 + c + 1)
                        if not (first and c == 0):
                            dve.wait_ge(gd, i * 8 + 4 * c)
                        dve.tensor_tensor(gate_z, bank[c][:, :], rstd[:, :], ALU.mult).then_inc(gd, 1)
                        dve.wait_ge(gu, i * 4 + c + 3)
                        dve.tensor_tensor(up_z, bank[2 + c][:, :], rstd[:, :], ALU.mult).then_inc(gd, 1)
                        dve.wait_ge(gd, i * 8 + 4 * c + 2)
                        dve.wait_ge(ga, i * 4 + 2 * c + 1)
                        dve.tensor_tensor(gate_z, gate_s, up_z, ALU.mult).then_inc(gd, 1)
                        dve.wait_ge(ga, i * 4 + 2 * c + 2)
                        f = bass.ds(i * 2 + c, 1)
                        dve.tensor_tensor(act_lo[:, f, :].rearrange("p a t -> p (a t)"), gate_z,
                                          act_hi[:, f, :].bitcast(F32).rearrange("p a t -> p (a t)"), ALU.subtract).then_inc(gd, 1)
                gateup_turn(0, True)
                with dve.Fori(1, 11) as i:
                    gateup_turn(i, False)
                dv, ac = sem(f"{to}_dve"), sem(f"{to}_act")

                def down_turn(q, first):
                    for j in range(4):
                        n = d0 + j + 1
                        dve.wait_ge(hi_sem, q * 4 + (n + 1))
                        dve.tensor_tensor(w_lo[:, n % 2, :], raw(n), w_hi[:, n % 2, :].bitcast(F32), ALU.subtract).then_inc(lo_sem, 1)
                    for c in range(2):
                        k = q * 2 + c
                        xt = xT[:, bass.ds(k, 1), :].rearrange("p a t -> p (a t)")
                        xh = xg_hi[:, bass.ds(k, 1), :].bitcast(F32).rearrange("p a t -> p (a t)")
                        xl = xg_lo[:, bass.ds(k, 1), :].rearrange("p a t -> p (a t)")
                        dve.wait_ge(dn, q * 8 + 7 + c)
                        dve.tensor_tensor(xt, bank[c][:, :], xt, ALU.add).then_inc(dv, 1)
                        dve.wait_ge(ac, q * (4 + 2 * l) + (2 + l) * c + 1)
                        dve.scalar_tensor_tensor(xl, xt, ffn_gain(l, k), xh, ALU.mult, ALU.subtract).then_inc(dv, 1)
                        dve.wait_ge(ac, q * (4 + 2 * l) + (2 + l) * c + 2)
                        if not (first and c == 0):
                            dve.wait_ge(dv, q * (6 + 2 * l) + (3 + l) * c)
                        dve.tensor_tensor(sq_sum[:, :], sq_sum[:, :], squares[:, c, :], ALU.add).then_inc(dv, 1)
                        if l == 1:
                            dve.wait_ge(ac, q * 6 + 3 * c + 3)
                            dve.tensor_tensor(sq_sum2[:, :], sq_sum2[:, :], root[:, :], ALU.add).then_inc(dv, 1)

                down_turn(0, True)
                with dve.Fori(1, 4) as q:
                    down_turn(q, False)

            def mla():
                n0 = FIRST["mla_down"]
                split_lo(n0 + 1)
                dve.wait_ge(*at("ffn0_root"))
                dve.reciprocal(rstd[:, :], root[:, :]).then_inc(*mark("ffn0_rstd"))
                dve.wait_ge(*at("ffn0_rstd"))
                dve.wait_ge(sem("mla_down_done"), 1)
                dve.tensor_tensor(down_q[:, 3, :], bank[0][:, :], rstd[:, :], ALU.mult).then_inc(sem("down_q_ready"), 1)

                def queries(n):
                    t, idx = QUERY_TILES[n], (1, 4, 5)[n]
                    dve.wait_ge(sem("mla_down_done"), idx + 1)
                    dve.tensor_tensor(down_q[:, t, :], bank[idx][:, :], rstd[:, :], ALU.mult).then_inc(sem("down_q_ready"), 1)
                    dve.wait_ge(sem("cq_act"), 2 * n + 2)
                    dve.scalar_tensor_tensor(cq_lo[:, t, :], down_q[:, t, :], gain("mla_q_norm", t), cq_hi[:, t, :].bitcast(F32),
                                             ALU.mult, ALU.subtract).then_inc(sem("cq_lo"), 1)
                    if n:
                        dve.wait_ge(sem("cq_act"), 2 * n + 3)
                        if n == 2:
                            dve.wait_ge(sem("cq_sum"), 1)
                        dve.tensor_tensor(sq_sum[:, :], sq_sum[:, :], squares[:, n - 1, :], ALU.add).then_inc(sem("cq_sum"), 1)

                dve.wait_ge(*at("rope_ready"))
                dve.tensor_tensor(cos_s, cos_t[:, :], rstd[:, :], ALU.mult).then_inc(sem("kr_step"), 1)
                dve.tensor_tensor(sin_s, sin_t[:, :], rstd[:, :], ALU.mult).then_inc(sem("kr_step"), 1)
                queries(0)
                split_lo(n0 + 2)
                dve.wait_ge(sem("kr_step"), 2)
                dve.wait_ge(sem("mla_down_done"), 3)
                dve.tensor_tensor(root[:, :], bank[2][:, :], cos_s, ALU.mult).then_inc(sem("kr_step"), 1)
                dve.wait_ge(sem("mla_down_done"), 4)
                dve.tensor_tensor(sq_sum2[:, :], bank[3][:, :], sin_s, ALU.mult).then_inc(sem("kr_step"), 1)
                dve.wait_ge(sem("kr_step"), 4)
                dve.tensor_tensor(root[:, :], root[:, :], sq_sum2[:, :], ALU.add).then_inc(*mark("kr_ready"))
                dve.wait_ge(*at("kv_root"))
                dve.wait_ge(*at("kr_ready"))
                dve.reciprocal(sq_sum2[:, :], squares[:, 1, :]).then_inc(*mark("rkv_ready"))
                dve.wait_ge(*at("rkv_ready"))
                dve.scalar_tensor_tensor(down_q[:, 3, :], down_q[:, 3, :], gain("mla_kv_norm", 0), sq_sum2[:, :], ALU.mult, ALU.mult)\
                   .then_inc(*mark("ckv_ready"))
                dve.wait_ge(*at("kr_hi"))
                dve.tensor_tensor(kr_lo[:, :], root[:, :], kr_hi[:, :].bitcast(F32), ALU.subtract).then_inc(*mark("kr_lo"))
                dve.wait_ge(*at("ckv_hi"))
                dve.tensor_tensor(ckv_lo[:, :], down_q[:, 3, :], ckv_hi[:, :].bitcast(F32), ALU.subtract).then_inc(*mark("ckv_lo"))
                split_lo(n0 + 3)
                queries(1)
                queries(2)
                def proj(pr, what):
                    idx = 8 * pr + PROJ.index(what)
                    h = 2 * pr + int(what[-1] == "1")
                    ps = bank[idx % 2][:, :]
                    dve.wait_ge(sem("proj_done"), idx + 1)
                    done = sem("proj_ready")
                    if idx:
                        dve.wait_ge(done, idx)
                    if what == "u":
                        dve.tensor_tensor(squares[:, 0, :], ps, cos_t[:, :], ALU.mult).then_inc(done, 1)
                        return
                    hi = 7 * pr + [x for x in PROJ if x != "u"].index(what) + 1
                    if what == "us":
                        dve.tensor_tensor(squares[:, 1, :], ps, sin_t[:, :], ALU.mult).then_inc(sem("rope_step"), 1)
                        dve.wait_ge(sem("rope_step"), pr + 1)
                        dve.tensor_tensor(squares[:, 0, :], squares[:, 0, :], squares[:, 1, :], ALU.add).then_inc(sem("proj_tmp"), 1)
                        src, (dst_hi, dst_lo) = squares[:, 0, :], rotary_q(pr)
                    else:
                        src = ps
                    if what != "us":
                        dst_hi, dst_lo = (x[:, {"q": QN, "k": KN, "v": VV}[what[0]] + h % 2, :] for x in (xg_hi, xg_lo))
                    dve.wait_ge(sem("proj_hi"), hi)
                    dve.tensor_tensor(dst_lo, src, dst_hi.bitcast(F32), ALU.subtract).then_inc(done, 1)

                proj(0, "kn0")
                dve.wait_ge(*at("rq_root"))
                dve.reciprocal(rq[:, 1, :], rq[:, 0, :]).then_inc(*mark("rq_ready"))
                dve.wait_ge(*at("rq_ready"))

                for what in PROJ[1:4]:
                    proj(0, what)

                def row_max(s):
                    w = (NB - s % NB) * P
                    dve.wait_ge(sem("att_scored"), s + 1)
                    i = NB - 1 - s % NB
                    c = slice(s % 8, s % 8 + 1)
                    dve.tensor_reduce(row_top[:, c], bank[2 + s % 3][:, 0:w], AX.X, ALU.max, negate=True).then_inc(sem("att_top"), 1)
                    dve.wait_ge(sem("att_top"), s + 1)
                    dve.tensor_tensor(neg_max[:, c], row_top[:, c], rq[:, 1, 2 * i:2 * i + 1], ALU.mult).then_inc(sem("att_max"), 1)

                def normalise(s):
                    w = (NB - s % NB) * P
                    dve.wait_ge(sem("att_exp"), s + 1)
                    dve.reciprocal(row_inv[:, s % 8:s % 8 + 1], row_sum[:, s % 8:s % 8 + 1]).then_inc(sem("att_inv"), 1)
                    dve.wait_ge(sem("att_inv"), s + 1)
                    dve.tensor_scalar(probs[:, s % 4, 0:w], probs[:, s % 4, 0:w], row_inv[:, s % 8:s % 8 + 1], None, ALU.mult)\
                       .then_inc(sem("att_probs"), 1)

                def turned_lo(s):
                    h, ii = divmod(s, NB)
                    i = NB - 1 - ii
                    dve.wait_ge(sem("att_hi"), s + 1)
                    at = (slice(None), h % 2, slice(0, i + 1), slice(i * P, (i + 1) * P))
                    dve.tensor_tensor(pt_lo[at], bank[5 + s % 2][:, 0:(i + 1) * P].rearrange("p (j q) -> p j q", q=P),
                                      pt_hi[at].bitcast(F32), ALU.subtract).then_inc(sem("att_lo"), 1)

                def head_out(h):
                    dve.wait_ge(sem("att_out_hi"), h + 1)
                    dve.tensor_tensor(o_lo[:, h, :], bank[7][:, :], o_hi[:, h, :].bitcast(F32), ALU.subtract).then_inc(sem("att_out"), 1)

                for s in range(NB * HEADS + 7):
                    h, ii = divmod(s, NB)
                    if s < NB * HEADS:
                        row_max(s)
                    if 0 <= s - 1 < NB * HEADS:
                        normalise(s - 1)
                    if 0 <= s - 4 < NB * HEADS:
                        turned_lo(s - 4)
                    if s < NB * HEADS:
                        for t in after_step(h, ii):
                            proj(*t)
                        if h % 2 == 0 and ii >= 1:
                            split_lo(FIRST["heads"] + 1 + h // 2, ii - 1)
                    if s >= 6 and (s - 6) % NB == NB - 1:
                        head_out((s - 6) // NB)
                dve.memset(sq_sum[:, :], 0.0).then_inc(*mark("attn_clear"))
                dve.wait_ge(*at("attn_clear"))
                for u in range(1, 5):
                    split_lo(FIRST["mla_o"] + u)
                    for m in (2 * u - 2, 2 * u - 1):
                        dve.wait_ge(sem("mla_o_done"), m + 1)
                        dve.tensor_tensor(xT[:, m, :], bank[m % 4][:, :], xT[:, m, :], ALU.add).then_inc(sem("attn_dve"), 1)
                        chain("attn", m, m, gain("norm_ffn", 8 + m))

            def compress(t):
                st = sem("cmp_step")
                pc = p_cmp.rearrange("p (x n) -> p x n", n=32)

                def wide(k):
                    return cst[:, k, :].rearrange("p (x o) -> p x o", o=1).to_broadcast([P, 24, 32])

                def by_head(k):
                    return cst[:, k, :].rearrange("p (h i) -> p h i", h=6)

                if t == 20:
                    dve.wait_ge(*at("pe_turned"))
                    dve.tensor_copy(pe_cols[:, :, :].rearrange("p j l -> p (j l)"), bank[6][:, 0:64]).then_inc(*mark("pe_kept"))
                    dve.wait_ge(*at("pe_kept"))
                    dve.wait_ge(*at("kcv_padded"))
                    dve.wait_ge(sem("u_free"), KINDS.index("vc") + 1)
                    for kv in range(2):
                        for g in range(2):
                            for par in range(2):
                                r = slice(64 * g, 64 * g + 64)
                                win = bass.AP(kcv.tensor, kcv[r, kv, par:par + 1].offset, [list(kcv[r, kv, 0:1].ap[0]), [2, 16], [16, 32]])
                                off = pe_cols[r, kv, par:32:2].rearrange("p (l o) -> p l o", o=1).to_broadcast([64, 16, 32])
                                dve.tensor_tensor(cpe[kv][64 * par:64 * par + 64, :, g, :], win, off, ALU.add).then_inc(sem("cmp_windows"), 1)
                if t == 23:
                    dve.wait_ge(sem("cmp_kv_hi"), 1)
                    dve.tensor_tensor(kc_st[:, 1, :, :].rearrange("p g n -> p (g n)"), CMP_BANKS[2][:, 0:64],
                                      kc_st[:, 0, :, :].bitcast(F32).rearrange("p g n -> p (g n)"), ALU.subtract).then_inc(sem("cmp_kv_lo"), 1)
                    dve.wait_ge(sem("cmp_kv_hi"), 2)
                    dve.tensor_tensor(vc_st[:, :, 64:128], CMP_BANKS[3][0:32, 0:P].rearrange("n (g e) -> n g e", g=2),
                                      vc_st[:, :, 0:64].bitcast(F32), ALU.subtract).then_inc(sem("cmp_kv_lo"), 1)
                if t == 25:
                    dve.wait_ge(*at("c_scored"))
                    cm = cmask[:, :, :].rearrange("p i n -> p (i n)").rearrange("p (o c) -> p o c", o=1)
                    dve.tensor_tensor(p_cmp[:, 0:512].rearrange("p (h c) -> p h c", h=4), CMP_BANKS[0][:, :].rearrange("p (h c) -> p h c", h=4),
                                      cm.to_broadcast([P, 4, P]), ALU.add).then_inc(st, 1)
                    dve.tensor_tensor(p_cmp[:, 512:768].rearrange("p (h c) -> p h c", h=2), CMP_BANKS[1][:, 0:256].rearrange("p (h c) -> p h c", h=2),
                                      cm.to_broadcast([P, 2, P]), ALU.add).then_inc(st, 1)
                    dve.wait_ge(st, 2)
                    dve.tensor_reduce(cst[:, 0, :], pc, AX.X, ALU.max).then_inc(st, 1)
                    dve.wait_ge(st, 3)
                    dve.tensor_tensor(pc, pc, wide(0), ALU.subtract).then_inc(*mark("cmp_shifted"))
                if t == 27:
                    dve.wait_ge(*at("cmp_exp"))
                    dve.tensor_reduce(cst[:, 1, :], pc, AX.X, ALU.add).then_inc(st, 1)
                    dve.wait_ge(st, 4)
                    dve.reciprocal(cst[:, 2, :], cst[:, 1, :]).then_inc(st, 1)
                    dve.wait_ge(st, 5)
                    dve.tensor_tensor(by_head(2), by_head(2), cvalid[:, :].rearrange("p (o i) -> p o i", o=1).to_broadcast([P, 6, NB]), ALU.mult).then_inc(st, 1)
                    dve.wait_ge(st, 6)
                    dve.wait_ge(*at("gates_kept"))
                    dve.tensor_tensor(by_head(3), by_head(2), gates[:, :, 0:18:3].rearrange("p i h -> p h i"), ALU.mult).then_inc(st, 1)
                    dve.wait_ge(st, 7)
                    dve.tensor_tensor(pc, pc, wide(3), ALU.mult).then_inc(*mark("cmp_probs"))

            def w_in():
                n0 = FIRST["w_in"]
                dve.wait_ge(*at("ffn1_root"))
                dve.reciprocal(rstd[:, :], root[:, :]).then_inc(*mark("ffn1_rstd"))
                dve.wait_ge(*at("ffn1_rstd"))
                dve.wait_ge(*at("inner_stat"))
                dve.tensor_tensor(sq_sum[:, :], bank[6][:, :], rstd[:, :], ALU.mult).then_inc(sem("inner_step"), 1)
                dve.wait_ge(sem("inner_step"), 1)
                dve.tensor_tensor(sq_sum[:, :], sq_sum[:, :], rstd[:, :], ALU.mult).then_inc(*mark("inner_ready"))
                split_lo(n0 + 1)
                dve.wait_ge(*at("inner_root"))
                dve.reciprocal(sq_sum2[:, :], root[:, :]).then_inc(sem("inner_step"), 1)
                dve.wait_ge(sem("inner_step"), 2)
                dve.tensor_tensor(sq_sum2[:, :], sq_sum2[:, :], rstd[:, :], ALU.mult).then_inc(sem("inner_step"), 1)
                dve.wait_ge(sem("mix_loaded"), 9 * 16)
                dve.tensor_copy(dmask[:, :, :].rearrange("p m c -> p (m c)"), du[:, 0:2, :].rearrange("p a t -> p (a t)")[:, 0:5 * P]).then_inc(*mark("dmask_ready"))
                dve.memset(kcv[:, :, T:528], 0.0).then_inc(*mark("kcv_padded"))
                dve.wait_ge(sem("inner_step"), 3)

                cv = sem("conv_step")

                def conv(n):
                    c0 = 7 * n
                    tap = lambda k: gain("conv_w_2", 2 * k + n)
                    v, c, b, z = br[:, 2 + n, :], br[:, 4 + n, :], br[:, n, :], br[:, 6 + n, :]
                    dve.wait_ge(sem("u_free"), 8)
                    dve.tensor_tensor(v, v, c, ALU.mult).then_inc(cv, 1)
                    dve.wait_ge(cv, c0 + 1)
                    dve.tensor_scalar(c, v, tap(2), gain("conv_b_2", n), ALU.mult, ALU.add).then_inc(cv, 1)
                    for k in (1, 2):
                        dve.wait_ge(cv, c0 + 1 + k)
                        dve.scalar_tensor_tensor(c[:, k:T], v[:, 0:T - k], tap(2 - k), c[:, k:T], ALU.mult, ALU.add).then_inc(cv, 1)
                    dve.wait_ge(cv, c0 + 4)
                    dve.tensor_tensor(b, b, c, ALU.mult).then_inc(cv, 1)
                    dve.wait_ge(cv, c0 + 5)
                    dve.wait_ge(sem("conv_gate"), n + 1)
                    dve.tensor_tensor(z, z, b, ALU.mult).then_inc(cv, 2)

                for t in range(NT):
                    kind, dst = KINDS[t], u_dst(t)
                    dve.wait_ge(sem("u_done"), t + 1)
                    if t in SCRATCHED and SCRATCHED.index(t) >= 2:
                        last = SCRATCHED[SCRATCHED.index(t) - 2]
                        if KINDS[last] == "nq":
                            dve.wait_ge(sem("nq_lo"), 2 * (last - 8) + 2)
                        elif KINDS[last][0] == "k":
                            dve.wait_ge(sem("nk_lo"), 4 + 4 * int(KINDS[last] == "kw"))
                        elif KINDS[last][0] == "v":
                            dve.wait_ge(sem("nv_turned"), VTILES.index(last) + 1)
                    if t == 23:
                        dve.wait_ge(sem("cmp_hidden"), 2)
                    if kind == "z":
                        dve.wait_ge(cv, 14)
                    dve.tensor_tensor(dst, bank[t % 4][:, :], sq_sum2[:, :], ALU.mult).then_inc(sem("u_free"), 1)
                    if kind == "nq":
                        for e in range(2):
                            r, other = slice(64 * e, 64 * e + 64), slice(64 - 64 * e, 128 - 64 * e)
                            h = 2 * (t - 8) + e
                            dve.wait_ge(sem("nq_hi"), h + 1)
                            dve.scalar_tensor_tensor(q_st[other, h, :], dst[r, :], 0.125, q_st[r, h, :].bitcast(F32), ALU.mult, ALU.subtract)\
                               .then_inc(sem("nq_lo"), 1)
                    elif kind in ("ks", "kw"):
                        b = int(kind == "kw")
                        for g in range(2):
                            r = slice(64 * g, 64 * g + 64)
                            dve.wait_ge(sem("nk_hi"), 4 * b + 2 * g + 2)
                            for e in range(2):
                                dve.tensor_tensor(k_st[64 * e:64 * e + 64, 2 * b + g, 1, :], dst[r, :], k_st[r, 2 * b + g, 0, :].bitcast(F32),
                                                  ALU.subtract).then_inc(sem("nk_lo"), 1)
                    if t - 2 in VTILES:
                        v = VTILES.index(t - 2)
                        dve.wait_ge(sem("nv_hi"), v + 1)
                        dve.tensor_tensor(v_st[:, v, :, :, 64:128], bank[5 + v][:, :].rearrange("p (j h d) -> p h j d", h=2, d=64),
                                          v_st[:, v, :, :, 0:64].bitcast(F32), ALU.subtract).then_inc(sem("nv_lo"), 1)
                    if t == 19:
                        dve.wait_ge(*at("g_turned"))
                        dve.tensor_copy(gates[:, :, :].rearrange("p i c -> p (i c)"), bank[5][:, 0:P]).then_inc(*mark("gates_kept"))
                    if t == 8:
                        conv(0)
                    if t == 10:
                        conv(1)
                    if t >= 24 and t < 32:
                        m = t - 24
                        dve.wait_ge(sem("ffn1_act"), 24)
                        dve.scalar_tensor_tensor(xT[:, m, :], xT[:, m, :], gain("norm_final", m), rstd[:, :], ALU.mult, ALU.mult)\
                           .then_inc(sem("x_normed"), 1)
                    compress(t)
                    if t % 2 == 0 and t // 2 + 2 <= 17:
                        split_lo(n0 + t // 2 + 2)

            def add_halves(r, ps, dst, done):
                dve.tensor_tensor(sq_sum[r, :], ps[0:64, :], root[0:64, :], ALU.add).then_inc(sem("halves"), 1)
                sums[0] += 1
                dve.wait_ge(sem("halves"), sums[0])
                dve.tensor_tensor(dst, dst, sq_sum[r, :], ALU.mult).then_inc(done, 1)

            sums = [0]

            def nsa():
                dve.wait_ge(sem("z_gate"), 6)

                def row_max(s):
                    i = NSTEP[s][2]
                    dve.wait_ge(sem("n_scored"), s + 1)
                    dve.tensor_reduce(neg_max[:, s % 8:s % 8 + 1], bank[s % 3][:, 0:(i + 1) * P], AX.X, ALU.max, negate=True).then_inc(sem("n_max"), 1)

                def normalise(s):
                    h, b, i = NSTEP[s]
                    w = (i + 1) * P
                    dve.wait_ge(sem("n_exp"), s + 1)
                    dve.reciprocal(row_inv[:, s % 8:s % 8 + 1], row_sum[:, s % 8:s % 8 + 1]).then_inc(sem("n_inv"), 1)
                    dve.wait_ge(sem("n_inv"), s + 1)
                    c = 3 * h + 1 + b
                    dve.tensor_scalar(pm[:, s % 4, 0:w], pm[:, s % 4, 0:w], row_inv[:, s % 8:s % 8 + 1], gates[:, i, c:c + 1], ALU.mult, ALU.mult)\
                       .then_inc(sem("n_probs"), 1)

                def turned_lo(s):
                    i, u = NSTEP[s][2], s // NB
                    dve.wait_ge(sem("n_hi"), s + 1)
                    at = (slice(None), u % 2, slice(0, i + 1), slice(i * P, (i + 1) * P))
                    dve.tensor_tensor(pt2_lo[at], bank[5 + s % 2][:, 0:(i + 1) * P].rearrange("p (j q) -> p j q", q=P),
                                      pt2_hi[at].bitcast(F32), ALU.subtract).then_inc(sem("n_lo"), 1)

                for s in range(len(NSTEP) + 6):
                    if s < len(NSTEP):
                        row_max(s)
                    if 0 <= s - 1 < len(NSTEP):
                        normalise(s - 1)
                    if 0 <= s - 4 < len(NSTEP):
                        turned_lo(s - 4)
                    if s < len(NSTEP) and s % 8 == 3:
                        dve.wait_ge(sem("c_hi"), s // 8 + 1)
                        dve.tensor_tensor(ptc_lo[:, :], bank[4][0:32, :], ptc_hi[:, :].bitcast(F32), ALU.subtract).then_inc(sem("c_lo"), 1)
                    if s >= 6 and (s - 6) % 8 == 7:
                        h = (s - 6) // 8
                        r = slice(64 * (h % 2), 64 * (h % 2) + 64)
                        dve.wait_ge(sem("n_out_act"), h + 1)
                        add_halves(r, n_out(h), br[r, h // 2, :], sem("n_sum"))

            def dilated():
                for g in range(3):
                    for e in range(2):
                        r, other = slice(64 * e, 64 * e + 64), slice(64 - 64 * e, 128 - 64 * e)
                        dve.wait_ge(sem("dq_hi"), 2 * g + e + 1)
                        dve.scalar_tensor_tensor(q_st[other, 2 * g + e, :], du[r, g, :], 0.125, q_st[r, 2 * g + e, :].bitcast(F32),
                                                 ALU.mult, ALU.subtract).then_inc(sem("dq_lo"), 1)
                kd = k_st[:, :, :, :].rearrange("p a b t -> p (a b) t")

                def keys(j):
                    r = slice(64 * j, 64 * j + 64)
                    for g in range(3):
                        dve.wait_ge(sem("dk_hi"), 6 * j + 2 * g + 2)
                        for e in range(2):
                            dve.tensor_tensor(kd[64 * e:64 * e + 64, 2 * g + 1, :], du[r, 3 + g, :], kd[r, 2 * g, :].bitcast(F32), ALU.subtract)\
                               .then_inc(sem("dk_lo"), 1)

                keys(0)
                for g in range(3):
                    dve.wait_ge(sem("dv_hi"), g + 1)
                    dve.tensor_tensor(v_st[:, g, :, :, 64:128], bank[5 + g % 2][:, :].rearrange("p (j h d) -> p h j d", h=2, d=64),
                                      v_st[:, g, :, :, 0:64].bitcast(F32), ALU.subtract).then_inc(sem("dv_lo"), 1)

                def row_max(s):
                    j, i = DSTEP[s]
                    if s >= 2:
                        dve.wait_ge(sem("d_exp"), 3 * (s - 1))
                    for g in range(3):
                        x = 3 * s + g
                        dve.wait_ge(sem("d_scored"), x + 1)
                        dve.tensor_reduce(row_inv[:, 4 * (s % 2) + g:4 * (s % 2) + g + 1], bank[x % 5][:, 0:len(d_keys(g, i)) * P], AX.X, ALU.max)\
                           .then_inc(sem("d_max3"), 1)
                    dve.wait_ge(sem("d_max3"), 3 * s + 3)
                    dve.tensor_reduce(neg_max[:, 4 + s % 2:5 + s % 2], row_inv[:, 4 * (s % 2):4 * (s % 2) + 3], AX.X, ALU.max, negate=True)\
                       .then_inc(sem("d_max"), 1)

                def normalise(s):
                    j, i = DSTEP[s]
                    c = 4 * (s % 2)
                    dve.wait_ge(sem("d_exp"), 3 * s + 3)
                    dve.tensor_reduce(neg_max[:, s % 2:s % 2 + 1], row_sum[:, c:c + 3], AX.X, ALU.add).then_inc(sem("d_inv"), 1)
                    dve.wait_ge(sem("d_inv"), 2 * s + 1)
                    dve.reciprocal(neg_max[:, 2 + s % 2:3 + s % 2], neg_max[:, s % 2:s % 2 + 1]).then_inc(sem("d_inv"), 1)
                    dve.wait_ge(sem("d_inv"), 2 * s + 2)
                    for g in range(3):
                        x = 3 * s + g
                        w = len(d_keys(g, i)) * P
                        dve.tensor_scalar(pm[:, x % 4, 0:w], pm[:, x % 4, 0:w], neg_max[:, 2 + s % 2:3 + s % 2], None, ALU.mult).then_inc(sem("d_probs"), 1)

                parts = [0]

                def turned_lo(s):
                    j, i = DSTEP[s]
                    for g in range(3):
                        x = 3 * s + g
                        todo = [(n, kb) for n, kb in enumerate(d_keys(g, i))] if g == 0 else [(0, slice(0, i + 1))]
                        parts[0] += len(todo)
                        dve.wait_ge(sem("d_hi"), parts[0])
                        for m, (n, kb) in enumerate(todo):
                            src = bank[5 + x % 2][:, n * P:(n + 1) * P] if g == 0 else \
                                bank[5 + x % 2][:, 0:(i + 1) * P].rearrange("p (j q) -> p j q", q=P)
                            at = d_turned(g, kb, i)
                            dve.tensor_tensor(pt2_lo[at], src, pt2_hi[at].bitcast(F32), ALU.subtract)\
                               .then_inc(sem("d_lo") if m == len(todo) - 1 else sem("d_lo_part"), 1)

                def out(j):
                    for g in range(3):
                        r = slice(64 * j, 64 * j + 64)
                        dve.wait_ge(sem("d_out_act"), 3 * j + g + 1)
                        add_halves(r, bank[7], br[r, 3 + g, :], sem("d_out"))

                for s in range(len(DSTEP) + 1):
                    if s == 4:
                        keys(1)
                    if s < len(DSTEP):
                        row_max(s)
                    if s:
                        normalise(s - 1)
                        turned_lo(s - 1)
                    if s == 4:
                        out(0)
                out(1)

            def tail():
                n_out, n_pp, n_pg = FIRST["w_out"], FIRST["ple_proj"], FIRST["ple_gate"]
                for f in range(KD):
                    dve.wait_ge(sem("y_hi"), f + 1)
                    dve.tensor_tensor(xg_lo[:, f, :], br[:, (f + 6) % 8, :], xg_hi[:, f, :].bitcast(F32), ALU.subtract).then_inc(sem("y_lo"), 1)
                for j in range(2):
                    dve.wait_ge(sem("p_hi_ready"), j + 1)
                    dve.tensor_tensor(p_lo[:, j, :], bank[5 + j][:, :], p_hi[:, j, :].bitcast(F32), ALU.subtract).then_inc(sem("p_lo_ready"), 1)
                dve.memset(sq_sum[:, :], 0.0).then_inc(*mark("fin_clear"))
                dve.wait_ge(sem("x_normed"), KD)
                for m in range(KD):
                    if m % 2 == 0:
                        split_lo(n_out + m // 2 + 1)
                    dve.wait_ge(sem("w_out_done"), m + 1)
                    dve.tensor_tensor(xT[:, m, :], bank[m % 4][:, :], xT[:, m, :], ALU.add).then_inc(sem("w_out_added"), 1)
                    dve.wait_ge(sem("xs_hi_ready"), m + 1)
                    dve.tensor_tensor(xs_lo[:, m, :], xT[:, m, :], xs_hi[:, m, :].bitcast(F32), ALU.subtract).then_inc(sem("xs_lo_ready"), 1)
                split_lo(n_pg)
                for m in range(KD):
                    dve.wait_ge(sem("ple_proj_done"), m + 1)
                    dve.tensor_copy(emb[:, m, :], bank[4 + m % 2][:, :]).then_inc(sem("emb_ready"), 1)
                dve.wait_ge(sem("emb_ready"), KD)
                dve.wait_ge(*at("fin_clear"))
                pd = sem("ple_dve")
                for m in range(KD):
                    if m % 2 == 0 and m < 6:
                        split_lo(n_pg + m // 2 + 1)
                    gate = (root, rstd)[m % 2][:, :]
                    dve.wait_ge(sem("ple_act"), 2 * m + 1)
                    dve.tensor_tensor(gate, gate, emb[:, m, :], ALU.mult).then_inc(sem("ple_step"), 1)
                    dve.wait_ge(sem("ple_step"), m + 1)
                    dve.wait_ge(sem("w_out_added"), KD)
                    dve.tensor_tensor(xT[:, m, :], xT[:, m, :], gate, ALU.add).then_inc(pd, 2)
                    dve.wait_ge(sem("ple_act"), 2 * m + 2)
                    dve.wait_ge(pd, 3 * m)
                    dve.tensor_tensor(sq_sum[:, :], sq_sum[:, :], squares[:, m % 2, :], ALU.add).then_inc(pd, 1)
                dve.wait_ge(*at("fin_root"))
                dve.reciprocal(fin[:, 1, :], fin[:, 0, :]).then_inc(*mark("fin_rstd"))
                dve.wait_ge(*at("fin_rstd"))
                for o in range(0, 2 * NB, 2):
                    i = o // 2
                    dve.wait_ge(sem("fin_turned"), o + 1)
                    if o >= 4:
                        dve.wait_ge(sem(f"out_stored{o % 4}"), 16)
                    if o:
                        dve.wait_ge(sem("out_ready"), o)
                    dve.tensor_scalar(out_tok[:, o % 4, :], bank[o % 4][:, :], fin[:, 1, 2 * i:2 * i + 1], None, ALU.mult).then_inc(sem("out_ready"), 1)

            ffn(0)
            mla()
            ffn(1)
            w_in()
            nsa()
            dilated()
            tail()

        @block.tensor
        def _(pe):
            def triple(o, wh, wl, xh, xl, start, stop):
                pe.matmul(o, wh, xh, start=start, stop=False, skip_group_check=True)
                pe.matmul(o, wh, xl, start=False, stop=False, skip_group_check=True)
                return pe.matmul(o, wl, xh, start=False, stop=stop, skip_group_check=True)

            def chunk(o, n, nk, c, xh, xl, start=True, stop=True, k0=0, before=None):
                wh, wl = hi_tiles(n, nk)
                for k in range(nk):
                    if before:
                        before(k)
                    mm = triple(o, wh[:, k, c * P:(c + 1) * P], wl[:, k, c * P:(c + 1) * P], xh[:, k0 + k, :], xl[:, k0 + k, :],
                                start and k == 0, stop and k == nk - 1)
                return mm

            pe.wait_ge(sem("ident_loaded"), 16)
            pe.wait_ge(sem("vectors_loaded"), 16 * len(ROWS))
            pe.transpose(bank[7][:, 0:NROWS], vec_rows[0:NROWS, :], ident[0:NROWS, 0:NROWS]).then_inc(*mark("vec_turned"))
            for m in range(KD):
                if m >= 4:
                    pe.wait_ge(sem("xT_ready"), m - 3)
                for i in range(NB):
                    pe.wait_ge(sem(f"x_loaded{i // 2}"), 16)
                    mm = pe.transpose(bank[m % 4][:, i * P:(i + 1) * P], x_tok[:, i, m * P:(m + 1) * P], ident[:, :])
                mm.then_inc(sem("x_turned"), 1)
            pe.wait_ge(sem("band_loaded"), 16)
            for c in range(KD):
                if c >= 2:
                    pe.wait_ge(sem("pooled_lo"), c - 1)
                for i in range(NB):
                    pe.wait_ge(sem("h_tok_ready"), i + 1)
                    n = min(BAND, T - i * P)
                    mm = pe.matmul(bank[4 + c % 2][:, i * P:i * P + n], h_tok[:, i, c * P:(c + 1) * P], band[:, c // 2, int(i == 0), 0:n],
                                   start=i == 0, stop=i == NB - 1, skip_group_check=True)
                mm.then_inc(sem("pooled_done"), 1)
            pe.wait_ge(lo_sem, 1)
            pe.wait_ge(sem("xT_ready"), KD)
            wh, wl = hi_tiles(0, 8)
            for m in range(KD):
                g, c = divmod(m, 2)
                if m >= 4:
                    pe.wait_ge(sem("mix_dve"), 3 * (m - 4) + 1)
                for k in range(2):
                    pe.wait_ge(sem("pooled_lo"), 2 * g + k + 1)
                    mm = triple(bank[m % 4][:, :], wh[:, 2 * g + k, c * P:(c + 1) * P], wl[:, 2 * g + k, c * P:(c + 1) * P],
                                pooled_hi[:, 2 * g + k, :], pooled_lo[:, 2 * g + k, :], k == 0, k == 1)
                mm.then_inc(sem("mixed_done"), 1)

            def stat(tag):
                pe.wait_ge(sem(f"{tag}_dve"), 3 * KD)
                pe.wait_ge(sem("ones_set"), 1)
                pe.matmul(bank[7][:, :], ones[:, :], sq_sum[:, :], start=True, stop=True).then_inc(*mark(f"{tag}_stat"))

            def ffn(l):
                tag, to = ffn_from[l], ffn_to[l]
                n0, d0 = FIRST[f"gateup{l}"], FIRST[f"down{l}"]
                gu, gd, dn = sem(f"gateup{l}_done"), sem(f"gated{l}_dve"), sem(f"down{l}_done")

                def turn(i, first):
                    for j in range(2):
                        n = n0 + j
                        pe.wait_ge(lo_sem, i * 2 + (n + 1))
                        for c in range(2):
                            if not first:
                                pe.wait_ge(gd, i * 8 + (4 * c + j + 1 - 8))
                            before = (lambda k: pe.wait_ge(sem(f"{tag}_dve"), 3 * k + 2)) if first and j == c == 0 else None
                            chunk(bank[2 * j + c][:, :], n, 8, c, xg_hi, xg_lo, before=before).then_inc(gu, 1)
                            if first and j == c == 0:
                                stat(tag)

                pe.wait_ge(sem(f"{tag}_dve"), 3 * 7 + 1)
                turn(0, True)
                with pe.Fori(1, 11) as i:
                    turn(i, False)

                def down_turn(q, first):
                    for j, (k0, nk) in enumerate(DOWN_SPLIT):
                        n = d0 + j
                        pe.wait_ge(lo_sem, q * 4 + (n + 1))
                        for c in range(2):
                            if first:
                                pe.wait_ge(gd, max(4 * (k0 + nk), 81 + 4 * c))
                            if not first and j == 0:
                                pe.wait_ge(sem(f"{to}_dve"), q * (6 + 2 * l) + ((3 + l) * c + 1 - (6 + 2 * l)))
                            chunk(bank[c][:, :], n, nk, c, act_hi, act_lo, j == 0, j == 3, k0).then_inc(dn, 1)

                down_turn(0, True)
                with pe.Fori(1, 4) as q:
                    down_turn(q, False)

            def mla():
                n0 = FIRST["mla_down"]
                for idx in range(6):
                    n, c = n0 + idx // 2, idx % 2 if idx >= 2 else 1 - idx
                    pe.wait_ge(lo_sem, n + 1)
                    if idx == 0:
                        pe.wait_ge(sem("ffn0_dve"), 3 * 7 + 1)
                    before = (lambda k: pe.wait_ge(sem("ffn0_dve"), 3 * k + 2)) if idx == 0 else None
                    chunk(bank[idx][:, :], n, 8, c, xg_hi, xg_lo, before=before).then_inc(sem("mla_down_done"), 1)
                    if idx == 0:
                        stat("ffn0")
                    if idx == 2:
                        pe.wait_ge(sem("cq_act"), 1)
                        pe.wait_ge(*at("ffn0_root"))
                        pe.matmul(bank[7][:, :], ones[:, :], squares[:, 0, :], start=True, stop=True).then_inc(*mark("kv_stat"))

                def proj(pr, what):
                    idx = 8 * pr + PROJ.index(what)
                    n = FIRST["heads"] + pr
                    wh, wl = (w[:, n % 2, :].rearrange("p (t c) -> p t c", c=P) for w in (w_hi, w_lo))
                    ps = bank[idx % 2]
                    pe.wait_ge(lo_sem, n + 1)
                    if idx < 2:
                        pe.wait_ge(*(sem("down_q_ready"), 1 + idx))
                    else:
                        pe.wait_ge(sem("proj_ready"), idx - 1)
                    if what in ("qn0", "qn1", "u", "us"):
                        pe.wait_ge(sem("cq_lo"), 3)
                        t0 = {"qn0": 0, "qn1": 3, "u": 6, "us": 9}[what]
                        for k in range(3):
                            mm = triple(ps[:, :], wh[:, t0 + k, :], wl[:, t0 + k, :], cq_hi[:, k, :], cq_lo[:, k, :], k == 0, k == 2)
                    else:
                        pe.wait_ge(*at("ckv_lo"))
                        t0 = 12 + 2 * int(what[-1]) + int(what[0] == "v")
                        if what[0] == "k":
                            mm = triple(ps[:, :], wh[:, t0, :], wl[:, t0, :], ckv_hi[:, :], ckv_lo[:, :], True, True)
                        else:
                            for j in range(NB):
                                tok = slice(j * P, (j + 1) * P)
                                mm = triple(ps[:, tok], ckv_hi[:, tok], ckv_lo[:, tok], wh[:, t0, :], wl[:, t0, :], True, True)
                    mm.then_inc(sem("proj_done"), 1)

                for what in PROJ[:4]:
                    proj(0, what)
                    if what == "qn0":
                        pe.wait_ge(sem("cq_sum"), 2)
                        for i in range(NB):
                            mm = pe.matmul(bank[6][:, 2 * i:2 * i + 2], sq_sum[:, i * P:(i + 1) * P], ones[:, 0:2], start=True, stop=True)
                        mm.then_inc(*mark("rq_stat"))

                def scores(s):
                    h, ii = divmod(s, NB)
                    i = NB - 1 - ii
                    o = bank[2 + s % 3][:, 0:(i + 1) * P]
                    q, k = slice(i * P, (i + 1) * P), slice(0, (i + 1) * P)
                    if s == 0:
                        pe.wait_ge(*at("kr_lo"))
                        pe.wait_ge(sem("masks_ready"), 2)
                    pe.wait_ge(sem("proj_ready"), 8 * (h // 2) + (7 if h % 2 else 4))
                    if s >= 3:
                        pe.wait_ge(sem("att_exp"), s - 2)
                    hs = h % 2
                    triple(o, xg_hi[:, QN + hs, q], xg_lo[:, QN + hs, q], xg_hi[:, KN + hs, k], xg_lo[:, KN + hs, k], True, False)
                    r = slice(64 * hs, 64 * hs + 64)
                    qh, ql = rotary_q(h // 2)
                    triple(o, qh[r, q], ql[r, q], kr_hi[r, k], kr_lo[r, k], False, False)
                    pe.matmul(o[:, i * P:(i + 1) * P], ident_r[:, :], causal[:, :], start=False, stop=True, skip_group_check=True)\
                      .then_inc(sem("att_scored"), 1)

                def turn(s):
                    i = NB - 1 - s % NB
                    pe.wait_ge(sem("att_probs"), s + 1)
                    if s >= 2:
                        pe.wait_ge(sem("att_lo"), s - 1)
                    for j in range(i + 1):
                        mm = pe.transpose(bank[5 + s % 2][:, j * P:(j + 1) * P], probs[:, s % 4, j * P:(j + 1) * P], ident[:, :])
                    mm.then_inc(sem("att_turned"), 1)

                def values(h):
                    pe.wait_ge(sem("att_lo"), NB * (h + 1))
                    pe.wait_ge(sem("proj_ready"), 8 * (h // 2) + (8 if h % 2 else 5))
                    if h:
                        pe.wait_ge(sem("att_out"), h)
                    vh, vl = (x[:, VV + h % 2, :].rearrange("p (j d) -> p j d", d=P) for x in (xg_hi, xg_lo))
                    for j in range(NB):
                        q = slice(j * P, T)
                        mm = triple(bank[7][:, q], vh[:, j, :], vl[:, j, :], pt_hi[:, h % 2, j, q], pt_lo[:, h % 2, j, q], j == 0, j == NB - 1)
                    mm.then_inc(sem("att_out_done"), 1)

                def out(m, k0, k1):
                    wh, wl = hi_tiles(FIRST["mla_o"] + m // 2, 8)
                    c = slice(m % 2 * P, m % 2 * P + P)
                    if k0 == 0:
                        pe.wait_ge(lo_sem, FIRST["mla_o"] + m // 2 + 1)
                        if m < 2:
                            pe.wait_ge(sem("proj_ready"), 32)
                        elif m < 4:
                            pe.wait_ge(sem("att_exp"), NB * HEADS)
                        else:
                            pe.wait_ge(sem("attn_dve"), 3 * (m - 4) + 1)
                    for k in range(k0, k1):
                        pe.wait_ge(sem("att_out"), k + 1)
                        mm = triple(bank[m % 4][:, :], wh[:, k, c], wl[:, k, c], o_hi[:, k, :], o_lo[:, k, :], k == 0, k == HEADS - 1)
                    if k1 == HEADS:
                        mm.then_inc(sem("mla_o_done"), 1)

                for s in range(NB * HEADS + 6):
                    h, ii = divmod(s, NB)
                    if s < NB * HEADS:
                        scores(s)
                    if 0 <= s - 3 < NB * HEADS:
                        turn(s - 3)
                    if s >= 5 and (s - 5) % NB == NB - 1:
                        values((s - 5) // NB)
                    if s < NB * HEADS:
                        for t in after_step(h, ii):
                            proj(*t)
                    if s - NB * HEADS in (0, 1):
                        out(s - NB * HEADS, 0, 6)
                for m in range(KD):
                    out(m, 6 if m < 2 else 0, HEADS)

            def compress(t):
                if t == 21:
                    pe.wait_ge(*at("ffn1_root"))
                    for kv in range(2):
                        pe.wait_ge(sem("cmp_windows"), 4 * kv + 4)
                        for l in range(16):
                            mm = pe.matmul(CMP_BANKS[kv][0:64, 0:64], w1_t[:, kv, l, :], cpe[kv][:, l, :, :].rearrange("p g n -> p (g n)"),
                                           start=l == 0, stop=l == 15)
                        mm.then_inc(sem("cmp_hidden"), 1)
                if t == 22:
                    pe.wait_ge(sem("cmp_act"), 1)
                    pe.wait_ge(*at("pe_kept"))
                    pe.matmul(CMP_BANKS[2][:, 0:64], w2_t[:, 0, :, :].rearrange("p d e -> p (d e)"), h1[:, 0, :], start=True, stop=True)\
                      .then_inc(sem("cmp_done"), 1)
                    pe.wait_ge(sem("cmp_act"), 2)
                    for g in range(2):
                        mm = pe.matmul(CMP_BANKS[3][0:32, g * 64:(g + 1) * 64], h1[:, 1, g * 32:(g + 1) * 32], w2_t[:, 1, 0, :], start=True, stop=True)
                    mm.then_inc(sem("cmp_done"), 1)
                if t == 24:
                    pe.wait_ge(sem("cmp_kv_lo"), 2)
                    pe.wait_ge(sem("nq_lo"), 6)
                    for h in range(6):
                        for i in range(NB):
                            c = ((h % 4) * NB + i) * 32
                            for part in range(2):
                                mm = pe.matmul(CMP_BANKS[h // 4][:, c:c + 32], q_st[:, h, i * P:(i + 1) * P], kc_st[:, part, h // 3, :],
                                               start=part == 0, stop=part == 1, skip_group_check=True)
                    mm.then_inc(*mark("c_scored"))

            def w_in():
                n0 = FIRST["w_in"]
                for t in range(NT):
                    n = n0 + t // 2
                    pe.wait_ge(lo_sem, n + 1)
                    if t == 0:
                        pe.wait_ge(sem("ffn1_dve"), 4 * 7 + 1)
                    if t >= 4:
                        pe.wait_ge(sem("u_free"), t - 3)
                    before = (lambda k: pe.wait_ge(sem("ffn1_dve"), 4 * k + 2)) if t == 0 else None
                    chunk(bank[t % 4][:, :], n, 8, t % 2, xg_hi, xg_lo, before=before).then_inc(sem("u_done"), 1)
                    if t == 0:
                        pe.wait_ge(sem("ffn1_dve"), 4 * KD)
                        pe.matmul(bank[7][:, :], ones[:, :], sq_sum[:, :], start=True, stop=True).then_inc(*mark("ffn1_stat"))
                        pe.matmul(bank[6][:, :], ones[:, :], sq_sum2[:, :], start=True, stop=True).then_inc(*mark("inner_stat"))
                    if t - 1 in VTILES:
                        v = VTILES.index(t - 1)
                        pe.wait_ge(sem("u_free"), t)
                        if v == 1:
                            pe.wait_ge(*at("inner_ready"))
                        for j in range(NB):
                            mm = pe.transpose(bank[5 + v][:, j * P:(j + 1) * P], u_dst(t - 1)[:, j * P:(j + 1) * P], ident[:, :])
                        mm.then_inc(sem("nv_turned"), 1)
                    compress(t)
                    if t == 18:
                        pe.wait_ge(*at("gates_ready"))
                        pe.wait_ge(sem("nv_lo"), 1)
                        for j in range(NB):
                            mm = pe.transpose(bank[5][:, j * 32:(j + 1) * 32], u_dst(17)[0:32, j * P:(j + 1) * P], ident[0:32, 0:32])
                        mm.then_inc(*mark("g_turned"))
                    if t == 19:
                        pe.wait_ge(sem("mix_loaded"), 9 * 16)
                        pe.wait_ge(sem("nv_lo"), 2)
                        for j in range(2):
                            mm = pe.transpose(bank[6][:, j * 32:(j + 1) * 32], pe_rows[:, j, :], ident[0:32, 0:32])
                        mm.then_inc(*mark("pe_turned"))

            def nsa():
                def scores(s):
                    h, b, i = NSTEP[s]
                    o = bank[s % 3][:, 0:(i + 1) * P]
                    if s == 0:
                        pe.wait_ge(sem("nk_lo"), 8)
                        pe.wait_ge(sem("u_free"), NT)
                    if s >= 3:
                        pe.wait_ge(sem("n_exp"), s - 2)
                    for part in range(2):
                        pe.matmul(o, q_st[:, h, i * P:(i + 1) * P], k_st[:, 2 * b + h // 3, part, 0:(i + 1) * P], start=part == 0, stop=False,
                                  skip_group_check=True)
                    pe.matmul(o[:, i * P:(i + 1) * P], ident_r[:, :], causal[:, :], start=False, stop=True, skip_group_check=True)\
                      .then_inc(sem("n_scored"), 1)

                def turn(s):
                    i = NSTEP[s][2]
                    pe.wait_ge(sem("n_probs"), s + 1)
                    if s >= 2:
                        pe.wait_ge(sem("n_lo"), s - 1)
                    for j in range(i + 1):
                        mm = pe.transpose(bank[5 + s % 2][:, j * P:(j + 1) * P], pm[:, s % 4, j * P:(j + 1) * P], ident[:, :])
                    mm.then_inc(sem("n_turned"), 1)

                def values(s):
                    h, b, i = NSTEP[s]
                    o, u, q = n_out(h), s // NB, slice(i * P, T)
                    pe.wait_ge(sem("n_lo"), s + 1)
                    if s % 8 == 0:
                        if h >= 2:
                            pe.wait_ge(sem("n_sum"), h - 1)
                        pe.wait_ge(sem("c_lo"), h + 1)
                        for part, pt in enumerate((ptc_hi, ptc_lo)):
                            pe.matmul(o[:, :], vc_st[:, h // 3, :], pt[:, :], start=part == 0, stop=False, skip_group_check=True)
                    for part, pt in enumerate((pt2_hi, pt2_lo)):
                        mm = pe.matmul(o[:, q], v_st[:, b, h // 3, i, :], pt[:, u % 2, i, q], start=False, stop=s % 8 == 7 and part == 1,
                                       skip_group_check=True)
                    mm.then_inc(sem("n_pv"), 1)

                pe.wait_ge(sem("nv_lo"), 2)
                for s in range(len(NSTEP) + 5):
                    if s < len(NSTEP):
                        scores(s)
                        if s % 8 == 2:
                            h = s // 8
                            pe.wait_ge(*at("cmp_probs"))
                            if h:
                                pe.wait_ge(sem("c_lo"), h)
                            for i in range(NB):
                                c = (h * NB + i) * 32
                                mm = pe.transpose(bank[4][0:32, i * P:(i + 1) * P], p_cmp[:, c:c + 32], ident[:, :])
                            mm.then_inc(sem("c_turned"), 1)
                    if 0 <= s - 3 < len(NSTEP):
                        turn(s - 3)
                    if s >= 5:
                        values(s - 5)

            def dilated():
                kd = k_st[:, :, :, :].rearrange("p a b t -> p (a b) t")
                pe.wait_ge(sem("n_lo"), len(NSTEP))
                for g in range(3):
                    if g == 2:
                        pe.wait_ge(sem("dv_lo"), 1)
                    for j in range(NB):
                        mm = pe.transpose(bank[5 + g % 2][:, j * P:(j + 1) * P], du[:, 6 + g, j * P:(j + 1) * P], ident[:, :])
                    mm.then_inc(sem("dv_turned"), 1)
                pe.wait_ge(sem("n_exp"), len(NSTEP))
                pe.wait_ge(sem("n_sum"), 5)
                pe.wait_ge(*at("dmask_ready"))
                pe.wait_ge(sem("dq_lo"), 6)

                def scores(s):
                    j, i = DSTEP[s]
                    pe.wait_ge(sem("dk_lo"), 6 * j + 6)
                    for g in range(3):
                        x = 3 * s + g
                        kbs = d_keys(g, i)
                        o = bank[x % 5][:, 0:len(kbs) * P]
                        if x >= 5:
                            pe.wait_ge(sem("d_exp"), x - 4)
                        k = slice(kbs[0] * P, (i + 1) * P)
                        for part in range(2):
                            pe.matmul(o, q_st[:, 2 * g + j, i * P:(i + 1) * P], kd[:, 2 * g + part, k], start=part == 0, stop=False, skip_group_check=True)
                        n = len(kbs) - 1
                        for b in range(n):
                            pe.matmul(o[:, b * P:(b + 1) * P], ident_r[:, :], dmask[:, (0, 1, 3)[g], :], start=False, stop=False, skip_group_check=True)
                        diag = causal[:, :] if g == 0 else dmask[:, 2 * g, :]
                        pe.matmul(o[:, n * P:(n + 1) * P], ident_r[:, :], diag, start=False, stop=True, skip_group_check=True).then_inc(sem("d_scored"), 1)

                def turn(s):
                    j, i = DSTEP[s]
                    for g in range(3):
                        x = 3 * s + g
                        pe.wait_ge(sem("d_probs"), x + 1)
                        if x >= 2:
                            pe.wait_ge(sem("d_lo"), x - 1)
                        for n in range(len(d_keys(g, i))):
                            mm = pe.transpose(bank[5 + x % 2][:, n * P:(n + 1) * P], pm[:, x % 4, n * P:(n + 1) * P], ident[:, :])
                        mm.then_inc(sem("d_turned"), 1)

                def values(j):
                    pe.wait_ge(sem("d_lo"), 12 * (j + 1))
                    pe.wait_ge(sem("n_sum"), 6)
                    for g in range(3):
                        if 3 * j + g:
                            pe.wait_ge(sem("d_out"), 3 * j + g)
                        for kb in range(NB):
                            last = min(kb + 1, NB - 1) if g == 0 else NB - 1
                            a0, a1 = d_turned(g, kb, kb), d_turned(g, kb, last)
                            at = (a0[0], a0[1], a0[2], slice(a0[3].start, a1[3].stop))
                            for part, pt in enumerate((pt2_hi, pt2_lo)):
                                mm = pe.matmul(bank[7][:, kb * P:(last + 1) * P], v_st[:, g, j, kb, :], pt[at], start=kb == 0 and part == 0,
                                               stop=kb == NB - 1 and part == 1, skip_group_check=True)
                        mm.then_inc(sem("d_pv"), 1)

                pe.wait_ge(sem("dv_lo"), 3)
                for s in range(len(DSTEP) + 1):
                    if s < len(DSTEP):
                        scores(s)
                    if s:
                        turn(s - 1)
                    if s == 4:
                        values(0)
                values(1)

            def tail():
                n_out, n_pp, n_pg = FIRST["w_out"], FIRST["ple_proj"], FIRST["ple_gate"]
                pe.wait_ge(sem("p_loaded"), 16)
                for j in range(2):
                    for i in range(NB):
                        mm = pe.transpose(bank[5 + j][:, i * P:(i + 1) * P], p_tok[:, i, j * P:(j + 1) * P], ident[:, :])
                    mm.then_inc(sem("p_turned"), 1)
                pe.wait_ge(sem("d_exp"), 24)
                for m in range(KD):
                    n = n_out + m // 2
                    pe.wait_ge(lo_sem, n + 1)
                    if m >= 4:
                        pe.wait_ge(sem("w_out_added"), m - 3)
                    before = (lambda k: pe.wait_ge(sem("y_lo"), k + 1)) if m == 0 else None
                    chunk(bank[m % 4][:, :], n, 8, m % 2, xg_hi, xg_lo, before=before).then_inc(sem("w_out_done"), 1)
                pe.wait_ge(lo_sem, n_pp + 1)
                pe.wait_ge(sem("p_lo_ready"), 2)
                wh, wl = (w[:, n_pp % 2, :].rearrange("p (k c) -> p k c", k=2) for w in (w_hi, w_lo))
                for m in range(KD):
                    if m >= 2:
                        pe.wait_ge(sem("emb_ready"), m - 1)
                    for k in range(2):
                        mm = triple(bank[4 + m % 2][:, :], wh[:, k, m * P:(m + 1) * P], wl[:, k, m * P:(m + 1) * P], p_hi[:, k, :], p_lo[:, k, :], k == 0, k == 1)
                    mm.then_inc(sem("ple_proj_done"), 1)
                for m in range(KD):
                    n = n_pg + m // 2
                    pe.wait_ge(lo_sem, n + 1)
                    pe.wait_ge(sem("w_out_added"), KD) if m == 0 else None
                    if m >= 4:
                        pe.wait_ge(sem("ple_act"), 2 * (m - 4) + 1)
                    before = (lambda k: pe.wait_ge(sem("xs_lo_ready"), k + 1)) if m == 0 else None
                    chunk(bank[m % 4][:, :], n, 8, m % 2, xs_hi, xs_lo, before=before).then_inc(sem("ple_gate_done"), 1)
                pe.wait_ge(sem("ple_dve"), 24)
                pe.wait_ge(sem("emb_ready"), KD)
                for i in range(NB):
                    mm = pe.matmul(bank[4][:, 2 * i:2 * i + 2], sq_sum[:, i * P:(i + 1) * P], ones[:, 0:2], start=True, stop=True)
                mm.then_inc(*mark("fin_stat"))
                pe.wait_ge(sem("fin_gained"), KD)
                pe.wait_ge(sem("ple_act"), 16)
                for o in range(2 * NB):
                    i, half = divmod(o, 2)
                    if o >= 4:
                        pe.wait_ge(sem("out_ready"), o - 3)
                    for m in range(4):
                        mm = pe.transpose(bank[o % 4][:, m * P:(m + 1) * P], emb[:, 4 * half + m, i * P:(i + 1) * P], ident[:, :])
                    mm.then_inc(sem("fin_turned"), 1)

            ffn(0)
            mla()
            ffn(1)
            w_in()
            nsa()
            dilated()
            tail()


def constants():
    import numpy as np
    c = {"c_ident": np.eye(P, dtype=np.float32)}
    s, t = np.arange(P)[:, None], np.arange(BAND)[None, :]
    band = np.zeros((P, len(WINDOWS), 2, BAND), np.float32)
    for g, w in enumerate(WINDOWS):
        inside = (t >= s) & (t - s < w)
        for first in range(2):
            n = np.minimum(t + 1, w) if first else np.full_like(t, w)
            band[:, g, first] = inside / n.astype(np.float32) - (t == s)
    c["c_band"] = band
    lane = np.arange(P)
    inv = 1.0 / (np.float32(10000.0) ** (np.arange(0, ROPE, 2, dtype=np.float32) / np.float32(ROPE)))
    c["c_rope"] = np.stack([inv[lane % 32], np.where(lane % 64 < 32, -1.0, 1.0)], 1).astype(np.float32)
    q, k = np.arange(P)[:, None], np.arange(P)[None, :]
    ok = [k <= q, k >= q]
    for dil in (4, 16):
        same = (q - k) % dil == 0
        ok += [same, same & (k <= q)]
    n = np.arange(32)[None, None, :]
    tok = P * np.arange(NB)[None, :, None] + np.arange(P)[:, None, None]
    c["c_cmask"] = np.where((16 * n + 31 <= tok) & (n < 31), 0.0, NEG).astype(np.float32)
    c["c_cvalid"] = np.ascontiguousarray((tok[:, :, 0] >= 31).astype(np.float32))
    c["c_masks"] = np.ascontiguousarray(np.stack([np.where(m, 0.0, NEG) for m in ok], 1).astype(np.float32))
    return c


def kernel(**inputs):
    import numpy as np
    import concourse.bacc as bacc
    from concourse.bass_utils import run_bass_kernel_spmd

    nc = bacc.Bacc("TRN2", target_bir_lowering=False, num_devices=1)
    arrays, aps = {}, {}
    for name, v in list(inputs.items()) + list(constants().items()):
        v = np.ascontiguousarray(v)
        arrays[f"in_{name}"] = v
        key = name
        aps[key] = nc.dram_tensor(f"in_{name}", v.shape, mybir.dt.from_np(v.dtype), kind="ExternalInput").ap()
    out = nc.dram_tensor("out_0", (1, T, D), F32, kind="ExternalOutput").ap()
    program(nc, aps, out)
    r = run_bass_kernel_spmd(nc, [arrays], core_ids=[0])
    return r.results[0]["out_0"]
```

```python
from contextlib import ExitStack

import concourse.bass as bass
from concourse import mybir

F32 = mybir.dt.float32
F32R = mybir.dt.float32r
I32 = mybir.dt.int32
ALU = mybir.AluOpType
ACT = mybir.ActivationFunctionType
AX = mybir.AxisListType

P = 128
T = 512
NB = T // P
D = 1024
KD = D // P
FF = 2816
KF = FF // P
EPS = 1e-6
WINDOWS = (2, 4, 8, 16)
BAND = P + 16
QL, KVL, ROPE = 384, 128, 64
HEADS = 8
NEG = -1e30
U_COLS = 2048
DOWN_SPLIT = ((0, 6), (6, 6), (12, 5), (17, 5))

ROWS = {}
for _name, _n in (("norm_mix", 16), ("norm_ffn", 16), ("norm_final", 8), ("pool_scale", 8), ("norm_mix_2", 8),
                  ("norm_final_2", 8), ("mla_q_norm", 3), ("mla_kv_norm", 1), ("conv_w_2", 6), ("conv_b_2", 2)):
    ROWS[_name] = (sum(n for _, n in ROWS.values()), _n)
NROWS = sum(n for _, n in ROWS.values())


def weight_units():
    first, n = {}, 0
    for name, count in (("pool", 1), ("gateup0", 22), ("down0", 16), ("mla_down", 3), ("heads", 4), ("mla_o", 4),
                        ("gateup1", 22), ("down1", 16), ("w_in", 17), ("w_out", 4), ("ple_proj", 1), ("ple_gate", 4)):
        first[name] = n
        n += count
    return first, n


FIRST, UNITS = weight_units()


MARKS = {
    "scalar_mark": ("tok_root", "mix_root", "ffn0_root", "kv_root", "kr_hi", "ckv_hi", "rq_root", "attn_root", "ffn1_root", "inner_root",
                    "gates_ready", "cmp_exp", "fin_root"),
    "tensor_mark": ("vec_turned", "ffn0_stat", "kv_stat", "rq_stat", "attn_stat", "ffn1_stat", "inner_stat", "pe_turned",
                    "c_scored", "g_turned", "fin_stat"),
    "vector_mark": ("cols_ready", "gain2_ready", "tok_rstd", "mix_rstd", "rope_ready",
                    "ffn0_rstd", "kr_ready", "rkv_ready", "ckv_ready", "kr_lo", "ckv_lo", "rq_ready",
                    "attn_clear", "attn_rstd", "ffn1_rstd", "inner_ready", "dmask_ready", "kcv_padded", "pe_kept", "gates_kept",
                    "cmp_shifted", "cmp_probs", "fin_clear", "fin_rstd"),
}


def program(nc, a, out):
    ctx = ExitStack()
    with ctx:
        def sb(name, shape, dt=F32, stack=ctx):
            return stack.enter_context(nc.sbuf_tensor(name, shape, dt))

        sems = {}

        def sem(name):
            if name not in sems:
                sems[name] = ctx.enter_context(nc.semaphore(name))
            return sems[name]

        given = {engine: 0 for engine in MARKS}

        def at(name):
            engine = next(e for e, names in MARKS.items() if name in names)
            return sem(engine), MARKS[engine].index(name) + 1

        def mark(name):
            engine = next(e for e, names in MARKS.items() if name in names)
            assert MARKS[engine][given[engine]] == name
            given[engine] += 1
            return sem(engine), 1

        xg_hi = sb("xg_hi", [P, KD, T], F32R)
        xg_lo = sb("xg_lo", [P, KD, T], F32R)
        w_raw = sb("w_raw", [P, 2, U_COLS])
        w_hi = sb("w_hi", [P, 2, U_COLS], F32R)
        w_lo = sb("w_lo", [P, 2, U_COLS], F32R)
        ident = sb("ident", [P, P])
        ones = sb("ones", [P, P])
        cols = sb("cols", [P, NROWS])
        eps_col = sb("eps_col", [P, 4])
        rstd = sb("rstd", [P, T])
        root = sb("root", [P, T])
        squares = sb("squares", [P, 2, T])
        sq_sum = sb("sq_sum", [P, T])
        sq_sum2 = sb("sq_sum2", [P, T])
        ident_r = sb("ident_r", [P, P], F32R)
        causal = sb("causal", [P, P], F32R)
        neg_max = sb("neg_max", [P, 8])
        row_top = sb("row_top", [P, 8])
        row_sum = sb("row_sum", [P, 8])
        row_inv = sb("row_inv", [P, 8])
        rope_col = sb("rope_col", [P, 2])
        gain2 = sb("gain2", [P, KD])
        psum = ctx.enter_context(nc.psum_tensor("psum", [P, 8, T], F32))
        bank = [psum[:, i, :] for i in range(8)]

        def gain(name, m):
            c = ROWS[name][0] + m
            return cols[:, c:c + 1] if isinstance(c, int) else cols[:, bass.ds(c, 1)]

        res_mem = ExitStack()
        xT = sb("xT", [P, KD, T], stack=res_mem)
        x_away = nc.dram_tensor("residual", (P, KD, T), F32).ap()

        rope_mem = ExitStack()
        cos_t = sb("cos_t", [P, T], stack=rope_mem)
        sin_t = sb("sin_t", [P, T], stack=rope_mem)
        pool_mem = ExitStack()
        x_tok = sb("x_tok", [P, NB, D], stack=pool_mem)
        h_tok = sb("h_tok", [P, NB, D], stack=pool_mem)
        pooled_hi = sb("pooled_hi", [P, KD, T], F32R, pool_mem)
        pooled_lo = sb("pooled_lo", [P, KD, T], F32R, pool_mem)
        band = sb("band", [P, len(WINDOWS), 2, BAND], stack=pool_mem)
        tok_stat = sb("tok_stat", [P, 3, NB], stack=pool_mem)
        vec_rows = sb("vec_rows", [P, P], stack=pool_mem)
        pos_i = sb("pos_i", [P, T], I32, pool_mem)
        angle = sb("angle", [P, 3, T], stack=pool_mem)
        masks0 = sb("masks0", [P, P], stack=pool_mem)
        pool_mem.close()

        ffn_mem = ExitStack()
        act_hi = sb("act_hi", [P, KF, T], F32R, ffn_mem)
        act_lo = sb("act_lo", [P, KF, T], F32R, ffn_mem)
        ffn_mem.close()
        gate_z, up_z, gate_s = squares[:, 1, :], squares[:, 0, :], root[:, :]

        mla_mem = ExitStack()
        o_hi = sb("o_hi", [P, HEADS, T], F32R, mla_mem)
        o_lo = sb("o_lo", [P, HEADS, T], F32R, mla_mem)
        pt_hi = sb("pt_hi", [P, 2, NB, T], F32R, mla_mem)
        pt_lo = sb("pt_lo", [P, 2, NB, T], F32R, mla_mem)
        probs = sb("probs", [P, 4, T], stack=mla_mem)
        cq_hi = sb("cq_hi", [P, 3, T], F32R, mla_mem)
        kr_hi = sb("kr_hi", [P, T], F32R, mla_mem)
        kr_lo = sb("kr_lo", [P, T], F32R, mla_mem)
        cq_lo = sb("cq_lo", [P, 3, T], F32R, mla_mem)
        ckv_hi = sb("ckv_hi", [P, T], F32R, mla_mem)
        ckv_lo = sb("ckv_lo", [P, T], F32R, mla_mem)
        rq = sb("rq", [P, 2, 2 * NB], stack=mla_mem)
        mla_mem.close()
        rope_mem.close()

        res_mem.close()
        mix_mem = ExitStack()
        pn_hi = sb("pn_hi", [P, NB, (NB + 1) * P], F32R, mix_mem)
        pn_lo = sb("pn_lo", [P, NB, (NB + 1) * P], F32R, mix_mem)
        ptc_lo = sb("ptc_lo", [96, 2, T], F32R, mix_mem)
        q_st = sb("q_st", [P, 6, T], F32R, mix_mem)
        k_st = sb("k_st", [P, 4, 2, T], F32R, mix_mem)
        v_st = sb("v_st", [P, 3, 2, NB, P], F32R, mix_mem)
        br = sb("br", [P, 8, T], stack=mix_mem)
        du = sb("du", [P, 9, T], stack=mix_mem)
        pm = sb("pm", [P, 4, T], stack=mix_mem)
        dmask = sb("dmask", [P, 2, 5, P], F32R, mix_mem)
        cmask = sb("cmask", [P, NB, 32], stack=mix_mem)
        cvalid = sb("cvalid", [P, NB], stack=mix_mem)
        gates = rstd[:, 0:NB * 32].rearrange("p (i c) -> p i c", c=32)
        kc_st = sb("kc_st", [P, 2, 2, 32], F32R, mix_mem)
        vc_st = sb("vc_st", [96, 2, P], F32R, mix_mem)
        cst = rstd[:, 128:224].rearrange("p (n c) -> p n c", c=24)
        pe_cols = rstd[:, 256:320].rearrange("p (j l) -> p j l", j=2)
        h1 = sq_sum[0:64, 0:64 + 2 * 96]
        mix_mem.close()
        kcv = pm[:, 0:3, :].rearrange("p a t -> p (a t)")[:, 0:2 * 528].rearrange("p (a t) -> p a t", a=2)
        w1_t = du[:, 2:6, :].rearrange("p a t -> p (a t)").rearrange("p (j l c) -> p j l c", j=2, c=64)
        cpe = [x.rearrange("p a t -> p (a t)").rearrange("p (l g n) -> p l g n", l=16, g=2) for x in (du[:, 0:2, :], du[:, 6:8, :])]
        pe_rows = du[0:32, 8, 0:2 * P].rearrange("p (j e) -> p j e", j=2)
        w2_t = du[0:64, 8, 2 * P:4 * P].rearrange("p (j d e) -> p j d e", j=2, d=2)
        ptc_hi = v_st[0:96, 2, :, :, :].rearrange("p g j d -> p g (j d)")
        p_cmp = squares[:, :, :].rearrange("p a t -> p (a t)")[:, 0:768]
        pt2_hi, pt2_lo = (x[:, :, :].rearrange("p (b j) t -> p b j t", b=2) for x in (xg_hi, xg_lo))

        tail_mem = ExitStack()
        xR = sb("xR", [P, KD, T], stack=tail_mem)
        xs_hi = sb("xs_hi", [P, KD, T], F32R, tail_mem)
        xs_lo = sb("xs_lo", [P, KD, T], F32R, tail_mem)
        p_tok = sb("p_tok", [P, NB, 256], stack=tail_mem)
        p_hi = sb("p_hi", [P, 2, T], F32R, tail_mem)
        p_lo = sb("p_lo", [P, 2, T], F32R, tail_mem)
        emb = sb("emb", [P, KD, T], stack=tail_mem)
        out_tok = sb("out_tok", [P, 4, T], stack=tail_mem)
        fin = sb("fin", [P, 3, 2 * NB], stack=tail_mem)
        tail_mem.close()
        down_q = probs
        cos_s, sin_s = probs[:, 0, :], probs[:, 1, :]
        QN, KN, VV, QR = 0, 2, 4, 6

        raw_sem = [sem("weights_loaded0"), sem("weights_loaded1")]
        hi_sem, lo_sem = sem("weights_hi"), sem("weights_lo")
        unit_src = {}

        def raw(n):
            return w_raw[:, n % 2, :]

        def tiles256(ap, k):
            return ap[:, 0:k * 256].rearrange("p (k c) -> p k c", k=k)

        unit_src[0] = [(tiles256(raw(0), 8), a["pool_w"].rearrange("l g (k p) d -> p (l g k) d", p=P))]
        wd = a["mla_w_down"][0].rearrange("(k p) n -> p k n", p=P)
        n = FIRST["mla_down"]
        r0 = QL + KVL
        pieces = ((0, 2 * P, 2 * P), (256, 64, r0), (320, 64, r0), (384, 32, r0 + 32), (416, 32, r0), (448, 32, r0 + 32), (480, 32, r0),
                  (512, 2 * P, 0))
        for j in range(3):
            unit_src[n + j] = [(tiles256(raw(n + j), 8)[:, :, c % 256:c % 256 + w], wd[:, :, s0:s0 + w]) for c, w, s0 in pieces if c // 256 == j]
        wq = a["mla_w_uq"][0].rearrange("(k p) n -> p k n", p=P)
        for pr in range(HEADS // 2):
            n = FIRST["heads"] + pr
            t16 = raw(n).rearrange("p (t c) -> p t c", c=P)
            q0, q1 = 2 * pr * 192, (2 * pr + 1) * 192
            unit_src[n] = [(t16[:, 0:3, :], wq[:, :, q0:q0 + P]), (t16[:, 3:6, :], wq[:, :, q1:q1 + P])]
            for e, q in ((0, q0 + P), (64, q1 + P)):
                unit_src[n] += [(t16[:, 6:9, e:e + 64], wq[:, :, q:q + 64]),
                                (t16[:, 9:12, e:e + 32], wq[:, :, q + 32:q + 64]), (t16[:, 9:12, e + 32:e + 64], wq[:, :, q:q + 32])]
            unit_src[n] += [(raw(n)[:, 12 * P:16 * P], a["mla_w_ukv"][0][:, pr * 512:(pr + 1) * 512])]

        def square_units(stage, w):
            wv = w.rearrange("(k p) n -> p k n", p=P)
            for j in range(4):
                n = FIRST[stage] + j
                unit_src[n] = [(tiles256(raw(n), 8), wv[:, :, j * 256:(j + 1) * 256])]

        square_units("mla_o", a["mla_w_o"][0])
        wi = a["w_in_2"][0].rearrange("(k p) n -> p k n", p=P)
        for j in range(17):
            n = FIRST["w_in"] + j
            c0, w = (256 * j, 256) if j < 9 else (2194 + 256 * (j - 9), 256 if j < 16 else 128)
            unit_src[n] = [(tiles256(raw(n), 8)[:, :, 0:w], wi[:, :, c0:c0 + w])]
        square_units("w_out", a["w_out_2"][0])
        square_units("ple_gate", a["w_ple_gate_2"][0])
        n = FIRST["ple_proj"]
        unit_src[n] = [(raw(n).rearrange("p (k c) -> p k c", k=2), a["w_ple_proj_2"][0].rearrange("(k p) n -> p k n", p=P))]
        loads = [len(unit_src.get(n, [0])) for n in range(UNITS)]

        def loaded(n):
            return 16 * sum(loads[m] for m in range(n % 2, n + 1, 2))

        used = {}

        def hi_tiles(n, k, c=None):
            return tiles256(w_hi[:, n % 2, :], k), tiles256(w_lo[:, n % 2, :], k)

        block = ctx.enter_context(nc.Block())
        used[0] = (sem("mixed_done"), 8)
        for l in range(2):
            for i in range(11):
                used[FIRST[f"gateup{l}"] + 2 * i] = (sem(f"gateup{l}_done"), 4 * i + 2)
                used[FIRST[f"gateup{l}"] + 2 * i + 1] = (sem(f"gateup{l}_done"), 4 * i + 4)
            for d in range(16):
                used[FIRST[f"down{l}"] + d] = (sem(f"down{l}_done"), 2 * d + 2)
        for j in range(3):
            used[FIRST["mla_down"] + j] = (sem("mla_down_done"), 2 * j + 2)
        for pr in range(4):
            used[FIRST["heads"] + pr] = (sem("proj_done"), 8 * pr + 8)
            used[FIRST["mla_o"] + pr] = (sem("mla_o_done"), 2 * pr + 2)
            used[FIRST["w_out"] + pr] = (sem("w_out_done"), 2 * pr + 2)
            used[FIRST["ple_gate"] + pr] = (sem("ple_gate_done"), 2 * pr + 2)
        used[FIRST["ple_proj"]] = (sem("ple_proj_done"), KD)
        for j in range(17):
            used[FIRST["w_in"] + j] = (sem("u_done"), min(2 * j + 2, 33))

        QUERY_TILES = (2, 0, 1)

        FIRST_PROJ = ("kn0", "qn0", "u", "us")

        def after_step(h, ii):
            if h % 2 == 0:
                return tuple((h // 2, what) for what in (("kn1",), (), ("qn1", "v0"), ())[ii])
            return tuple((h // 2 + int(what != "v1"), what) for what in (("kn0",), ("u", "us"), ("qn0", "v1"), ())[ii] if what == "v1" or h + 1 < HEADS)

        PROJ_ORDER = [(0, what) for what in FIRST_PROJ] + [x for h in range(HEADS) for ii in range(NB) for x in after_step(h, ii)]

        def proj_count(pr, *whats):
            return max(PROJ_ORDER.index((pr, what)) for what in whats) + 1

        def rotary_q(pr):
            return xg_hi[:, QR + pr % 2, :], xg_lo[:, QR + pr % 2, :]

        ffn_from = ("mix", "attn")

        def tile_added(l, m):
            return (sem("mix_added"), m + 1) if l == 0 else (sem("attn_dve"), 3 * m + 1)

        def tile_split(l, m):
            return (sem("mix_lo"), m + 1) if l == 0 else (sem("attn_dve"), 3 * m + 2)

        def stat_done(l):
            return (sem("mix_summed"), KD) if l == 0 else at("attn_stat")

        ffn_to = ("ffn0", "ffn1")
        
        def ffn_gain(l, k):
            if l == 1:
                return gain2[:, bass.ds(k, 1)]
            return cols[:, bass.ds(k + (ROWS["norm_mix"][0] + KD), 1)]

        def inner_gain(k):
            return cols[:, bass.ds(k + ROWS["norm_final"][0], 1)]


        KINDS = (["ab"] * 2 + ["ac"] * 2 + ["ah"] * 2 + ["az"] * 2 + ["nq"] * 3 + ["kc", "vc", "ks", "vs", "kw", "vw", "gate"]
                 + ["z"] * 3 + ["dq"] * 3 + ["dk"] * 3 + ["dv"] * 3 + ["z"] * 3)
        NT = len(KINDS)
        SCRATCHED = [t for t in range(NT) if KINDS[t] in ("nq", "ks", "vs", "kw", "vw", "gate")]
        VTILES = [t for t in range(NT) if KINDS[t] in ("vs", "vw")]

        def u_dst(t):
            kind = KINDS[t]
            if t < 8:
                return br[:, t, :]
            if kind in ("kc", "vc"):
                return kcv[:, int(kind == "vc"), 0:T]
            if kind == "z":
                return br[:, t - 18 if t < 21 else 3 + t - 30, :]
            if kind[0] == "d":
                return du[:, t - 21, :]
            return squares[:, SCRATCHED.index(t) % 2, :]

        CMP_BANKS = (bank[7], bank[4])

        W_MAIN = 21

        def u_bank(t):
            return bank[t % 4] if t < W_MAIN else bank[3 + (t - W_MAIN) % 2]

        def pn_cells(x, u, i):
            if u % 2 == 0:
                return x[:, 0:i + 1, (i + 1) * P:(i + 2) * P]
            return bass.AP(x, (NB - 1 - i) * (NB + 1) * P, [list(x[:, 0, 0:1].ap[0]), [(NB + 2) * P, i + 1], [1, P]])

        def c_bank(g):
            return bank[(7, 6)[g]]

        def pn_row(x, u, j):
            return x[:, j, (j + 1) * P:(NB + 1) * P] if u % 2 == 0 else x[:, NB - 1 - j, 0:(NB - j) * P]

        NSTEP = [(h, b, i) for h in range(6) for b in range(2) for i in (3, 2, 1, 0)]
        DSTEP = ((0, 3), (0, 2), (0, 1), (0, 0), (1, 2), (1, 3), (1, 1), (1, 0))
        D_BANK = (0, 3, 0, 2, 3, 0, 3, 0)
        D_FREE = (0, 0, 1, 1, 2, 4, 5, 6)
        D_BLOCKS = {3: [(1, k) for k in range(4)] + [(2, k) for k in range(4)] + [(0, 2), (0, 3)],
                    2: [(1, 0), (1, 1), (1, 2), (0, 1), (2, 0), (2, 1), (2, 2), (0, 2)],
                    1: [(1, 0), (1, 1), (2, 0), (2, 1), (0, 0), (0, 1)],
                    0: [(1, 0), (2, 0), (0, 0)]}
        D_FILLS = {3: ((0, 1, 2, 3), (4, 5, 6, 7), (8, 9)), 2: ((0, 1, 2), (4, 5, 6), (3, 7)), 1: ((0, 1, 2, 3), (4, 5)), 0: ((0, 2, 1),)}
        D_ORDER = (1, 0, 2)
        D_OUT = ((bank[7], bank[5], bank[6]), (bank[7], bank[3], bank[4]))

        def d_cell(g, kb, i):
            return ((g - 1) * NB + kb) * T + i * P if g else (kb // 2 * NB + 2 + kb % 2) * T + (i - kb) * P

        def d_fill(x, i, n):
            at = [d_cell(*D_BLOCKS[i][b], i) for b in D_FILLS[i][n]]
            steps = [[at[1] - at[0], len(at)]]
            if len(at) == 4 and at[2] - at[1] != at[1] - at[0]:
                steps = [[at[2] - at[0], 2], [at[1] - at[0], 2]]
            return bass.AP(x, at[0], [list(x[:, 0, 0:1].ap[0])] + steps + [[1, P]])

        def d_turned(i, n, f):
            ps = bank[5 + f % 2][:, 0:len(D_FILLS[i][n]) * P]
            return ps.rearrange("p (a b q) -> p a b q", a=2, q=P) if i == 1 and n == 0 else ps.rearrange("p (a q) -> p a q", q=P)

        def d_masks(i):
            rows = dmask[:, :, :, :].rearrange("p g m c -> p (g m) c")
            far_and_diagonal = dmask[:, :, 4, :]
            return {3: ((0, 4, rows[:, 0:4, :]), (4, 4, rows[:, 5:9, :]), (8, 2, far_and_diagonal)),
                    2: ((0, 4, rows[:, 1:5, :]), (4, 4, rows[:, 6:10, :])),
                    1: ((0, 4, dmask[:, :, 2:4, :]), (4, 2, far_and_diagonal)),
                    0: ((0, 2, dmask[:, :, 3, :]), (2, 1, rows[:, 9, :]))}[i]

        def d_width(x):
            return len(D_BLOCKS[DSTEP[x][1]]) * P

        def d_scores(x):
            return psum[:, :, :].rearrange("p b t -> p (b t)")[:, D_BANK[x] * T:D_BANK[x] * T + d_width(x)]

        def d_probs(x):
            return (pm[:, :, :] if x % 2 == 0 else du[:, 0:3, :]).rearrange("p a t -> p (a t)")[:, 0:d_width(x)]

        def first_fill(x):
            return sum(len(D_FILLS[i]) for _, i in DSTEP[:x])

        def d_keys(j, g):
            if j == 0:
                n = (0, 2, 1)[g]
                return k_st[:, n, 0, :], k_st[:, n, 1, :]
            return tuple(x[:, :, :].rearrange("p a t -> p (a t)")[:, g * T:(g + 1) * T] for x in (pn_hi, pn_lo))

        @block.sync
        def _(sp):
            def load(n):
                if n >= 2:
                    sp.wait_ge(lo_sem, n - 1)
                for dst, src in unit_src[n]:
                    sp.dma_start(dst, src).then_inc(raw_sem[n % 2], 16)

            sp.dma_start(x_tok[:, 0:2, :], a["x"][0].rearrange("(i p) f -> p i f", p=P)[:, 0:2]).then_inc(sem("x_loaded0"), 16)
            sp.dma_start(x_tok[:, 2:4, :], a["x"][0].rearrange("(i p) f -> p i f", p=P)[:, 2:4]).then_inc(sem("x_loaded1"), 16)
            sp.dma_start(ident[:, :], a["c_ident"]).then_inc(sem("ident_loaded"), 16)
            for name, (r, n) in ROWS.items():
                v = a[name]
                flat = v if len(v.shape) == 1 else v.rearrange("a b -> (a b)") if len(v.shape) == 2 else v.rearrange("a b c -> (a b c)")
                sp.dma_start(vec_rows[r:r + n, :], flat.rearrange("(r p) -> r p", p=P)).then_inc(sem("vectors_loaded"), 16)
            sp.dma_start(band[:, :, :, :], a["c_band"]).then_inc(sem("band_loaded"), 16)
            sp.dma_start(pos_i[:, :], a["positions"][0:1, :].to_broadcast([P, T])).then_inc(sem("pos_loaded"), 16)
            sp.dma_start(rope_col[:, :], a["c_rope"]).then_inc(sem("pos_loaded"), 16)
            sp.dma_start(masks0[:, :], a["c_masks"][:, 0, :]).then_inc(sem("mask_loaded"), 16)
            load(0)
            for l in range(2):
                if l == 1:
                    for n in range(FIRST["mla_down"], FIRST["gateup1"]):
                        load(n)
                up, gate, down = (a[f"ffn_w_{x}"][l] for x in ("up", "gate", "down"))
                gv, uv = (w.rearrange("(k p) n -> p k n", p=P) for w in (gate, up))
                dv = down.rearrange("(k p) n -> p k n", p=P)
                n0 = FIRST[f"gateup{l}"]
                with sp.Fori(0, 11) as i:
                    for j, src in enumerate((gv, uv)):
                        n = n0 + j
                        sp.wait_ge(lo_sem, i * 2 + (n - 1))
                        sp.dma_start(tiles256(raw(n), 8), src[:, :, bass.ds(i * 256, 256)]).then_inc(raw_sem[n % 2], 16)
                n0 = FIRST[f"down{l}"]
                with sp.Fori(0, 4) as q:
                    for j, (k0, nk) in enumerate(DOWN_SPLIT):
                        n = n0 + j
                        sp.wait_ge(lo_sem, q * 4 + (n - 1))
                        sp.dma_start(tiles256(raw(n), nk), dv[:, k0:k0 + nk, bass.ds(q * 256, 256)]).then_inc(raw_sem[n % 2], 16)

            n_mix, n_out = FIRST["w_in"], FIRST["w_out"]
            for n in range(n_mix, n_mix + 2):
                load(n)
            sp.wait_ge(sem("down1_done"), 32)
            for src, dst in ((a["c_masks"][:, 1:7, :], du[:, 0:2, :].rearrange("p a t -> p (a t)")[:, 0:6 * P].rearrange("p (m c) -> p m c", c=P)),
                             (a["c_cmask"], cmask[:, :, :]), (a["c_cvalid"], cvalid[:, :]),
                             (a["cmp_pe_2"][0].rearrange("j l e -> l j e"), pe_rows[:, :, 0:64]),
                             (a["cmp_pe_2"][0].rearrange("j l e -> l j e"), pe_rows[:, :, 64:128]),
                             (a["cmp_w2_2"][0].rearrange("j a e -> a j e"), w2_t[:, :, 0, :]),
                             (a["cmp_w2_2"][0].rearrange("j a e -> a j e"), w2_t[:, :, 1, :]),
                             *((a["cmp_w1_2"][0, j].rearrange("(l p) c -> p l c", p=P), w1_t[:, j, :, :]) for j in range(2))):
                sp.dma_start(dst, src).then_inc(sem("mix_loaded"), 16)
            for n in range(n_mix + 2, n_out + 2):
                load(n)
                if n == n_mix + 8:
                    sp.wait_ge(sem("x_normed"), KD)
                    sp.dma_start(x_away, xT[:, :, :]).then_inc(sem("x_stored"), 16)
            sp.wait_ge(sem("x_stored"), 16)
            sp.wait_ge(sem("d_scored"), len(DSTEP))
            sp.dma_start(xR[:, :, :], x_away).then_inc(sem("x_back"), 16)
            sp.wait_ge(sem("d_gated"), 3)
            sp.dma_start(p_tok[:, :, :], a["p_2"][0, 0].rearrange("(i p) f -> p i f", p=P)).then_inc(sem("p_loaded"), 16)
            for n in range(n_out + 2, UNITS):
                load(n)
            ov = out[0].rearrange("(i p) f -> p i f", p=P)
            for o in range(2 * NB):
                i, half = divmod(o, 2)
                sp.wait_ge(sem("out_ready"), o + 1)
                sp.dma_start(ov[:, i, half * T:(half + 1) * T], out_tok[:, o % 4, :]).then_inc(sem(f"out_stored{o % 4}"), 16)
            for o in range(4):
                sp.wait_ge(sem(f"out_stored{o}"), 32)

        @block.gpsimd
        def _(pool):
            pool.memset(ones[:, :], 1.0).then_inc(sem("ones_set"), 1)
            pool.memset(eps_col[:, 0:1], EPS).then_inc(sem("eps_set"), 1)
            pool.memset(eps_col[:, 1:2], EPS * (128 + ROPE)).then_inc(sem("eps_set"), 1)
            MAGIC, TWO_PI = 1.5 * 2.0 ** 23, 6.283185307179586
            parts = (6.28125, 0.001934051513671875, 1.2556659146019695e-06)
            ang = sem("angle_step")
            pool.wait_ge(sem("pos_loaded"), 32)
            pool.tensor_copy(angle[:, 0, :], pos_i[:, :]).then_inc(ang, 1)
            pool.wait_ge(ang, 1)
            pool.tensor_scalar(angle[:, 0, :], angle[:, 0, :], rope_col[:, 0:1], None, ALU.mult).then_inc(ang, 1)
            pool.wait_ge(ang, 2)
            pool.tensor_scalar(angle[:, 1, :], angle[:, 0, :], 1.0 / TWO_PI, MAGIC, ALU.mult, ALU.add).then_inc(ang, 1)
            pool.wait_ge(ang, 3)
            pool.tensor_scalar(angle[:, 1, :], angle[:, 1, :], MAGIC, None, ALU.subtract).then_inc(ang, 1)
            for n, c in enumerate(parts):
                pool.wait_ge(ang, 4 + 2 * n)
                pool.tensor_scalar(angle[:, 2, :], angle[:, 1, :], c, None, ALU.mult).then_inc(ang, 1)
                pool.wait_ge(ang, 5 + 2 * n)
                pool.tensor_tensor(angle[:, 0, :], angle[:, 0, :], angle[:, 2, :], ALU.subtract).then_inc(ang, 1)
            pool.wait_ge(ang, 10)
            pool.tensor_scalar(angle[:, 0, :], angle[:, 0, :], 3.1415925, -3.1415925, ALU.min, ALU.max).then_inc(ang, 1)
            pool.wait_ge(ang, 11)
            pool.tensor_scalar(angle[:, 1, :], angle[:, 0, :], TWO_PI / 4, -TWO_PI, ALU.is_gt, ALU.mult).then_inc(ang, 1)
            pool.tensor_scalar(angle[:, 2, :], angle[:, 0, :], TWO_PI / 4, None, ALU.add).then_inc(ang, 1)
            pool.wait_ge(ang, 13)
            pool.tensor_tensor(angle[:, 1, :], angle[:, 1, :], angle[:, 2, :], ALU.add).then_inc(ang, 1)
            pool.wait_ge(ang, 14)
            pool.tensor_scalar(angle[:, 1, :], angle[:, 1, :], 3.1415925, -3.1415925, ALU.min, ALU.max).then_inc(ang, 1)

        @block.scalar
        def _(act):
            def split_hi(n, waits=()):
                act.wait_ge(raw_sem[n % 2], loaded(n))
                if n >= 2:
                    act.wait_ge(*used[n - 2])
                act.activation(w_hi[:, n % 2, :], raw(n), ACT.Copy).then_inc(hi_sem, 1)

            def chain(tag, k, m, gcol, extra=None):
                act.wait_ge(sem(f"{tag}_dve"), k * 3 + 1)
                act.activation(xg_hi[:, m, :], xT[:, m, :], ACT.Copy, scale=gcol).then_inc(sem(f"{tag}_act"), 1)
                act.activation(squares[:, k % 2 if isinstance(k, int) else 0, :], xT[:, m, :], ACT.Square).then_inc(sem(f"{tag}_act"), 1)

            act.preload_act_table(ACT.Sqrt)
            for i in range(NB):
                act.wait_ge(sem(f"x_loaded{i // 2}"), 16)
                act.activation(h_tok[:, i, :], x_tok[:, i, :], ACT.Square, accum_out=tok_stat[:, 0, i:i + 1]).then_inc(sem("tok_squares"), 1)
            act.wait_ge(sem("eps_set"), 2)
            act.wait_ge(sem("tok_squares"), NB)
            act.activation(tok_stat[:, 1, :], tok_stat[:, 0, :], ACT.Sqrt, scale=1.0 / D, bias=eps_col[:, 0:1]).then_inc(*mark("tok_root"))
            for m in range(KD):
                act.wait_ge(sem("x_turned"), m + 1)
                act.activation(xT[:, m, :], bank[m % 4][:, :], ACT.Copy).then_inc(sem("xT_ready"), 1)
            split_hi(0)
            act.wait_ge(*at("cols_ready"))
            for c in range(KD):
                act.wait_ge(sem("pooled_done"), c + 1)
                act.activation(pooled_hi[:, c, :], bank[4 + c % 4][:, :], ACT.Copy, scale=gain("norm_mix", c)).then_inc(sem("pooled_hi"), 1)
            split_hi(1)
            for m in range(KD):
                act.wait_ge(sem("mix_added"), m + 1)
                act.activation(xg_hi[:, m, :], xT[:, m, :], ACT.Copy, scale=gain("norm_ffn", m)).then_inc(sem("mix_act"), 1)
                if m >= 2:
                    act.wait_ge(sem("mix_summed"), m - 1)
                act.activation(squares[:, m % 2, :], xT[:, m, :], ACT.Square).then_inc(sem("mix_act"), 1)

            def ffn(l):
                tag, to = ffn_from[l], ffn_to[l]
                n0, d0 = FIRST[f"gateup{l}"], FIRST[f"down{l}"]
                gu, gd, ga = sem(f"gateup{l}_done"), sem(f"gated{l}_dve"), sem(f"gated{l}_act")
                split_hi(n0 + 1)
                act.wait_ge(*stat_done(l))
                act.activation(root[:, :], bank[7][:, :], ACT.Sqrt, scale=1.0 / D, bias=eps_col[:, 0:1]).then_inc(*mark(f"{tag}_root"))
                if l == 0:
                    act.preload_act_table(ACT.Sin)
                    act.wait_ge(sem("angle_step"), 15)
                    act.activation(sin_t[:, :], angle[:, 0, :], ACT.Sin).then_inc(sem("sin_done"), 1)
                    act.activation(cos_t[:, :], angle[:, 1, :], ACT.Sin).then_inc(sem("sin_done"), 1)
                act.preload_act_table(ACT.Silu)

                def gateup_turn(i, first):
                    for j in (2,) if first else (1, 2):
                        n = n0 + j
                        act.wait_ge(raw_sem[n % 2], i * 16 + loaded(n))
                        act.wait_ge(gu, i * 4 + 2 * (j - 1))
                        act.activation(w_hi[:, n % 2, :], raw(n), ACT.Copy).then_inc(hi_sem, 1)
                    for c in range(2):
                        act.wait_ge(gd, i * 8 + 4 * c + 1)
                        act.activation(gate_s, gate_z, ACT.Silu).then_inc(ga, 1)
                        act.wait_ge(gd, i * 8 + 4 * c + 3)
                        act.activation(act_hi[:, bass.ds(i * 2 + c, 1), :].rearrange("p a t -> p (a t)"), gate_z, ACT.Copy).then_inc(ga, 1)
                gateup_turn(0, True)
                with act.Fori(1, 11) as i:
                    gateup_turn(i, False)
                dn = sem(f"down{l}_done")

                def down_turn(q, first):
                    for j in range(4):
                        n = d0 + j + 1
                        act.wait_ge(raw_sem[n % 2], q * 32 + loaded(n))
                        if first and j == 0:
                            act.wait_ge(gu, 44)
                        else:
                            act.wait_ge(dn, q * 8 + 2 * j)
                        act.activation(w_hi[:, n % 2, :], raw(n), ACT.Copy).then_inc(hi_sem, 1)
                    for c in range(2):
                        k = q * 2 + c
                        act.wait_ge(sem(f"{to}_dve"), q * (6 + 2 * l) + (3 + l) * c + 1)
                        xt = xT[:, bass.ds(k, 1), :].rearrange("p a t -> p (a t)")
                        act.activation(xg_hi[:, bass.ds(k, 1), :].rearrange("p a t -> p (a t)"), xt, ACT.Copy,
                                       scale=ffn_gain(l, k)).then_inc(sem(f"{to}_act"), 1)
                        act.activation(squares[:, c, :], xt, ACT.Square).then_inc(sem(f"{to}_act"), 1)
                        if l == 1:
                            act.activation(root[:, :], xt, ACT.Square, scale=inner_gain(k)).then_inc(sem(f"{to}_act"), 1)

                down_turn(0, True)
                with act.Fori(1, 4) as q:
                    down_turn(q, False)

            def mla():
                n0 = FIRST["mla_down"]
                s2 = 1.0 / (128 + ROPE)
                split_hi(n0 + 1)
                act.wait_ge(*at("ffn0_stat"))
                act.activation(root[:, :], bank[7][:, :], ACT.Sqrt, scale=1.0 / D, bias=eps_col[:, 0:1]).then_inc(*mark("ffn0_root"))
                def proj(pr, what):
                    idx = PROJ_ORDER.index((pr, what))
                    h = 2 * pr + int(what[-1] == "1")
                    if what == "u":
                        return
                    if what == "us":
                        act.wait_ge(sem("proj_tmp"), pr + 1)
                        src = squares[:, 0, :]
                    else:
                        act.wait_ge(sem("proj_done"), idx + 1)
                        src = bank[idx % 2][:, :]
                    dst = rotary_q(pr)[0] if what == "us" else xg_hi[:, {"q": QN, "k": KN, "v": VV}[what[0]] + h % 2, :]
                    if what == "us" and pr >= 2:
                        act.wait_ge(sem("att_scored"), 8 * (pr - 1))
                    elif what[0] in "qk" and h >= 2:
                        act.wait_ge(sem("att_scored"), 4 * (h - 1))
                    elif what[0] == "v" and h >= 2:
                        act.wait_ge(sem("att_out_done"), h - 1)
                    act.activation(dst, src, ACT.Copy).then_inc(sem("proj_hi"), 1)

                act.wait_ge(sem("down_q_ready"), 1)
                act.activation(squares[:, 0, :], down_q[:, 3, :], ACT.Square).then_inc(sem("cq_act"), 1)

                def queries(n):
                    t = QUERY_TILES[n]
                    act.wait_ge(sem("down_q_ready"), n + 2)
                    act.activation(cq_hi[:, t, :], down_q[:, t, :], ACT.Copy, scale=gain("mla_q_norm", t)).then_inc(sem("cq_act"), 1)
                    act.activation(squares[:, n - 1, :] if n else sq_sum[:, :], down_q[:, t, :], ACT.Square).then_inc(sem("cq_act"), 1)

                queries(0)
                split_hi(n0 + 2)
                act.wait_ge(*at("kv_stat"))
                act.activation(squares[:, 1, :], bank[7][:, :], ACT.Sqrt, scale=1.0 / KVL, bias=eps_col[:, 0:1]).then_inc(*mark("kv_root"))
                act.wait_ge(*at("kr_ready"))
                act.activation(kr_hi[:, :], root[:, :], ACT.Copy).then_inc(*mark("kr_hi"))
                act.wait_ge(*at("ckv_ready"))
                act.activation(ckv_hi[:, :], down_q[:, 3, :], ACT.Copy).then_inc(*mark("ckv_hi"))
                split_hi(n0 + 3)
                queries(1)
                queries(2)
                proj(0, "kn0")
                act.wait_ge(*at("rq_stat"))
                act.activation(rq[:, 0, :], bank[6][:, 0:2 * NB], ACT.Sqrt, scale=1.0 / (QL * s2), bias=eps_col[:, 1:2]).then_inc(*mark("rq_root"))
                act.preload_act_table(ACT.Exp)

                for what in FIRST_PROJ[1:]:
                    proj(0, what)

                def softmax_exp(s):
                    act.wait_ge(sem("att_max"), s + 1)
                    if s >= 4:
                        act.wait_ge(sem("att_turned"), s - 3)
                    w = (NB - s % NB) * P
                    i = NB - 1 - s % NB
                    act.activation(probs[:, s % 4, 0:w], bank[2 + s % 3][:, 0:w], ACT.Exp, bias=neg_max[:, s % 8:s % 8 + 1],
                                   scale=rq[:, 1, 2 * i:2 * i + 1],
                                   accum_out=row_sum[:, s % 8:s % 8 + 1]).then_inc(sem("att_exp"), 1)

                def turned_hi(s):
                    h, ii = divmod(s, NB)
                    i = NB - 1 - ii
                    act.wait_ge(sem("att_turned"), s + 1)
                    if h >= 2:
                        act.wait_ge(sem("att_out_done"), h - 1)
                    act.activation(pt_hi[:, h % 2, 0:i + 1, i * P:(i + 1) * P], bank[5 + s % 2][:, 0:(i + 1) * P].rearrange("p (j q) -> p j q", q=P),
                                   ACT.Copy).then_inc(sem("att_hi"), 1)

                def head_out(h):
                    act.wait_ge(sem("att_out_done"), h + 1)
                    act.activation(o_hi[:, h, :], bank[7][:, :], ACT.Copy).then_inc(sem("att_out_hi"), 1)

                for s in range(NB * HEADS + 7):
                    h, ii = divmod(s, NB)
                    if s < NB * HEADS:
                        softmax_exp(s)
                    if 0 <= s - 3 < NB * HEADS:
                        turned_hi(s - 3)
                    if s < NB * HEADS:
                        for t in after_step(h, ii):
                            proj(*t)
                        if h % 2 == 0 and ii == 0:
                            split_hi(FIRST["heads"] + 1 + h // 2)
                    if s >= 6 and (s - 6) % NB == NB - 1:
                        head_out((s - 6) // NB)
                act.preload_act_table(ACT.Sqrt)
                for u in range(1, 5):
                    split_hi(FIRST["mla_o"] + u)
                    for m in (2 * u - 2, 2 * u - 1):
                        chain("attn", m, m, gain("norm_ffn", 8 + m))

            def compress(t):
                if t == 16:
                    act.wait_ge(sem("cmp_hidden"), 1)
                    act.activation(h1[:, 0:64], CMP_BANKS[0][0:64, 0:64], ACT.Silu).then_inc(sem("cmp_act"), 1)
                    act.wait_ge(sem("cmp_hidden"), 2)
                    act.activation(h1[:, 64:256].rearrange("p (g r n) -> p g r n", g=2, r=3),
                                   CMP_BANKS[1][0:64, 0:64].rearrange("p (g o n) -> p g o n", g=2, o=1).to_broadcast([64, 2, 3, 32]),
                                   ACT.Silu).then_inc(sem("cmp_act"), 1)
                if t == 17:
                    act.wait_ge(sem("cmp_done"), 1)
                    act.activation(kc_st[:, 0, :, :].rearrange("p g n -> p (g n)"), CMP_BANKS[0][:, 0:64], ACT.Copy).then_inc(sem("cmp_kv_hi"), 1)
                    act.wait_ge(sem("cmp_done"), 2)
                    act.activation(vc_st[:, :, 0:64], CMP_BANKS[1][0:96, 0:P].rearrange("n (g e) -> n g e", g=2), ACT.Copy).then_inc(sem("cmp_kv_hi"), 1)
                if t == 20:
                    act.preload_act_table(ACT.Exp)
                    act.wait_ge(*at("cmp_shifted"))
                    act.activation(p_cmp, p_cmp, ACT.Exp).then_inc(*mark("cmp_exp"))

            def w_in():
                n0 = FIRST["w_in"]
                split_hi(n0 + 1)
                act.wait_ge(*at("ffn1_stat"))
                act.activation(root[:, :], bank[7][:, :], ACT.Sqrt, scale=1.0 / D, bias=eps_col[:, 0:1]).then_inc(*mark("ffn1_root"))
                act.wait_ge(*at("inner_ready"))
                act.activation(root[:, :], sq_sum[:, :], ACT.Sqrt, scale=1.0 / D, bias=eps_col[:, 0:1]).then_inc(*mark("inner_root"))
                act.preload_act_table(ACT.Silu)
                for t in range(W_MAIN):
                    kind = KINDS[t]
                    ready = (sem("u_free"), t + 1)
                    if kind == "az":
                        act.wait_ge(*ready)
                        act.activation(br[:, t, :], br[:, t, :], ACT.Silu).then_inc(sem("conv_gate"), 1)
                    elif kind == "z":
                        act.wait_ge(*ready)
                        act.activation(u_dst(t), u_dst(t), ACT.Silu).then_inc(sem("z_gate"), 1)
                    elif kind == "nq":
                        act.wait_ge(*ready)
                        for e in range(2):
                            r = slice(64 * e, 64 * e + 64)
                            act.activation(q_st[r, 2 * (t - 8) + e, :], u_dst(t)[r, :], ACT.Copy, scale=0.125).then_inc(sem("nq_hi"), 1)
                    elif kind in ("ks", "kw"):
                        act.wait_ge(*ready)
                        for g in range(2):
                            for e in range(2):
                                act.activation(k_st[64 * e:64 * e + 64, 2 * int(kind == "kw") + g, 0, :], u_dst(t)[64 * g:64 * g + 64, :], ACT.Copy)\
                                   .then_inc(sem("nk_hi"), 1)
                    elif kind == "gate":
                        act.preload_act_table(ACT.Sigmoid)
                        act.wait_ge(*ready)
                        act.activation(u_dst(t)[0:32, :], u_dst(t)[0:32, :], ACT.Sigmoid).then_inc(*mark("gates_ready"))
                        act.preload_act_table(ACT.Silu)
                    if t - 2 in VTILES:
                        v = VTILES.index(t - 2)
                        act.wait_ge(sem("nv_turned"), v + 1)
                        act.activation(v_st[:, v, :, :, 0:64], bank[5 + v][:, :].rearrange("p (j h d) -> p h j d", h=2, d=64), ACT.Copy)\
                           .then_inc(sem("nv_hi"), 1)
                    compress(t)
                    if t % 2 == 1:
                        split_hi(n0 + t // 2 + 2)

            def keys_hi(j, g):
                for e in range(2):
                    act.activation(d_keys(j, g)[0][64 * e:64 * e + 64, :], du[64 * j:64 * j + 64, 3 + g, :], ACT.Copy).then_inc(sem("dk_hi"), 1)

            def nsa():
                def softmax_exp(s):
                    h, b, i = NSTEP[s]
                    act.wait_ge(sem("n_max"), s + 1)
                    if s >= 4:
                        act.wait_ge(sem("n_turned"), s - 3)
                    w = (i + 1) * P
                    act.activation(pm[:, s % 4, 0:w], bank[s % 3][:, 0:w], ACT.Exp, bias=neg_max[:, s % 8:s % 8 + 1],
                                   accum_out=row_sum[:, s % 8:s % 8 + 1]).then_inc(sem("n_exp"), 1)

                def dilated_query(x):
                    r = slice(64 * (x % 2), 64 * (x % 2) + 64)
                    act.wait_ge(sem("n_scored"), 8 * x + 8)
                    act.wait_ge(sem("u_free"), KINDS.index("dq") + x // 2 + 1)
                    act.activation(q_st[r, x, :], du[r, x // 2, :], ACT.Copy, scale=0.125).then_inc(sem("dq_hi"), 1)

                def turned_hi(s):
                    i, u = NSTEP[s][2], s // NB
                    act.wait_ge(sem("n_turned"), s + 1)
                    if s == 0:
                        act.wait_ge(sem("x_stored"), 16)
                    if u >= 2:
                        act.wait_ge(sem("n_pv"), NB * (u - 1))
                    act.activation(pn_cells(pn_hi, u, i), bank[5 + s % 2][:, 0:(i + 1) * P].rearrange("p (j q) -> p j q", q=P),
                                   ACT.Copy).then_inc(sem("n_hi"), 1)

                for s in range(len(NSTEP) + 7):
                    if s >= 6 and (s - 6) % 8 == 7:
                        h = (s - 6) // 8
                        act.wait_ge(sem("n_pv"), 8 * h + 8)
                        if h:
                            act.wait_ge(sem("n_sum"), h)
                        act.activation(root[0:64, :], bank[7][64:128, :], ACT.Copy).then_inc(sem("n_out_act"), 1)
                    if s < len(NSTEP):
                        softmax_exp(s)
                    if 0 <= s - 3 < len(NSTEP):
                        turned_hi(s - 3)
                    if s == 3:
                        for g in range(2):
                            act.wait_ge(sem("c_turned"), g + 1)
                            act.activation(ptc_hi[:, g, :], c_bank(g)[0:96, :], ACT.Copy).then_inc(sem("c_hi"), 1)
                    w, step = divmod(s, 4)
                    if step == 2 and w % 2 == 1 and w <= NT - W_MAIN:
                        split_hi(FIRST["w_in"] + (W_MAIN - 1 + w) // 2 + 2)
                    if s >= 13 and s % 8 == 5:
                        dilated_query((s - 13) // 8)
                    if s in (30, 34, 46):
                        g = (30, 34, 46).index(s)
                        act.wait_ge(sem("n_scored"), (24, 24, 44)[g])
                        act.wait_ge(sem("u_free"), KINDS.index("dk") + g + 1)
                        keys_hi(0, g)

            def dilated():
                def softmax_exp(x):
                    act.wait_ge(sem("d_max"), x + 1)
                    if x >= 2:
                        act.wait_ge(sem("d_turned"), first_fill(x - 1))
                    c = slice(x % 8, x % 8 + 1)
                    act.activation(d_probs(x), d_scores(x), ACT.Exp, bias=neg_max[:, c], accum_out=row_sum[:, c]).then_inc(sem("d_exp"), 1)

                def turned_hi(x):
                    j, i = DSTEP[x]
                    for n in range(len(D_FILLS[i])):
                        f = first_fill(x) + n
                        act.wait_ge(sem("d_turned"), f + 1)
                        if j:
                            act.wait_ge(sem("d_pv"), 3)
                        act.activation(d_fill(xg_hi, i, n), d_turned(i, n, f), ACT.Copy).then_inc(sem("d_hi"), 1)

                def out(n):
                    j, g = n // 3, D_ORDER[n % 3]
                    act.wait_ge(sem("d_pv"), n + 1)
                    if n >= 2:
                        act.wait_ge(sem("d_out"), n - 1)
                    act.activation((root, rstd)[n % 2][0:64, :], D_OUT[j][g][64:128, :], ACT.Copy).then_inc(sem("d_out_act"), 1)

                def v_hi(g):
                    act.wait_ge(sem("dv_turned"), g + 1)
                    act.activation(v_st[:, g, :, :, 0:64], bank[5 + g % 2][:, :].rearrange("p (j h d) -> p h j d", h=2, d=64), ACT.Copy)\
                       .then_inc(sem("dv_hi"), 1)

                def y_hi(f):
                    act.activation(xg_hi[:, f, :], br[:, (f + 6) % 8, :], ACT.Copy).then_inc(sem("y_hi"), 1)

                v_hi(0)
                v_hi(1)
                for x in range(len(DSTEP) + 2):
                    if x < len(DSTEP):
                        softmax_exp(x)
                    if x == 1:
                        v_hi(2)
                    if x == 5:
                        for n in range(3):
                            out(n)
                    if 0 <= x - 1 < len(DSTEP):
                        turned_hi(x - 1)
                    if x == 0:
                        act.wait_ge(sem("n_pv"), len(NSTEP))
                        keys_hi(1, 0)
                    if x == 1:
                        keys_hi(1, 1)
                        keys_hi(1, 2)
                act.preload_act_table(ACT.Silu)

                def gate(n):
                    t = NT - 3 + D_ORDER[n]
                    act.wait_ge(sem("u_free"), t + 1)
                    act.activation(u_dst(t), u_dst(t), ACT.Silu).then_inc(sem("z_gate"), 1)

                act.wait_ge(sem("conv_step"), 14)
                out(3)
                for f in (0, 1):
                    y_hi(f)
                gate(0)
                act.wait_ge(sem("n_sum"), 6)
                out(4)
                for f in (2, 3):
                    y_hi(f)
                gate(1)
                gate(2)
                out(5)
                y_hi(4)
                for f in (5, 6, 7):
                    act.wait_ge(sem("d_gated"), (2, 1, 3)[f - 5])
                    y_hi(f)

            def tail():
                n_out, n_pp, n_pg = FIRST["w_out"], FIRST["ple_proj"], FIRST["ple_gate"]
                act.preload_act_table(ACT.Sigmoid)
                for m in range(KD):
                    if m % 2 == 0:
                        split_hi(n_out + m // 2 + 1)
                    act.wait_ge(sem("w_out_added"), m + 1)
                    act.activation(xs_hi[:, m, :], xR[:, m, :], ACT.Copy).then_inc(sem("xs_hi_ready"), 1)
                    if m in (4, 5):
                        act.wait_ge(sem("p_turned"), m - 3)
                        act.activation(p_hi[:, m - 4, :], bank[m + 1][:, :], ACT.Copy).then_inc(sem("p_hi_ready"), 1)
                split_hi(n_pg)
                for m in range(KD):
                    if m % 2 == 0 and m < 6:
                        split_hi(n_pg + m // 2 + 1)
                    act.wait_ge(sem("ple_gate_done"), m + 1)
                    if m >= 2:
                        act.wait_ge(sem("ple_dve"), 3 * (m - 2) + 1)
                    act.activation((root, rstd)[m % 2][:, :], bank[m % 4][:, :], ACT.Sigmoid).then_inc(sem("ple_act"), 1)
                    act.wait_ge(sem("ple_dve"), 3 * m + 2)
                    act.activation(squares[:, m % 2, :], xR[:, m, :], ACT.Square).then_inc(sem("ple_act"), 1)
                    act.activation(emb[:, m, :], xR[:, m, :], ACT.Copy, scale=gain("norm_final_2", m)).then_inc(sem("fin_gained"), 1)
                act.preload_act_table(ACT.Sqrt)
                act.wait_ge(*at("fin_stat"))
                act.activation(fin[:, 0, :], bank[4][:, 0:2 * NB], ACT.Sqrt, scale=1.0 / D, bias=eps_col[:, 0:1]).then_inc(*mark("fin_root"))
                act.wait_ge(*at("fin_rstd"))
                for o in range(1, 2 * NB, 2):
                    i = o // 2
                    act.wait_ge(sem("fin_turned"), o + 1)
                    if o >= 4:
                        act.wait_ge(sem(f"out_stored{o % 4}"), 16)
                    act.wait_ge(sem("out_ready"), o)
                    act.activation(out_tok[:, o % 4, :], bank[o % 4][:, :], ACT.Copy, scale=fin[:, 1, 2 * i:2 * i + 1]).then_inc(sem("out_ready"), 1)

            ffn(0)
            mla()
            ffn(1)
            w_in()
            nsa()
            dilated()
            tail()

        @block.vector
        def _(dve):
            def split_lo(n, third=None):
                c = slice(0, U_COLS) if third is None else slice((0, 768, 1408)[third], (768, 1408, U_COLS)[third])
                dve.wait_ge(hi_sem, n + 1)
                lo = dve.tensor_tensor(w_lo[:, n % 2, c], raw(n)[:, c], w_hi[:, n % 2, c].bitcast(F32), ALU.subtract)
                if third in (None, 2):
                    lo.then_inc(lo_sem, 1)

            def chain(tag, k, m, gcol, c=None):
                dv, ac = sem(f"{tag}_dve"), sem(f"{tag}_act")
                dve.wait_ge(ac, k * 2 + 1)
                dve.scalar_tensor_tensor(xg_lo[:, m, :], xT[:, m, :], gcol, xg_hi[:, m, :].bitcast(F32), ALU.mult, ALU.subtract).then_inc(dv, 1)
                dve.wait_ge(ac, k * 2 + 2)
                dve.wait_ge(dv, k * 3)
                dve.tensor_tensor(sq_sum[:, :], sq_sum[:, :], squares[:, c if c is not None else k % 2, :], ALU.add).then_inc(dv, 1)

            dve.wait_ge(sem("ident_loaded"), 16)
            dve.tensor_copy(ident_r[:, :], ident[:, :]).then_inc(sem("masks_ready"), 1)
            dve.wait_ge(sem("mask_loaded"), 16)
            dve.tensor_copy(causal[:, :], masks0[:, :]).then_inc(sem("masks_ready"), 1)
            dve.wait_ge(*at("vec_turned"))
            dve.tensor_copy(cols[:, :], bank[7][:, 0:NROWS]).then_inc(*mark("cols_ready"))
            dve.wait_ge(*at("cols_ready"))
            f0, m0 = ROWS["norm_final"][0], ROWS["norm_mix_2"][0]
            dve.tensor_tensor(gain2[:, :], cols[:, f0:f0 + KD], cols[:, m0:m0 + KD], ALU.mult).then_inc(*mark("gain2_ready"))
            dve.wait_ge(*at("tok_root"))
            dve.reciprocal(tok_stat[:, 2, :], tok_stat[:, 1, :]).then_inc(*mark("tok_rstd"))
            dve.wait_ge(*at("tok_rstd"))
            for i in range(NB):
                dve.tensor_scalar(h_tok[:, i, :], x_tok[:, i, :], tok_stat[:, 2, i:i + 1], None, ALU.mult).then_inc(sem("h_tok_ready"), 1)
            split_lo(0)
            dve.wait_ge(*at("cols_ready"))
            for c in range(KD):
                dve.wait_ge(sem("pooled_hi"), c + 1)
                dve.scalar_tensor_tensor(pooled_lo[:, c, :], bank[4 + c % 4][:, :], gain("norm_mix", c), pooled_hi[:, c, :].bitcast(F32),
                                         ALU.mult, ALU.subtract).then_inc(sem("pooled_lo"), 1)
            split_lo(1)
            dve.wait_ge(sem("xT_ready"), KD)
            for m in range(KD + 1):
                if m < KD:
                    dve.wait_ge(sem("mixed_done"), m + 1)
                    dve.scalar_tensor_tensor(xT[:, m, :], bank[m % 4][:, :], gain("pool_scale", m), xT[:, m, :], ALU.mult, ALU.add).then_inc(sem("mix_added"), 1)
                if m:
                    dve.wait_ge(sem("mix_act"), 2 * m - 1)
                    dve.scalar_tensor_tensor(xg_lo[:, m - 1, :], xT[:, m - 1, :], gain("norm_ffn", m - 1), xg_hi[:, m - 1, :].bitcast(F32),
                                             ALU.mult, ALU.subtract).then_inc(sem("mix_lo"), 1)

            def ffn(l):
                tag, to = ffn_from[l], ffn_to[l]
                n0, d0 = FIRST[f"gateup{l}"], FIRST[f"down{l}"]
                gu, gd, ga, dn = sem(f"gateup{l}_done"), sem(f"gated{l}_dve"), sem(f"gated{l}_act"), sem(f"down{l}_done")
                split_lo(n0 + 1)
                dve.wait_ge(*at(f"{tag}_root"))
                dve.reciprocal(rstd[:, :], root[:, :]).then_inc(*mark(f"{tag}_rstd"))
                dve.memset(sq_sum[:, :], 0.0).then_inc(sem(f"{to}_clear"), 1)
                dve.memset(sq_sum2[:, :], 0.0).then_inc(sem(f"{to}_clear"), 1)
                dve.wait_ge(*at(f"{tag}_rstd"))
                dve.wait_ge(sem(f"{to}_clear"), 2)
                if l == 0:
                    dve.wait_ge(sem("sin_done"), 2)
                    dve.tensor_scalar(sin_t[:, :], sin_t[:, :], rope_col[:, 1:2], None, ALU.mult).then_inc(*mark("rope_ready"))

                def gateup_turn(i, first):
                    for j in (2,) if first else (1, 2):
                        n = n0 + j
                        dve.wait_ge(hi_sem, i * 2 + (n + 1))
                        dve.tensor_tensor(w_lo[:, n % 2, :], raw(n), w_hi[:, n % 2, :].bitcast(F32), ALU.subtract).then_inc(lo_sem, 1)
                    for c in range(2):
                        dve.wait_ge(gu, i * 4 + c + 1)
                        if not (first and c == 0):
                            dve.wait_ge(gd, i * 8 + 4 * c)
                        dve.tensor_tensor(gate_z, bank[c][:, :], rstd[:, :], ALU.mult).then_inc(gd, 1)
                        dve.wait_ge(gu, i * 4 + c + 3)
                        dve.tensor_tensor(up_z, bank[2 + c][:, :], rstd[:, :], ALU.mult).then_inc(gd, 1)
                        dve.wait_ge(gd, i * 8 + 4 * c + 2)
                        dve.wait_ge(ga, i * 4 + 2 * c + 1)
                        dve.tensor_tensor(gate_z, gate_s, up_z, ALU.mult).then_inc(gd, 1)
                        dve.wait_ge(ga, i * 4 + 2 * c + 2)
                        f = bass.ds(i * 2 + c, 1)
                        dve.tensor_tensor(act_lo[:, f, :].rearrange("p a t -> p (a t)"), gate_z,
                                          act_hi[:, f, :].bitcast(F32).rearrange("p a t -> p (a t)"), ALU.subtract).then_inc(gd, 1)
                gateup_turn(0, True)
                with dve.Fori(1, 11) as i:
                    gateup_turn(i, False)
                dv, ac = sem(f"{to}_dve"), sem(f"{to}_act")

                def down_turn(q, first):
                    for j in range(4):
                        n = d0 + j + 1
                        dve.wait_ge(hi_sem, q * 4 + (n + 1))
                        dve.tensor_tensor(w_lo[:, n % 2, :], raw(n), w_hi[:, n % 2, :].bitcast(F32), ALU.subtract).then_inc(lo_sem, 1)
                    for c in range(2):
                        k = q * 2 + c
                        xt = xT[:, bass.ds(k, 1), :].rearrange("p a t -> p (a t)")
                        xh = xg_hi[:, bass.ds(k, 1), :].bitcast(F32).rearrange("p a t -> p (a t)")
                        xl = xg_lo[:, bass.ds(k, 1), :].rearrange("p a t -> p (a t)")
                        dve.wait_ge(dn, q * 8 + 7 + c)
                        dve.tensor_tensor(xt, bank[c][:, :], xt, ALU.add).then_inc(dv, 1)
                        dve.wait_ge(ac, q * (4 + 2 * l) + (2 + l) * c + 1)
                        dve.scalar_tensor_tensor(xl, xt, ffn_gain(l, k), xh, ALU.mult, ALU.subtract).then_inc(dv, 1)
                        dve.wait_ge(ac, q * (4 + 2 * l) + (2 + l) * c + 2)
                        if not (first and c == 0):
                            dve.wait_ge(dv, q * (6 + 2 * l) + (3 + l) * c)
                        dve.tensor_tensor(sq_sum[:, :], sq_sum[:, :], squares[:, c, :], ALU.add).then_inc(dv, 1)
                        if l == 1:
                            dve.wait_ge(ac, q * 6 + 3 * c + 3)
                            dve.tensor_tensor(sq_sum2[:, :], sq_sum2[:, :], root[:, :], ALU.add).then_inc(dv, 1)

                down_turn(0, True)
                with dve.Fori(1, 4) as q:
                    down_turn(q, False)

            def mla():
                n0 = FIRST["mla_down"]
                split_lo(n0 + 1)
                dve.wait_ge(*at("ffn0_root"))
                dve.reciprocal(rstd[:, :], root[:, :]).then_inc(*mark("ffn0_rstd"))
                dve.wait_ge(*at("ffn0_rstd"))
                dve.wait_ge(sem("mla_down_done"), 1)
                dve.tensor_tensor(down_q[:, 3, :], bank[0][:, :], rstd[:, :], ALU.mult).then_inc(sem("down_q_ready"), 1)

                def queries(n):
                    t, idx = QUERY_TILES[n], (1, 4, 5)[n]
                    dve.wait_ge(sem("mla_down_done"), idx + 1)
                    dve.tensor_tensor(down_q[:, t, :], bank[idx][:, :], rstd[:, :], ALU.mult).then_inc(sem("down_q_ready"), 1)
                    dve.wait_ge(sem("cq_act"), 2 * n + 2)
                    dve.scalar_tensor_tensor(cq_lo[:, t, :], down_q[:, t, :], gain("mla_q_norm", t), cq_hi[:, t, :].bitcast(F32),
                                             ALU.mult, ALU.subtract).then_inc(sem("cq_lo"), 1)
                    if n:
                        dve.wait_ge(sem("cq_act"), 2 * n + 3)
                        if n == 2:
                            dve.wait_ge(sem("cq_sum"), 1)
                        dve.tensor_tensor(sq_sum[:, :], sq_sum[:, :], squares[:, n - 1, :], ALU.add).then_inc(sem("cq_sum"), 1)

                dve.wait_ge(*at("rope_ready"))
                dve.tensor_tensor(cos_s, cos_t[:, :], rstd[:, :], ALU.mult).then_inc(sem("kr_step"), 1)
                dve.tensor_tensor(sin_s, sin_t[:, :], rstd[:, :], ALU.mult).then_inc(sem("kr_step"), 1)
                queries(0)
                split_lo(n0 + 2)
                dve.wait_ge(sem("kr_step"), 2)
                dve.wait_ge(sem("mla_down_done"), 3)
                dve.tensor_tensor(root[:, :], bank[2][:, :], cos_s, ALU.mult).then_inc(sem("kr_step"), 1)
                dve.wait_ge(sem("mla_down_done"), 4)
                dve.tensor_tensor(sq_sum2[:, :], bank[3][:, :], sin_s, ALU.mult).then_inc(sem("kr_step"), 1)
                dve.wait_ge(sem("kr_step"), 4)
                dve.tensor_tensor(root[:, :], root[:, :], sq_sum2[:, :], ALU.add).then_inc(*mark("kr_ready"))
                dve.wait_ge(*at("kv_root"))
                dve.wait_ge(*at("kr_ready"))
                dve.reciprocal(sq_sum2[:, :], squares[:, 1, :]).then_inc(*mark("rkv_ready"))
                dve.wait_ge(*at("rkv_ready"))
                dve.scalar_tensor_tensor(down_q[:, 3, :], down_q[:, 3, :], gain("mla_kv_norm", 0), sq_sum2[:, :], ALU.mult, ALU.mult)\
                   .then_inc(*mark("ckv_ready"))
                dve.wait_ge(*at("kr_hi"))
                dve.tensor_tensor(kr_lo[:, :], root[:, :], kr_hi[:, :].bitcast(F32), ALU.subtract).then_inc(*mark("kr_lo"))
                dve.wait_ge(*at("ckv_hi"))
                dve.tensor_tensor(ckv_lo[:, :], down_q[:, 3, :], ckv_hi[:, :].bitcast(F32), ALU.subtract).then_inc(*mark("ckv_lo"))
                split_lo(n0 + 3)
                queries(1)
                queries(2)
                def proj(pr, what):
                    idx = PROJ_ORDER.index((pr, what))
                    h = 2 * pr + int(what[-1] == "1")
                    ps = bank[idx % 2][:, :]
                    dve.wait_ge(sem("proj_done"), idx + 1)
                    done = sem("proj_ready")
                    if idx:
                        dve.wait_ge(done, idx)
                    if what == "u":
                        dve.tensor_tensor(squares[:, 0, :], ps, cos_t[:, :], ALU.mult).then_inc(done, 1)
                        return
                    hi = [x for x in PROJ_ORDER if x[1] != "u"].index((pr, what)) + 1
                    if what == "us":
                        dve.tensor_tensor(squares[:, 1, :], ps, sin_t[:, :], ALU.mult).then_inc(sem("rope_step"), 1)
                        dve.wait_ge(sem("rope_step"), pr + 1)
                        dve.tensor_tensor(squares[:, 0, :], squares[:, 0, :], squares[:, 1, :], ALU.add).then_inc(sem("proj_tmp"), 1)
                        src, (dst_hi, dst_lo) = squares[:, 0, :], rotary_q(pr)
                    else:
                        src = ps
                    if what != "us":
                        dst_hi, dst_lo = (x[:, {"q": QN, "k": KN, "v": VV}[what[0]] + h % 2, :] for x in (xg_hi, xg_lo))
                    dve.wait_ge(sem("proj_hi"), hi)
                    dve.tensor_tensor(dst_lo, src, dst_hi.bitcast(F32), ALU.subtract).then_inc(done, 1)

                proj(0, "kn0")
                dve.wait_ge(*at("rq_root"))
                dve.reciprocal(rq[:, 1, :], rq[:, 0, :]).then_inc(*mark("rq_ready"))
                dve.wait_ge(*at("rq_ready"))

                for what in FIRST_PROJ[1:]:
                    proj(0, what)

                def row_max(s):
                    w = (NB - s % NB) * P
                    dve.wait_ge(sem("att_scored"), s + 1)
                    i = NB - 1 - s % NB
                    c = slice(s % 8, s % 8 + 1)
                    dve.tensor_reduce(row_top[:, c], bank[2 + s % 3][:, 0:w], AX.X, ALU.max, negate=True).then_inc(sem("att_top"), 1)
                    dve.wait_ge(sem("att_top"), s + 1)
                    dve.tensor_tensor(neg_max[:, c], row_top[:, c], rq[:, 1, 2 * i:2 * i + 1], ALU.mult).then_inc(sem("att_max"), 1)

                def normalise(s):
                    w = (NB - s % NB) * P
                    dve.wait_ge(sem("att_exp"), s + 1)
                    dve.reciprocal(row_inv[:, s % 8:s % 8 + 1], row_sum[:, s % 8:s % 8 + 1]).then_inc(sem("att_inv"), 1)
                    dve.wait_ge(sem("att_inv"), s + 1)
                    dve.tensor_scalar(probs[:, s % 4, 0:w], probs[:, s % 4, 0:w], row_inv[:, s % 8:s % 8 + 1], None, ALU.mult)\
                       .then_inc(sem("att_probs"), 1)

                def turned_lo(s):
                    h, ii = divmod(s, NB)
                    i = NB - 1 - ii
                    dve.wait_ge(sem("att_hi"), s + 1)
                    at = (slice(None), h % 2, slice(0, i + 1), slice(i * P, (i + 1) * P))
                    dve.tensor_tensor(pt_lo[at], bank[5 + s % 2][:, 0:(i + 1) * P].rearrange("p (j q) -> p j q", q=P),
                                      pt_hi[at].bitcast(F32), ALU.subtract).then_inc(sem("att_lo"), 1)

                def head_out(h):
                    dve.wait_ge(sem("att_out_hi"), h + 1)
                    dve.tensor_tensor(o_lo[:, h, :], bank[7][:, :], o_hi[:, h, :].bitcast(F32), ALU.subtract).then_inc(sem("att_out"), 1)

                for s in range(NB * HEADS + 7):
                    h, ii = divmod(s, NB)
                    if s < NB * HEADS:
                        row_max(s)
                    if 0 <= s - 1 < NB * HEADS:
                        normalise(s - 1)
                    if 0 <= s - 4 < NB * HEADS:
                        turned_lo(s - 4)
                    if s < NB * HEADS:
                        for t in after_step(h, ii):
                            proj(*t)
                        if h % 2 == 0 and ii >= 1:
                            split_lo(FIRST["heads"] + 1 + h // 2, ii - 1)
                    if s >= 6 and (s - 6) % NB == NB - 1:
                        head_out((s - 6) // NB)
                dve.memset(sq_sum[:, :], 0.0).then_inc(*mark("attn_clear"))
                dve.wait_ge(*at("attn_clear"))
                for u in range(1, 5):
                    split_lo(FIRST["mla_o"] + u)
                    for m in (2 * u - 2, 2 * u - 1):
                        dve.wait_ge(sem("mla_o_done"), m + 1)
                        dve.tensor_tensor(xT[:, m, :], bank[m % 4][:, :], xT[:, m, :], ALU.add).then_inc(sem("attn_dve"), 1)
                        chain("attn", m, m, gain("norm_ffn", 8 + m))

            def compress(t):
                st = sem("cmp_step")
                pc = p_cmp.rearrange("p (x n) -> p x n", n=32)

                def wide(k):
                    return cst[:, k, :].rearrange("p (x o) -> p x o", o=1).to_broadcast([P, 24, 32])

                def by_head(k):
                    return cst[:, k, :].rearrange("p (g i h) -> p g i h", g=2, h=3)

                if t == 13:
                    dve.wait_ge(*at("pe_turned"))
                    dve.tensor_copy(pe_cols[:, :, :].rearrange("p j l -> p (j l)"), bank[6][:, 0:64]).then_inc(*mark("pe_kept"))
                    dve.wait_ge(*at("pe_kept"))
                    dve.wait_ge(*at("kcv_padded"))
                    dve.wait_ge(sem("dmask_far"), 1)
                    dve.wait_ge(*at("dmask_ready"))
                    dve.wait_ge(sem("u_free"), KINDS.index("vc") + 1)
                    for kv in range(2):
                        for g in range(2):
                            for par in range(2):
                                r = slice(64 * g, 64 * g + 64)
                                win = bass.AP(kcv.tensor, kcv[r, kv, par:par + 1].offset, [list(kcv[r, kv, 0:1].ap[0]), [2, 16], [16, 32]])
                                off = pe_cols[r, kv, par:32:2].rearrange("p (l o) -> p l o", o=1).to_broadcast([64, 16, 32])
                                dve.tensor_tensor(cpe[kv][64 * par:64 * par + 64, :, g, :], win, off, ALU.add).then_inc(sem("cmp_windows"), 1)
                if t == 17:
                    dve.wait_ge(sem("cmp_kv_hi"), 1)
                    dve.tensor_tensor(kc_st[:, 1, :, :].rearrange("p g n -> p (g n)"), CMP_BANKS[0][:, 0:64],
                                      kc_st[:, 0, :, :].bitcast(F32).rearrange("p g n -> p (g n)"), ALU.subtract).then_inc(sem("cmp_kv_lo"), 1)
                    dve.wait_ge(sem("cmp_kv_hi"), 2)
                    dve.tensor_tensor(vc_st[:, :, 64:128], CMP_BANKS[1][0:96, 0:P].rearrange("n (g e) -> n g e", g=2),
                                      vc_st[:, :, 0:64].bitcast(F32), ALU.subtract).then_inc(sem("cmp_kv_lo"), 1)
                if t == 19:
                    dve.wait_ge(*at("c_scored"))
                    dve.wait_ge(*at("g_turned"))
                    cm = cmask[:, :, :].rearrange("p i (o n) -> p i o n", o=1).to_broadcast([P, NB, 3, 32])
                    for g in range(2):
                        dve.tensor_tensor(p_cmp[:, 384 * g:384 * (g + 1)].rearrange("p (i h n) -> p i h n", i=NB, h=3),
                                          CMP_BANKS[g][:, 0:384].rearrange("p (i h n) -> p i h n", i=NB, h=3), cm, ALU.add).then_inc(st, 1)
                    dve.wait_ge(st, 2)
                    dve.tensor_reduce(cst[:, 0, :], pc, AX.X, ALU.max).then_inc(st, 1)
                    dve.wait_ge(st, 3)
                    dve.tensor_tensor(pc, pc, wide(0), ALU.subtract).then_inc(*mark("cmp_shifted"))
                if t == 20:
                    dve.wait_ge(*at("cmp_exp"))
                    dve.tensor_reduce(cst[:, 1, :], pc, AX.X, ALU.add).then_inc(st, 1)
                    dve.wait_ge(st, 4)
                    dve.reciprocal(cst[:, 2, :], cst[:, 1, :]).then_inc(st, 1)
                    dve.wait_ge(st, 5)
                    dve.tensor_tensor(by_head(2), by_head(2), cvalid[:, :].rearrange("p (a i b) -> p a i b", a=1, b=1).to_broadcast([P, 2, NB, 3]), ALU.mult)\
                       .then_inc(st, 1)
                    dve.wait_ge(st, 6)
                    dve.wait_ge(*at("gates_kept"))
                    dve.tensor_tensor(by_head(3), by_head(2), gates[:, :, 0:18:3].rearrange("p i (g h) -> p g i h", g=2), ALU.mult).then_inc(st, 1)
                    dve.wait_ge(st, 7)
                    dve.tensor_tensor(pc, pc, wide(3), ALU.mult).then_inc(*mark("cmp_probs"))

            def w_in():
                n0 = FIRST["w_in"]
                split_lo(n0 + 1)
                dve.wait_ge(*at("ffn1_root"))
                dve.reciprocal(rstd[:, :], root[:, :]).then_inc(*mark("ffn1_rstd"))
                dve.wait_ge(*at("ffn1_rstd"))
                dve.wait_ge(*at("inner_stat"))
                dve.tensor_tensor(sq_sum[:, :], bank[6][:, :], rstd[:, :], ALU.mult).then_inc(sem("inner_step"), 1)
                dve.wait_ge(sem("inner_step"), 1)
                dve.tensor_tensor(sq_sum[:, :], sq_sum[:, :], rstd[:, :], ALU.mult).then_inc(*mark("inner_ready"))
                dve.wait_ge(*at("inner_root"))
                dve.reciprocal(sq_sum2[:, :], root[:, :]).then_inc(sem("inner_step"), 1)
                dve.wait_ge(sem("inner_step"), 2)
                dve.tensor_tensor(sq_sum2[:, :], sq_sum2[:, :], rstd[:, :], ALU.mult).then_inc(sem("inner_step"), 1)
                dve.wait_ge(sem("mix_loaded"), 9 * 16)
                masks = du[:, 0:2, :].rearrange("p a t -> p (a t)")[:, 0:6 * P].rearrange("p (g m c) -> p g m c", g=2, c=P)
                dve.tensor_copy(dmask[:, :, 0:3, :], masks[:, :, 0:1, :].to_broadcast([P, 2, 3, P])).then_inc(sem("dmask_far"), 1)
                dve.tensor_copy(dmask[:, :, 3:5, :], masks[:, :, 1:3, :]).then_inc(*mark("dmask_ready"))
                dve.memset(kcv[:, :, T:528], 0.0).then_inc(*mark("kcv_padded"))
                dve.wait_ge(sem("inner_step"), 3)

                cv = sem("conv_step")

                def conv(n):
                    c0 = 7 * n
                    tap = lambda k: gain("conv_w_2", 2 * k + n)
                    v, c, b, z = br[:, 2 + n, :], br[:, 4 + n, :], br[:, n, :], br[:, 6 + n, :]
                    dve.wait_ge(sem("u_free"), 8)
                    dve.tensor_tensor(v, v, c, ALU.mult).then_inc(cv, 1)
                    dve.wait_ge(cv, c0 + 1)
                    dve.tensor_scalar(c, v, tap(2), gain("conv_b_2", n), ALU.mult, ALU.add).then_inc(cv, 1)
                    for k in (1, 2):
                        dve.wait_ge(cv, c0 + 1 + k)
                        dve.scalar_tensor_tensor(c[:, k:T], v[:, 0:T - k], tap(2 - k), c[:, k:T], ALU.mult, ALU.add).then_inc(cv, 1)
                    dve.wait_ge(cv, c0 + 4)
                    dve.tensor_tensor(b, b, c, ALU.mult).then_inc(cv, 1)
                    dve.wait_ge(cv, c0 + 5)
                    dve.wait_ge(sem("conv_gate"), n + 1)
                    dve.tensor_tensor(z, z, b, ALU.mult).then_inc(cv, 2)

                for t in range(W_MAIN):
                    kind, dst = KINDS[t], u_dst(t)
                    dve.wait_ge(sem("u_done"), t + 1)
                    if t in SCRATCHED and SCRATCHED.index(t) >= 2:
                        last = SCRATCHED[SCRATCHED.index(t) - 2]
                        if KINDS[last] == "nq":
                            dve.wait_ge(sem("nq_lo"), 2 * (last - 8) + 2)
                        elif KINDS[last][0] == "k":
                            dve.wait_ge(sem("nk_lo"), 4 + 4 * int(KINDS[last] == "kw"))
                        elif KINDS[last][0] == "v":
                            dve.wait_ge(sem("nv_turned"), VTILES.index(last) + 1)
                    if kind == "z":
                        dve.wait_ge(cv, 14)
                    dve.tensor_tensor(dst, u_bank(t)[:, :], sq_sum2[:, :], ALU.mult).then_inc(sem("u_free"), 1)
                    if kind == "nq":
                        for e in range(2):
                            r, other = slice(64 * e, 64 * e + 64), slice(64 - 64 * e, 128 - 64 * e)
                            h = 2 * (t - 8) + e
                            dve.wait_ge(sem("nq_hi"), h + 1)
                            dve.scalar_tensor_tensor(q_st[other, h, :], dst[r, :], 0.125, q_st[r, h, :].bitcast(F32), ALU.mult, ALU.subtract)\
                               .then_inc(sem("nq_lo"), 1)
                    elif kind in ("ks", "kw"):
                        b = int(kind == "kw")
                        for g in range(2):
                            r = slice(64 * g, 64 * g + 64)
                            dve.wait_ge(sem("nk_hi"), 4 * b + 2 * g + 2)
                            for e in range(2):
                                dve.tensor_tensor(k_st[64 * e:64 * e + 64, 2 * b + g, 1, :], dst[r, :], k_st[r, 2 * b + g, 0, :].bitcast(F32),
                                                  ALU.subtract).then_inc(sem("nk_lo"), 1)
                    if t - 2 in VTILES:
                        v = VTILES.index(t - 2)
                        dve.wait_ge(sem("nv_hi"), v + 1)
                        dve.tensor_tensor(v_st[:, v, :, :, 64:128], bank[5 + v][:, :].rearrange("p (j h d) -> p h j d", h=2, d=64),
                                          v_st[:, v, :, :, 0:64].bitcast(F32), ALU.subtract).then_inc(sem("nv_lo"), 1)
                    if t == 19:
                        dve.wait_ge(*at("g_turned"))
                        dve.tensor_copy(gates[:, :, :].rearrange("p i c -> p (i c)"), bank[5][:, 0:P]).then_inc(*mark("gates_kept"))
                    if t == 8:
                        conv(0)
                    if t == 10:
                        conv(1)
                    if 1 <= t <= KD:
                        m = t - 1
                        dve.wait_ge(sem("ffn1_act"), 24)
                        dve.scalar_tensor_tensor(xT[:, m, :], xT[:, m, :], gain("norm_final", m), rstd[:, :], ALU.mult, ALU.mult)\
                           .then_inc(sem("x_normed"), 1)
                    compress(t)
                    if t % 2 == 1:
                        split_lo(n0 + t // 2 + 2)

            def add_halves(r, ps, dst, done, low, total):
                dve.tensor_tensor(total[r, :], ps[0:64, :], low[0:64, :], ALU.add).then_inc(sem("halves"), 1)
                sums[0] += 1
                dve.wait_ge(sem("halves"), sums[0])
                dve.tensor_tensor(dst, dst, total[r, :], ALU.mult).then_inc(done, 1)

            def keys_lo(j, g):
                r = slice(64 * j, 64 * j + 64)
                hi, lo = d_keys(j, g)
                dve.wait_ge(sem("dk_hi"), 6 * j + 2 * g + 2)
                for e in range(2):
                    dve.tensor_tensor(lo[64 * e:64 * e + 64, :], du[r, 3 + g, :], hi[r, :].bitcast(F32), ALU.subtract).then_inc(sem("dk_lo"), 1)

            sums = [0]

            def nsa():
                dve.wait_ge(sem("z_gate"), 3)

                def row_max(s):
                    i = NSTEP[s][2]
                    dve.wait_ge(sem("n_scored"), s + 1)
                    dve.tensor_reduce(neg_max[:, s % 8:s % 8 + 1], bank[s % 3][:, 0:(i + 1) * P], AX.X, ALU.max, negate=True).then_inc(sem("n_max"), 1)

                def normalise(s):
                    h, b, i = NSTEP[s]
                    w = (i + 1) * P
                    dve.wait_ge(sem("n_exp"), s + 1)
                    dve.reciprocal(row_inv[:, s % 8:s % 8 + 1], row_sum[:, s % 8:s % 8 + 1]).then_inc(sem("n_inv"), 1)
                    dve.wait_ge(sem("n_inv"), s + 1)
                    c = 3 * h + 1 + b
                    dve.tensor_scalar(pm[:, s % 4, 0:w], pm[:, s % 4, 0:w], row_inv[:, s % 8:s % 8 + 1], gates[:, i, c:c + 1], ALU.mult, ALU.mult)\
                       .then_inc(sem("n_probs"), 1)

                def turned_lo(s):
                    i, u = NSTEP[s][2], s // NB
                    dve.wait_ge(sem("n_hi"), s + 1)
                    dve.tensor_tensor(pn_cells(pn_lo, u, i), bank[5 + s % 2][:, 0:(i + 1) * P].rearrange("p (j q) -> p j q", q=P),
                                      pn_cells(pn_hi, u, i).bitcast(F32), ALU.subtract).then_inc(sem("n_lo"), 1)

                for s in range(len(NSTEP) + 7):
                    if s < len(NSTEP):
                        row_max(s)
                    if 0 <= s - 1 < len(NSTEP):
                        normalise(s - 1)
                    if s >= 6 and (s - 6) % 8 == 7:
                        h = (s - 6) // 8
                        r = slice(64 * (h % 2), 64 * (h % 2) + 64)
                        dve.wait_ge(sem("n_out_act"), h + 1)
                        add_halves(r, bank[7], br[r, h // 2, :], sem("n_sum"), root, sq_sum)
                    if 0 <= s - 4 < len(NSTEP):
                        turned_lo(s - 4)
                    if s == 3:
                        for g in range(2):
                            dve.wait_ge(sem("c_hi"), g + 1)
                            dve.tensor_tensor(ptc_lo[:, g, :], c_bank(g)[0:96, :], ptc_hi[:, g, :].bitcast(F32), ALU.subtract).then_inc(sem("c_lo"), 1)
                    w, step = divmod(s, 4)
                    if step == 0 and 0 < w <= NT - W_MAIN:
                        t = W_MAIN - 1 + w
                        dve.wait_ge(sem("u_done"), t + 1)
                        dve.tensor_tensor(u_dst(t), u_bank(t)[:, :], sq_sum2[:, :], ALU.mult).then_inc(sem("u_free"), 1)
                    elif s >= 7 and s % 8 in (7, 1, 2):
                        split_lo(FIRST["w_in"] + (W_MAIN + (s - 7) // 8 * 2) // 2 + 2, (7, 1, 2).index(s % 8))
                    if s >= 14 and s % 8 == 6:
                        x = (s - 14) // 8
                        r, other = slice(64 * (x % 2), 64 * (x % 2) + 64), slice(64 - 64 * (x % 2), 128 - 64 * (x % 2))
                        dve.wait_ge(sem("dq_hi"), x + 1)
                        dve.scalar_tensor_tensor(q_st[other, x, :], du[r, x // 2, :], 0.125, q_st[r, x, :].bitcast(F32),
                                                 ALU.mult, ALU.subtract).then_inc(sem("dq_lo"), 1)
                    if s in (31, 35, 47):
                        keys_lo(0, (31, 35, 47).index(s))

            def dilated():
                def row_max(x):
                    dve.wait_ge(sem("d_scored"), x + 1)
                    dve.tensor_reduce(neg_max[:, x % 8:x % 8 + 1], d_scores(x), AX.X, ALU.max, negate=True).then_inc(sem("d_max"), 1)

                def normalise(x):
                    c = slice(x % 8, x % 8 + 1)
                    dve.wait_ge(sem("d_exp"), x + 1)
                    dve.reciprocal(row_inv[:, c], row_sum[:, c]).then_inc(sem("d_inv"), 1)
                    dve.wait_ge(sem("d_inv"), x + 1)
                    dve.tensor_scalar(d_probs(x), d_probs(x), row_inv[:, c], None, ALU.mult).then_inc(sem("d_probs"), 1)

                def turned_lo(x):
                    i = DSTEP[x][1]
                    for n in range(len(D_FILLS[i])):
                        f = first_fill(x) + n
                        dve.wait_ge(sem("d_hi"), f + 1)
                        dve.tensor_tensor(d_fill(xg_lo, i, n), d_turned(i, n, f), d_fill(xg_hi, i, n).bitcast(F32), ALU.subtract).then_inc(sem("d_lo"), 1)

                D_SUM = (squares[:, 0, :], squares[:, 1, :], sq_sum2[:, :])

                def out(n):
                    j, g = n // 3, D_ORDER[n % 3]
                    dve.wait_ge(sem("d_out_act"), n + 1)
                    dve.tensor_tensor(D_SUM[g][64 * j:64 * j + 64, :], D_OUT[j][g][0:64, :], (root, rstd)[n % 2][0:64, :], ALU.add).then_inc(sem("d_out"), 1)

                def gate(n):
                    g = D_ORDER[n]
                    dve.wait_ge(sem("d_out"), 4 + n)
                    dve.wait_ge(sem("z_gate"), 4 + n)
                    dve.tensor_tensor(br[:, 3 + g, :], br[:, 3 + g, :], D_SUM[g], ALU.mult).then_inc(sem("d_gated"), 1)

                def v_lo(g):
                    dve.wait_ge(sem("dv_hi"), g + 1)
                    dve.tensor_tensor(v_st[:, g, :, :, 64:128], bank[5 + g % 2][:, :].rearrange("p (j h d) -> p h j d", h=2, d=64),
                                      v_st[:, g, :, :, 0:64].bitcast(F32), ALU.subtract).then_inc(sem("dv_lo"), 1)

                def y_lo(f):
                    dve.wait_ge(sem("y_hi"), f + 1)
                    dve.tensor_tensor(xg_lo[:, f, :], br[:, (f + 6) % 8, :], xg_hi[:, f, :].bitcast(F32), ALU.subtract).then_inc(sem("y_lo"), 1)

                for x in range(len(DSTEP) + 2):
                    if x < len(DSTEP):
                        row_max(x)
                    if x == 0:
                        v_lo(0)
                        v_lo(1)
                    if 0 <= x - 1 < len(DSTEP):
                        normalise(x - 1)
                    if x == 1:
                        v_lo(2)
                        keys_lo(1, 0)
                    if 0 <= x - 2 < len(DSTEP):
                        turned_lo(x - 2)
                    if x == 2:
                        keys_lo(1, 1)
                        keys_lo(1, 2)
                    if x == 5:
                        for n in range(3):
                            out(n)
                out(3)
                y_lo(0)
                y_lo(1)
                gate(0)
                out(4)
                y_lo(2)
                y_lo(3)
                gate(1)
                out(5)
                y_lo(4)
                gate(2)
                for f in (5, 6, 7):
                    y_lo(f)

            def tail():
                n_out, n_pp, n_pg = FIRST["w_out"], FIRST["ple_proj"], FIRST["ple_gate"]
                dve.memset(sq_sum[:, :], 0.0).then_inc(*mark("fin_clear"))
                dve.wait_ge(sem("x_back"), 16)
                for m in range(KD):
                    if m % 2 == 0:
                        split_lo(n_out + m // 2 + 1)
                    dve.wait_ge(sem("w_out_done"), m + 1)
                    dve.tensor_tensor(xR[:, m, :], bank[m % 4][:, :], xR[:, m, :], ALU.add).then_inc(sem("w_out_added"), 1)
                    dve.wait_ge(sem("xs_hi_ready"), m + 1)
                    dve.tensor_tensor(xs_lo[:, m, :], xR[:, m, :], xs_hi[:, m, :].bitcast(F32), ALU.subtract).then_inc(sem("xs_lo_ready"), 1)
                    if m in (4, 5):
                        dve.wait_ge(sem("p_hi_ready"), m - 3)
                        dve.tensor_tensor(p_lo[:, m - 4, :], bank[m + 1][:, :], p_hi[:, m - 4, :].bitcast(F32), ALU.subtract).then_inc(sem("p_lo_ready"), 1)
                split_lo(n_pg)
                for m in range(KD):
                    dve.wait_ge(sem("ple_proj_done"), m + 1)
                    dve.tensor_copy(emb[:, m, :], bank[4 + m % 2][:, :]).then_inc(sem("emb_ready"), 1)
                dve.wait_ge(sem("emb_ready"), KD)
                dve.wait_ge(*at("fin_clear"))
                pd = sem("ple_dve")
                for m in range(KD):
                    if m % 2 == 0 and m < 6:
                        split_lo(n_pg + m // 2 + 1)
                    gate = (root, rstd)[m % 2][:, :]
                    dve.wait_ge(sem("ple_act"), 2 * m + 1)
                    dve.tensor_tensor(gate, gate, emb[:, m, :], ALU.mult).then_inc(sem("ple_step"), 1)
                    dve.wait_ge(sem("ple_step"), m + 1)
                    dve.wait_ge(sem("w_out_added"), KD)
                    dve.tensor_tensor(xR[:, m, :], xR[:, m, :], gate, ALU.add).then_inc(pd, 2)
                    dve.wait_ge(sem("ple_act"), 2 * m + 2)
                    dve.wait_ge(pd, 3 * m)
                    dve.tensor_tensor(sq_sum[:, :], sq_sum[:, :], squares[:, m % 2, :], ALU.add).then_inc(pd, 1)
                dve.wait_ge(*at("fin_root"))
                dve.reciprocal(fin[:, 1, :], fin[:, 0, :]).then_inc(*mark("fin_rstd"))
                dve.wait_ge(*at("fin_rstd"))
                for o in range(0, 2 * NB, 2):
                    i = o // 2
                    dve.wait_ge(sem("fin_turned"), o + 1)
                    if o >= 4:
                        dve.wait_ge(sem(f"out_stored{o % 4}"), 16)
                    if o:
                        dve.wait_ge(sem("out_ready"), o)
                    dve.tensor_scalar(out_tok[:, o % 4, :], bank[o % 4][:, :], fin[:, 1, 2 * i:2 * i + 1], None, ALU.mult).then_inc(sem("out_ready"), 1)

            ffn(0)
            mla()
            ffn(1)
            w_in()
            nsa()
            dilated()
            tail()

        @block.tensor
        def _(pe):
            def triple(o, wh, wl, xh, xl, start, stop):
                pe.matmul(o, wh, xh, start=start, stop=False, skip_group_check=True)
                pe.matmul(o, wh, xl, start=False, stop=False, skip_group_check=True)
                return pe.matmul(o, wl, xh, start=False, stop=stop, skip_group_check=True)

            def chunk(o, n, nk, c, xh, xl, start=True, stop=True, k0=0, before=None):
                wh, wl = hi_tiles(n, nk)
                for k in range(nk):
                    if before:
                        before(k)
                    mm = triple(o, wh[:, k, c * P:(c + 1) * P], wl[:, k, c * P:(c + 1) * P], xh[:, k0 + k, :], xl[:, k0 + k, :],
                                start and k == 0, stop and k == nk - 1)
                return mm

            pe.wait_ge(sem("ident_loaded"), 16)
            pe.wait_ge(sem("vectors_loaded"), 16 * len(ROWS))
            pe.transpose(bank[7][:, 0:NROWS], vec_rows[0:NROWS, :], ident[0:NROWS, 0:NROWS]).then_inc(*mark("vec_turned"))
            for m in range(KD):
                if m >= 4:
                    pe.wait_ge(sem("xT_ready"), m - 3)
                for i in range(NB):
                    pe.wait_ge(sem(f"x_loaded{i // 2}"), 16)
                    mm = pe.transpose(bank[m % 4][:, i * P:(i + 1) * P], x_tok[:, i, m * P:(m + 1) * P], ident[:, :])
                mm.then_inc(sem("x_turned"), 1)
            pe.wait_ge(sem("band_loaded"), 16)
            for c in range(KD):
                if c == 3:
                    pe.wait_ge(*at("cols_ready"))
                if c >= 4:
                    pe.wait_ge(sem("pooled_lo"), c - 3)
                for i in range(NB):
                    pe.wait_ge(sem("h_tok_ready"), i + 1)
                    n = min(BAND, T - i * P)
                    mm = pe.matmul(bank[4 + c % 4][:, i * P:i * P + n], h_tok[:, i, c * P:(c + 1) * P], band[:, c // 2, int(i == 0), 0:n],
                                   start=i == 0, stop=i == NB - 1, skip_group_check=True)
                mm.then_inc(sem("pooled_done"), 1)
            def mix_squares(m):
                if m == 0:
                    pe.wait_ge(sem("ones_set"), 1)
                pe.wait_ge(sem("mix_act"), 2 * m + 2)
                pe.matmul(bank[7][:, :], ones[:, :], squares[:, m % 2, :], start=m == 0, stop=m == KD - 1, skip_group_check=True).then_inc(sem("mix_summed"), 1)

            pe.wait_ge(lo_sem, 1)
            pe.wait_ge(sem("xT_ready"), KD)
            wh, wl = hi_tiles(0, 8)
            for m in range(KD):
                g, c = divmod(m, 2)
                if m >= 4:
                    pe.wait_ge(sem("mix_added"), m - 3)
                for k in range(2):
                    pe.wait_ge(sem("pooled_lo"), 2 * g + k + 1)
                    mm = triple(bank[m % 4][:, :], wh[:, 2 * g + k, c * P:(c + 1) * P], wl[:, 2 * g + k, c * P:(c + 1) * P],
                                pooled_hi[:, 2 * g + k, :], pooled_lo[:, 2 * g + k, :], k == 0, k == 1)
                mm.then_inc(sem("mixed_done"), 1)
                if m >= 3:
                    mix_squares(m - 3)
            mix_squares(5)

            def stat(tag):
                pe.wait_ge(sem(f"{tag}_dve"), 3 * KD)
                pe.wait_ge(sem("ones_set"), 1)
                pe.matmul(bank[7][:, :], ones[:, :], sq_sum[:, :], start=True, stop=True).then_inc(*mark(f"{tag}_stat"))

            def ffn(l):
                tag, to = ffn_from[l], ffn_to[l]
                n0, d0 = FIRST[f"gateup{l}"], FIRST[f"down{l}"]
                gu, gd, dn = sem(f"gateup{l}_done"), sem(f"gated{l}_dve"), sem(f"down{l}_done")

                def turn(i, first):
                    for j in range(2):
                        n = n0 + j
                        pe.wait_ge(lo_sem, i * 2 + (n + 1))
                        for c in range(2):
                            if first:
                                pe.wait_ge(*tile_added(l, 4 + 2 * j + c))
                            else:
                                pe.wait_ge(gd, i * 8 + (4 * c + j + 1 - 8))
                            before = (lambda k: pe.wait_ge(*tile_split(l, k))) if first and j == c == 0 else None
                            chunk(bank[2 * j + c][:, :], n, 8, c, xg_hi, xg_lo, before=before).then_inc(gu, 1)
                            if first and j == c == 0:
                                if l == 0:
                                    mix_squares(6)
                                    mix_squares(7)
                                else:
                                    stat(tag)

                turn(0, True)
                with pe.Fori(1, 11) as i:
                    turn(i, False)

                def down_turn(q, first):
                    for j, (k0, nk) in enumerate(DOWN_SPLIT):
                        n = d0 + j
                        pe.wait_ge(lo_sem, q * 4 + (n + 1))
                        for c in range(2):
                            if first:
                                pe.wait_ge(gd, max(4 * (k0 + nk), 81 + 4 * c))
                            if not first and j == 0:
                                pe.wait_ge(sem(f"{to}_dve"), q * (6 + 2 * l) + ((3 + l) * c + 1 - (6 + 2 * l)))
                            chunk(bank[c][:, :], n, nk, c, act_hi, act_lo, j == 0, j == 3, k0).then_inc(dn, 1)

                down_turn(0, True)
                with pe.Fori(1, 4) as q:
                    down_turn(q, False)

            def mla():
                n0 = FIRST["mla_down"]
                for idx in range(6):
                    n, c = n0 + idx // 2, idx % 2 if idx >= 2 else 1 - idx
                    pe.wait_ge(lo_sem, n + 1)
                    if idx < 2:
                        pe.wait_ge(sem("ffn0_dve"), 3 * (6 + idx) + 1)
                    before = (lambda k: pe.wait_ge(sem("ffn0_dve"), 3 * k + 2)) if idx == 0 else None
                    chunk(bank[idx][:, :], n, 8, c, xg_hi, xg_lo, before=before).then_inc(sem("mla_down_done"), 1)
                    if idx == 0:
                        stat("ffn0")
                    if idx == 2:
                        pe.wait_ge(sem("cq_act"), 1)
                        pe.wait_ge(*at("ffn0_root"))
                        pe.matmul(bank[7][:, :], ones[:, :], squares[:, 0, :], start=True, stop=True).then_inc(*mark("kv_stat"))

                def proj(pr, what):
                    idx = PROJ_ORDER.index((pr, what))
                    n = FIRST["heads"] + pr
                    wh, wl = (w[:, n % 2, :].rearrange("p (t c) -> p t c", c=P) for w in (w_hi, w_lo))
                    ps = bank[idx % 2]
                    pe.wait_ge(lo_sem, n + 1)
                    if idx < 2:
                        pe.wait_ge(*(sem("down_q_ready"), 1 + idx))
                    else:
                        pe.wait_ge(sem("proj_ready"), idx - 1)
                    if what in ("qn0", "qn1", "u", "us"):
                        pe.wait_ge(sem("cq_lo"), 3)
                        t0 = {"qn0": 0, "qn1": 3, "u": 6, "us": 9}[what]
                        for k in range(3):
                            mm = triple(ps[:, :], wh[:, t0 + k, :], wl[:, t0 + k, :], cq_hi[:, k, :], cq_lo[:, k, :], k == 0, k == 2)
                    else:
                        pe.wait_ge(*at("ckv_lo"))
                        t0 = 12 + 2 * int(what[-1]) + int(what[0] == "v")
                        if what[0] == "k":
                            mm = triple(ps[:, :], wh[:, t0, :], wl[:, t0, :], ckv_hi[:, :], ckv_lo[:, :], True, True)
                        else:
                            for j in range(NB):
                                tok = slice(j * P, (j + 1) * P)
                                mm = triple(ps[:, tok], ckv_hi[:, tok], ckv_lo[:, tok], wh[:, t0, :], wl[:, t0, :], True, True)
                    mm.then_inc(sem("proj_done"), 1)

                for what in FIRST_PROJ:
                    proj(0, what)
                    if what == "qn0":
                        pe.wait_ge(sem("cq_sum"), 2)
                        for i in range(NB):
                            mm = pe.matmul(bank[6][:, 2 * i:2 * i + 2], sq_sum[:, i * P:(i + 1) * P], ones[:, 0:2], start=True, stop=True)
                        mm.then_inc(*mark("rq_stat"))

                def scores(s):
                    h, ii = divmod(s, NB)
                    i = NB - 1 - ii
                    o = bank[2 + s % 3][:, 0:(i + 1) * P]
                    q, k = slice(i * P, (i + 1) * P), slice(0, (i + 1) * P)
                    if s == 0:
                        pe.wait_ge(*at("kr_lo"))
                        pe.wait_ge(sem("masks_ready"), 2)
                    pe.wait_ge(sem("proj_ready"), proj_count(h // 2, *(("kn1", "qn1") if h % 2 else FIRST_PROJ)))
                    if s >= 3:
                        pe.wait_ge(sem("att_exp"), s - 2)
                    hs = h % 2
                    triple(o, xg_hi[:, QN + hs, q], xg_lo[:, QN + hs, q], xg_hi[:, KN + hs, k], xg_lo[:, KN + hs, k], True, False)
                    r = slice(64 * hs, 64 * hs + 64)
                    qh, ql = rotary_q(h // 2)
                    triple(o, qh[r, q], ql[r, q], kr_hi[r, k], kr_lo[r, k], False, False)
                    pe.matmul(o[:, i * P:(i + 1) * P], ident_r[:, :], causal[:, :], start=False, stop=True, skip_group_check=True)\
                      .then_inc(sem("att_scored"), 1)

                def turn(s):
                    i = NB - 1 - s % NB
                    pe.wait_ge(sem("att_probs"), s + 1)
                    if s >= 2:
                        pe.wait_ge(sem("att_lo"), s - 1)
                    for j in range(i + 1):
                        mm = pe.transpose(bank[5 + s % 2][:, j * P:(j + 1) * P], probs[:, s % 4, j * P:(j + 1) * P], ident[:, :])
                    mm.then_inc(sem("att_turned"), 1)

                def values(h):
                    pe.wait_ge(sem("att_lo"), NB * (h + 1))
                    pe.wait_ge(sem("proj_ready"), proj_count(h // 2, f"v{h % 2}"))
                    if h:
                        pe.wait_ge(sem("att_out"), h)
                    vh, vl = (x[:, VV + h % 2, :].rearrange("p (j d) -> p j d", d=P) for x in (xg_hi, xg_lo))
                    for j in range(NB):
                        q = slice(j * P, T)
                        mm = triple(bank[7][:, q], vh[:, j, :], vl[:, j, :], pt_hi[:, h % 2, j, q], pt_lo[:, h % 2, j, q], j == 0, j == NB - 1)
                    mm.then_inc(sem("att_out_done"), 1)

                def out(m, k0, k1):
                    wh, wl = hi_tiles(FIRST["mla_o"] + m // 2, 8)
                    c = slice(m % 2 * P, m % 2 * P + P)
                    if k0 == 0:
                        pe.wait_ge(lo_sem, FIRST["mla_o"] + m // 2 + 1)
                        if m < 2:
                            pe.wait_ge(sem("proj_ready"), 32)
                        elif m < 4:
                            pe.wait_ge(sem("att_exp"), NB * HEADS)
                        else:
                            pe.wait_ge(sem("attn_dve"), 3 * (m - 4) + 1)
                    for k in range(k0, k1):
                        pe.wait_ge(sem("att_out"), k + 1)
                        mm = triple(bank[m % 4][:, :], wh[:, k, c], wl[:, k, c], o_hi[:, k, :], o_lo[:, k, :], k == 0, k == HEADS - 1)
                    if k1 == HEADS:
                        mm.then_inc(sem("mla_o_done"), 1)

                for s in range(NB * HEADS + 6):
                    h, ii = divmod(s, NB)
                    if s < NB * HEADS:
                        scores(s)
                    if 0 <= s - 3 < NB * HEADS:
                        turn(s - 3)
                    if s >= 5 and (s - 5) % NB == NB - 1:
                        values((s - 5) // NB)
                    if s < NB * HEADS:
                        for t in after_step(h, ii):
                            proj(*t)
                    if s - NB * HEADS in (0, 1):
                        out(s - NB * HEADS, 0, 6)
                for m in range(KD):
                    out(m, 6 if m < 2 else 0, HEADS)

            def compress(t):
                if t == 15:
                    pe.wait_ge(*at("ffn1_root"))
                    for kv in range(2):
                        pe.wait_ge(sem("cmp_windows"), 4 * kv + 4)
                        for l in range(16):
                            mm = pe.matmul(CMP_BANKS[kv][0:64, 0:64], w1_t[:, kv, l, :], cpe[kv][:, l, :, :].rearrange("p g n -> p (g n)"),
                                           start=l == 0, stop=l == 15)
                        mm.then_inc(sem("cmp_hidden"), 1)
                if t == 16:
                    pe.wait_ge(sem("cmp_act"), 1)
                    pe.matmul(CMP_BANKS[0][:, 0:64], w2_t[:, 0, :, :].rearrange("p d e -> p (d e)"), h1[:, 0:64], start=True, stop=True)\
                      .then_inc(sem("cmp_done"), 1)
                    pe.wait_ge(sem("cmp_act"), 2)
                    for g in range(2):
                        mm = pe.matmul(CMP_BANKS[1][0:96, g * 64:(g + 1) * 64], h1[:, 64 + g * 96:64 + (g + 1) * 96], w2_t[:, 1, 0, :], start=True, stop=True)
                    mm.then_inc(sem("cmp_done"), 1)
                if t == 18:
                    pe.wait_ge(sem("cmp_kv_lo"), 2)
                    pe.wait_ge(sem("nq_lo"), 6)
                    for h in range(6):
                        for i in range(NB):
                            c = (i * 3 + h % 3) * 32
                            for part in range(2):
                                mm = pe.matmul(CMP_BANKS[h // 3][:, c:c + 32], q_st[:, h, i * P:(i + 1) * P], kc_st[:, part, h // 3, :],
                                               start=part == 0, stop=part == 1, skip_group_check=True)
                    mm.then_inc(*mark("c_scored"))

            def w_in():
                n0 = FIRST["w_in"]
                for t in range(W_MAIN):
                    n = n0 + t // 2
                    pe.wait_ge(lo_sem, n + 1)
                    if t < 2:
                        pe.wait_ge(sem("ffn1_dve"), 4 * (6 + t) + 1)
                    if t >= 4:
                        pe.wait_ge(sem("u_free"), t - 3)
                    before = (lambda k: pe.wait_ge(sem("ffn1_dve"), 4 * k + 2)) if t == 0 else None
                    chunk(u_bank(t)[:, :], n, 8, t % 2, xg_hi, xg_lo, before=before).then_inc(sem("u_done"), 1)
                    if t == 0:
                        pe.wait_ge(sem("ffn1_dve"), 4 * KD)
                        pe.matmul(bank[7][:, :], ones[:, :], sq_sum[:, :], start=True, stop=True).then_inc(*mark("ffn1_stat"))
                        pe.matmul(bank[6][:, :], ones[:, :], sq_sum2[:, :], start=True, stop=True).then_inc(*mark("inner_stat"))
                    if t - 1 in VTILES:
                        v = VTILES.index(t - 1)
                        pe.wait_ge(sem("u_free"), t)
                        if v == 1:
                            pe.wait_ge(*at("pe_kept"))
                        for j in range(NB):
                            mm = pe.transpose(bank[5 + v][:, j * P:(j + 1) * P], u_dst(t - 1)[:, j * P:(j + 1) * P], ident[:, :])
                        mm.then_inc(sem("nv_turned"), 1)
                    compress(t)
                    if t == 18:
                        pe.wait_ge(*at("gates_ready"))
                        pe.wait_ge(sem("nv_lo"), 1)
                        for j in range(NB):
                            mm = pe.transpose(bank[5][:, j * 32:(j + 1) * 32], u_dst(17)[0:32, j * P:(j + 1) * P], ident[0:32, 0:32])
                        mm.then_inc(*mark("g_turned"))
                    if t == 10:
                        pe.wait_ge(sem("mix_loaded"), 9 * 16)
                        pe.wait_ge(*at("inner_ready"))
                        for j in range(2):
                            mm = pe.transpose(bank[6][:, j * 32:(j + 1) * 32], pe_rows[:, j, :], ident[0:32, 0:32])
                        mm.then_inc(*mark("pe_turned"))

            def nsa():
                def scores(s):
                    h, b, i = NSTEP[s]
                    o = bank[s % 3][:, 0:(i + 1) * P]
                    if s == 0:
                        pe.wait_ge(sem("nk_lo"), 8)
                        pe.wait_ge(sem("u_free"), W_MAIN)
                    if s >= 3:
                        pe.wait_ge(sem("n_exp"), s - 2)
                    for part in range(2):
                        pe.matmul(o, q_st[:, h, i * P:(i + 1) * P], k_st[:, 2 * b + h // 3, part, 0:(i + 1) * P], start=part == 0, stop=False,
                                  skip_group_check=True)
                    pe.matmul(o[:, i * P:(i + 1) * P], ident_r[:, :], causal[:, :], start=False, stop=True, skip_group_check=True)\
                      .then_inc(sem("n_scored"), 1)

                def turn(s):
                    i = NSTEP[s][2]
                    pe.wait_ge(sem("n_probs"), s + 1)
                    if s >= 2:
                        pe.wait_ge(sem("n_lo"), s - 1)
                    if s == 1:
                        pe.wait_ge(sem("c_lo"), 2)
                    for j in range(i + 1):
                        at_ = j if s // NB % 2 == 0 else i - j
                        mm = pe.transpose(bank[5 + s % 2][:, at_ * P:(at_ + 1) * P], pm[:, s % 4, j * P:(j + 1) * P], ident[:, :])
                    mm.then_inc(sem("n_turned"), 1)

                def values(s):
                    h, b, i = NSTEP[s]
                    o, u, g = bank[7], s // NB, h // 3
                    pe.wait_ge(sem("n_lo"), s + 1)
                    if s % 8 == 0:
                        pe.wait_ge(*(sem("n_sum"), h) if h else (sem("c_lo"), 2))
                        r = slice(h % 3 * 32, h % 3 * 32 + 32)
                        for part, pt in enumerate((ptc_hi, ptc_lo)):
                            pe.matmul(o[:, :], vc_st[r, g, :], pt[r, g, :], start=part == 0, stop=False, skip_group_check=True)
                    for part, pt in enumerate((pn_hi, pn_lo)):
                        mm = pe.matmul(o[:, i * P:T], v_st[:, b, g, i, :], pn_row(pt, u, i), start=False, stop=s % 8 == 7 and part == 1,
                                       skip_group_check=True)
                    mm.then_inc(sem("n_pv"), 1)

                def project(s):
                    t, step = W_MAIN + s // 4, s % 4
                    n, c = FIRST["w_in"] + t // 2, slice(t % 2 * P, t % 2 * P + P)
                    if step == 0:
                        pe.wait_ge(lo_sem, n + 1)
                        pe.wait_ge(sem("u_free"), t - 1)
                        if s == 4:
                            pe.wait_ge(*at("cmp_shifted"))
                    wh, wl = hi_tiles(n, 8)
                    for k in (2 * step, 2 * step + 1):
                        mm = triple(u_bank(t)[:, :], wh[:, k, c], wl[:, k, c], xg_hi[:, k, :], xg_lo[:, k, :], k == 0, k == KD - 1)
                    if step == 3:
                        mm.then_inc(sem("u_done"), 1)

                pe.wait_ge(sem("nv_lo"), 2)
                for s in range(len(NSTEP) + 5):
                    if s < len(NSTEP):
                        scores(s)
                        if s == 2:
                            pe.wait_ge(*at("cmp_probs"))
                            for g in range(2):
                                for i in range(NB):
                                    c = (g * NB + i) * 96
                                    mm = pe.transpose(c_bank(g)[0:96, i * P:(i + 1) * P], p_cmp[:, c:c + 96], ident[:, :])
                                mm.then_inc(sem("c_turned"), 1)
                    if 0 <= s - 3 < len(NSTEP):
                        turn(s - 3)
                    if s < len(NSTEP):
                        project(s)
                    if s >= 5 and (s - 5) % 8:
                        if (s - 5) % 8 == 1:
                            values(s - 6)
                        values(s - 5)

            def dilated():
                def scores(x):
                    j, i = DSTEP[x]
                    if x == 0:
                        pe.wait_ge(sem("n_exp"), len(NSTEP))
                        pe.wait_ge(sem("dmask_far"), 1)
                        pe.wait_ge(*at("dmask_ready"))
                    elif x == 1:
                        pe.wait_ge(sem("u_free"), NT)
                    else:
                        pe.wait_ge(sem("d_exp"), D_FREE[x])
                    pe.wait_ge(sem("dq_lo"), 5 + j)
                    pe.wait_ge(sem("dk_lo"), 6 * j + 6)
                    o, blocks = d_scores(x), D_BLOCKS[i]
                    n = 0
                    while n < len(blocks):
                        g, kb = blocks[n]
                        run = next((m for m in range(n, len(blocks)) if blocks[m][0] != g), len(blocks)) - n
                        for part, k in enumerate(d_keys(j, g)):
                            pe.matmul(o[:, n * P:(n + run) * P], q_st[:, 2 * g + j, i * P:(i + 1) * P], k[:, kb * P:(kb + run) * P],
                                      start=part == 0 and n * P % T == 0, stop=False, skip_group_check=True)
                        n += run
                    for n, count, mask in d_masks(i):
                        mm = pe.matmul(o[:, n * P:(n + count) * P], ident_r[:, :], mask, start=False, stop=True, skip_group_check=True)
                    mm.then_inc(sem("d_scored"), 1)

                def turn(x):
                    i = DSTEP[x][1]
                    pe.wait_ge(sem("d_probs"), x + 1)
                    for n, fill in enumerate(D_FILLS[i]):
                        f = first_fill(x) + n
                        if f >= 2:
                            pe.wait_ge(sem("d_lo"), f - 1)
                        if x == 4:
                            pe.wait_ge(sem("d_out"), 3)
                        for m, b in enumerate(fill):
                            mm = pe.transpose(bank[5 + f % 2][:, m * P:(m + 1) * P], d_probs(x)[:, b * P:(b + 1) * P], ident[:, :])
                        mm.then_inc(sem("d_turned"), 1)

                def values(j):
                    pe.wait_ge(sem("d_lo"), first_fill(7 if j else 4))
                    pe.wait_ge(sem("n_sum"), 6)
                    if j:
                        pe.wait_ge(sem("d_out"), 3)
                        pe.wait_ge(sem("d_exp"), len(DSTEP))
                    a, b, c = D_ORDER
                    for n, (g, kb) in enumerate([(g, kb) for g in (a, b) for kb in (3, 2, 1)] + [(a, 0), (b, 0)] + [(c, kb) for kb in (3, 2, 1, 0)]):
                        if j and n == 6:
                            pe.wait_ge(sem("d_lo"), first_fill(8))
                        last = min(kb + 1, NB - 1) if g == 0 else NB - 1
                        c0, c1 = d_cell(g, kb, kb), d_cell(g, kb, last) + P
                        for part, pt in enumerate((xg_hi, xg_lo)):
                            mm = pe.matmul(D_OUT[j][g][:, kb * P:(last + 1) * P], v_st[:, g, j, kb, :],
                                           pt[:, :, :].rearrange("p a t -> p (a t)")[:, c0:c1], start=kb == NB - 1 and part == 0,
                                           stop=kb == 0 and part == 1, skip_group_check=True)
                        if kb == 0:
                            mm.then_inc(sem("d_pv"), 1)

                scores(0)
                pe.wait_ge(sem("n_lo"), len(NSTEP))

                def turn_values(g):
                    for j in range(NB):
                        mm = pe.transpose(bank[5 + g % 2][:, j * P:(j + 1) * P], du[:, 6 + g, j * P:(j + 1) * P], ident[:, :])
                    mm.then_inc(sem("dv_turned"), 1)

                turn_values(0)
                turn_values(1)
                for x in range(len(DSTEP) + 1):
                    if x + 1 < len(DSTEP):
                        scores(x + 1)
                    if x == 0:
                        pe.wait_ge(sem("dv_lo"), 1)
                        turn_values(2)
                    if x == 1:
                        pe.wait_ge(sem("dv_lo"), 3)
                    if x == 5:
                        values(0)
                    if x >= 1:
                        turn(x - 1)
                values(1)

            def tail():
                n_out, n_pp, n_pg = FIRST["w_out"], FIRST["ple_proj"], FIRST["ple_gate"]
                pe.wait_ge(sem("d_exp"), len(DSTEP))
                for m in range(KD):
                    n = n_out + m // 2
                    pe.wait_ge(lo_sem, n + 1)
                    if m >= 4:
                        pe.wait_ge(sem("w_out_added"), m - 3)
                    before = (lambda k: pe.wait_ge(sem("y_lo"), k + 1)) if m == 0 else None
                    chunk(bank[m % 4][:, :], n, 8, m % 2, xg_hi, xg_lo, before=before).then_inc(sem("w_out_done"), 1)
                    if m in (3, 4):
                        pe.wait_ge(sem("p_loaded"), 16)
                        for i in range(NB):
                            mm = pe.transpose(bank[m + 2][:, i * P:(i + 1) * P], p_tok[:, i, (m - 3) * P:(m - 2) * P], ident[:, :])
                        mm.then_inc(sem("p_turned"), 1)
                pe.wait_ge(lo_sem, n_pp + 1)
                pe.wait_ge(sem("p_lo_ready"), 2)
                wh, wl = (w[:, n_pp % 2, :].rearrange("p (k c) -> p k c", k=2) for w in (w_hi, w_lo))
                for m in range(KD):
                    if m >= 2:
                        pe.wait_ge(sem("emb_ready"), m - 1)
                    for k in range(2):
                        mm = triple(bank[4 + m % 2][:, :], wh[:, k, m * P:(m + 1) * P], wl[:, k, m * P:(m + 1) * P], p_hi[:, k, :], p_lo[:, k, :], k == 0, k == 1)
                    mm.then_inc(sem("ple_proj_done"), 1)
                for m in range(KD):
                    n = n_pg + m // 2
                    pe.wait_ge(lo_sem, n + 1)
                    pe.wait_ge(sem("w_out_added"), KD) if m == 0 else None
                    if m >= 4:
                        pe.wait_ge(sem("ple_act"), 2 * (m - 4) + 1)
                    before = (lambda k: pe.wait_ge(sem("xs_lo_ready"), k + 1)) if m == 0 else None
                    chunk(bank[m % 4][:, :], n, 8, m % 2, xs_hi, xs_lo, before=before).then_inc(sem("ple_gate_done"), 1)
                pe.wait_ge(sem("ple_dve"), 24)
                pe.wait_ge(sem("emb_ready"), KD)
                for i in range(NB):
                    mm = pe.matmul(bank[4][:, 2 * i:2 * i + 2], sq_sum[:, i * P:(i + 1) * P], ones[:, 0:2], start=True, stop=True)
                mm.then_inc(*mark("fin_stat"))
                pe.wait_ge(sem("fin_gained"), KD)
                pe.wait_ge(sem("ple_act"), 16)
                for o in range(2 * NB):
                    i, half = divmod(o, 2)
                    if o >= 4:
                        pe.wait_ge(sem("out_ready"), o - 3)
                    for m in range(4):
                        mm = pe.transpose(bank[o % 4][:, m * P:(m + 1) * P], emb[:, 4 * half + m, i * P:(i + 1) * P], ident[:, :])
                    mm.then_inc(sem("fin_turned"), 1)

            ffn(0)
            mla()
            ffn(1)
            w_in()
            nsa()
            dilated()
            tail()


def constants():
    import numpy as np
    c = {"c_ident": np.eye(P, dtype=np.float32)}
    s, t = np.arange(P)[:, None], np.arange(BAND)[None, :]
    band = np.zeros((P, len(WINDOWS), 2, BAND), np.float32)
    for g, w in enumerate(WINDOWS):
        inside = (t >= s) & (t - s < w)
        for first in range(2):
            n = np.minimum(t + 1, w) if first else np.full_like(t, w)
            band[:, g, first] = inside / n.astype(np.float32) - (t == s)
    c["c_band"] = band
    lane = np.arange(P)
    inv = 1.0 / (np.float32(10000.0) ** (np.arange(0, ROPE, 2, dtype=np.float32) / np.float32(ROPE)))
    c["c_rope"] = np.stack([inv[lane % 32], np.where(lane % 64 < 32, -1.0, 1.0)], 1).astype(np.float32)
    q, k = np.arange(P)[:, None], np.arange(P)[None, :]
    ok = [k <= q]
    for dil, near in ((4, k >= q), (16, k <= q)):
        same = (q - k) % dil == 0
        ok += [same, same & (k <= q), near]
    n = np.arange(32)[None, None, :]
    tok = P * np.arange(NB)[None, :, None] + np.arange(P)[:, None, None]
    c["c_cmask"] = np.where((16 * n + 31 <= tok) & (n < 31), 0.0, NEG).astype(np.float32)
    c["c_cvalid"] = np.ascontiguousarray((tok[:, :, 0] >= 31).astype(np.float32))
    c["c_masks"] = np.ascontiguousarray(np.stack([np.where(m, 0.0, NEG) for m in ok], 1).astype(np.float32))
    return c


def kernel(**inputs):
    import numpy as np
    import concourse.bacc as bacc
    from concourse.bass_utils import run_bass_kernel_spmd

    nc = bacc.Bacc("TRN2", target_bir_lowering=False, num_devices=1)
    arrays, aps = {}, {}
    for name, v in list(inputs.items()) + list(constants().items()):
        v = np.ascontiguousarray(v)
        arrays[f"in_{name}"] = v
        key = name
        aps[key] = nc.dram_tensor(f"in_{name}", v.shape, mybir.dt.from_np(v.dtype), kind="ExternalInput").ap()
    out = nc.dram_tensor("out_0", (1, T, D), F32, kind="ExternalOutput").ap()
    program(nc, aps, out)
    r = run_bass_kernel_spmd(nc, [arrays], core_ids=[0])
    return r.results[0]["out_0"]
```
